# Optimizing a Trainium2 kernel written in Bass

```python
import math
import jax, jax.numpy as jnp
from jax import lax
import numpy as np

D_MODEL = 1024
BATCH = 1
SEQ = 1024
DEPTH = 1

CHUNK = 64
Q_BLOCK = 128
D_PLE = 256
D_MIX = D_MODEL
RET_WIDTH = D_MIX // 2
RET_HEADS = 4
RET_HEAD_DIM = RET_WIDTH // RET_HEADS
MLA_HEADS = 4
MLA_NOPE_DIM = 128
MLA_ROPE_DIM = 64
MLA_V_DIM = (D_MIX - RET_WIDTH) // MLA_HEADS
MLA_QK_DIM = MLA_NOPE_DIM + MLA_ROPE_DIM
Q_LORA = 256
KV_LORA = 128
D_FF = -(-8 * D_MODEL // (3 * 256)) * 256
ROPE_BASE = 10000.0
RMS_EPS = 1e-6
GN_EPS = 1e-5

IN_SIZES = (RET_WIDTH, RET_WIDTH, RET_WIDTH, RET_WIDTH, Q_LORA, KV_LORA, MLA_ROPE_DIM)
IN_COLS = sum(IN_SIZES)
IN_SPLITS = tuple(int(v) for v in np.cumsum(IN_SIZES)[:-1])

kernel_name = "hybrid_retention_mla_block"

def rmsnorm(x, g):
    xf = x.astype(jnp.float32)
    y = xf * lax.rsqrt(jnp.mean(xf * xf, axis=-1, keepdims=True) + RMS_EPS)
    return (y * g.astype(jnp.float32)).astype(x.dtype)

def rope(x, pos):
    half = x.shape[-1] // 2
    inv = jnp.exp(-math.log(ROPE_BASE) * jnp.arange(half, dtype=jnp.float32) / half)
    ang = pos.astype(jnp.float32)[..., None] * inv
    cos = jnp.cos(ang)[:, :, None, :]
    sin = jnp.sin(ang)[:, :, None, :]
    xf = x.astype(jnp.float32)
    x1, x2 = xf[..., :half], xf[..., half:]
    return jnp.concatenate([x1 * cos - x2 * sin, x2 * cos + x1 * sin], axis=-1).astype(x.dtype)

def retention(q, k, v, gate, pos):
    B, S, H, d = q.shape
    n = S // CHUNK
    dt = q.dtype
    q = rope(q, pos)
    k = rope(k, pos) * (d ** -0.5)
    q = q.reshape(B, n, CHUNK, H, d)
    k = k.reshape(B, n, CHUNK, H, d)
    v = v.reshape(B, n, CHUNK, H, d)
    log_g = jnp.log1p(-jnp.exp2(-5.0 - jnp.arange(H, dtype=jnp.float32)))
    idx = jnp.arange(CHUNK, dtype=jnp.float32)
    intra_dec = jnp.exp(log_g[:, None, None] * jnp.abs(idx[:, None] - idx[None, :]))
    q_dec = jnp.exp(log_g[:, None] * (idx + 1.0))
    k_dec = jnp.exp(log_g[:, None] * (CHUNK - 1.0 - idx))
    c_dec = jnp.exp(log_g * CHUNK)[None, :, None, None]
    s = jnp.einsum('bnihd,bnjhd->bnhij', q, k) * intra_dec.astype(dt)
    o_intra = jnp.einsum('bnhij,bnjhe->bnihe', s, v)
    kv = jnp.einsum('bnjhd,hj,bnjhe->nbhde', k, k_dec.astype(dt), v)

    def step(state, kv_c):
        return c_dec * state + kv_c.astype(jnp.float32), state

    _, prev = lax.scan(step, jnp.zeros((B, H, d, d), jnp.float32), kv)
    o_cross = jnp.einsum('bnihd,nbhde,hi->bnihe', q, prev.astype(dt), q_dec.astype(dt))
    o = (o_intra + o_cross).reshape(B, S, H, d).astype(jnp.float32)
    mu = jnp.mean(o, axis=-1, keepdims=True)
    var = jnp.mean(jnp.square(o - mu), axis=-1, keepdims=True)
    o = ((o - mu) * lax.rsqrt(var + GN_EPS)).reshape(B, S, H * d).astype(dt)
    return o * jax.nn.silu(gate)

def mla(c_q, c_kv, k_pe, pos, q_norm_g, w_uq, kv_norm_g, w_ukv):
    B, S, _ = c_q.shape
    H = MLA_HEADS
    q = (rmsnorm(c_q, q_norm_g) @ w_uq).reshape(B, S, H, MLA_QK_DIM)
    q = jnp.concatenate([q[..., :MLA_NOPE_DIM], rope(q[..., MLA_NOPE_DIM:], pos)], axis=-1)
    kv = (rmsnorm(c_kv, kv_norm_g) @ w_ukv).reshape(B, S, H, MLA_NOPE_DIM + MLA_V_DIM)
    k_nope, v = kv[..., :MLA_NOPE_DIM], kv[..., MLA_NOPE_DIM:]
    k_rot = rope(k_pe[:, :, None, :], pos)
    k = jnp.concatenate([k_nope, jnp.broadcast_to(k_rot, (B, S, H, MLA_ROPE_DIM))], axis=-1)
    nb = S // Q_BLOCK
    qb = q.reshape(B, nb, Q_BLOCK, H, MLA_QK_DIM).transpose(1, 0, 2, 3, 4)
    key_chunk = jnp.arange(S) // CHUNK
    scale = MLA_QK_DIM ** -0.5
    neg = jnp.finfo(jnp.float32).min

    def attend(args):
        q_blk, b = args
        q_chunk = (b * Q_BLOCK + jnp.arange(Q_BLOCK)) // CHUNK
        mask = key_chunk[None, :] <= q_chunk[:, None]
        s = jnp.einsum('bqhd,bkhd->bhqk', q_blk, k).astype(jnp.float32) * scale
        s = jnp.where(mask[None, None], s, neg)
        prob = jax.nn.softmax(s, axis=-1).astype(v.dtype)
        return jnp.einsum('bhqk,bkhe->bqhe', prob, v)

    out = lax.map(attend, (qb, jnp.arange(nb)))
    return out.transpose(1, 0, 2, 3, 4).reshape(B, S, H * MLA_V_DIM)

def setup_inputs(seed: int = 0) -> dict:
    key = jax.random.key(seed)
    ks = jax.random.split(key, 20)
    f32 = jnp.float32

    def w(k, shape, fan_in):
        return jax.random.normal(k, shape, f32) * (fan_in ** -0.5)

    def gain(k, shape):
        return 1.0 + 0.02 * jax.random.normal(k, shape, f32)

    start = jax.random.randint(ks[2], (BATCH, 1), 0, 4096, dtype=jnp.int32)
    positions = (start + jnp.arange(SEQ, dtype=jnp.int32)[None, :]).astype(jnp.int32)
    return {
        "x": jax.random.normal(ks[0], (BATCH, SEQ, D_MODEL), f32),
        "p": jax.random.normal(ks[1], (DEPTH, BATCH, SEQ, D_PLE), f32),
        "positions": positions,
        "mix_norm_g": gain(ks[3], (DEPTH, D_MODEL)),
        "w_in": w(ks[4], (DEPTH, D_MODEL, IN_COLS), D_MODEL),
        "q_norm_g": gain(ks[5], (DEPTH, Q_LORA)),
        "w_uq": w(ks[6], (DEPTH, Q_LORA, MLA_HEADS * MLA_QK_DIM), Q_LORA),
        "kv_norm_g": gain(ks[7], (DEPTH, KV_LORA)),
        "w_ukv": w(ks[8], (DEPTH, KV_LORA, MLA_HEADS * (MLA_NOPE_DIM + MLA_V_DIM)), KV_LORA),
        "w_o": w(ks[9], (DEPTH, D_MIX, D_MODEL), D_MIX),
        "ffn_norm_g": gain(ks[10], (DEPTH, D_MODEL)),
        "w_ffn_gate": w(ks[11], (DEPTH, D_MODEL, D_FF), D_MODEL),
        "w_ffn_up": w(ks[12], (DEPTH, D_MODEL, D_FF), D_MODEL),
        "w_ffn_down": w(ks[13], (DEPTH, D_FF, D_MODEL), D_FF),
        "ple_norm_g": gain(ks[14], (DEPTH, D_MODEL)),
        "w_ple_gate": w(ks[15], (DEPTH, D_MODEL, D_MODEL), D_MODEL),
        "w_ple_proj": w(ks[16], (DEPTH, D_PLE, D_MODEL), D_PLE),
        "final_norm_g": gain(ks[17], (D_MODEL,)),
    }

def reference(x, p, positions, mix_norm_g, w_in, q_norm_g, w_uq, kv_norm_g, w_ukv, w_o,
              ffn_norm_g, w_ffn_gate, w_ffn_up, w_ffn_down, ple_norm_g, w_ple_gate,
              w_ple_proj, final_norm_g):
    B, S, _ = x.shape
    for i in range(DEPTH):
        h = rmsnorm(x, mix_norm_g[i])
        z = h @ w_in[i]
        rq, rk, rv, rg, c_q, c_kv, k_pe = jnp.split(z, IN_SPLITS, axis=-1)
        shp = (B, S, RET_HEADS, RET_HEAD_DIM)
        ret = retention(rq.reshape(shp), rk.reshape(shp), rv.reshape(shp), rg, positions)
        att = mla(c_q, c_kv, k_pe, positions, q_norm_g[i], w_uq[i], kv_norm_g[i], w_ukv[i])
        x = x + jnp.concatenate([ret, att], axis=-1) @ w_o[i]
        h = rmsnorm(x, ffn_norm_g[i])
        x = x + (jax.nn.silu(h @ w_ffn_gate[i]) * (h @ w_ffn_up[i])) @ w_ffn_down[i]
        gate = jax.nn.sigmoid(rmsnorm(x, ple_norm_g[i]) @ w_ple_gate[i])
        x = x + gate * (p[i] @ w_ple_proj[i])
    return rmsnorm(x, final_norm_g)


_drawn_inputs = setup_inputs


def setup_inputs(seed=0):
    import zlib

    import numpy as np

    out = dict(_drawn_inputs(seed))
    spreads = {}
    factors = {'mix_norm_g': 3.549,
     'q_norm_g': 8.0,
     'kv_norm_g': 8.0,
     'ffn_norm_g': 4.538,
     'ple_norm_g': 8.0,
     'final_norm_g': 2.872}
    for name, (base, spread) in spreads.items():
        noise = np.random.default_rng([zlib.crc32(name.encode()), seed]).standard_normal(out[name].shape)
        drawn = base * np.exp(spread * noise) if base else spread * noise
        out[name] = __import__('jax').numpy.asarray(drawn.astype(out[name].dtype))
    for name, factor in factors.items():
        out[name] = (out[name] * factor).astype(out[name].dtype)
    return out
```

```python
from contextlib import ExitStack

import numpy as np

import concourse.bass as bass
from concourse import mybir

F32 = mybir.dt.float32
F32R = mybir.dt.float32r
I32 = mybir.dt.int32
ALU = mybir.AluOpType
ACT = mybir.ActivationFunctionType
AXX = mybir.AxisListType.X

P = 128
S = 1024
D = 1024
T = S // P
K = D // P
CHUNK = 64
HEADS = 4
HD = 128
ROPE = 64
QL, KVL = 256, 128
MLA_IN = QL + KVL + ROPE
QK = HD + ROPE
FF = 2816
GROUP = 2
NG = FF // P // GROUP
PLE = 256
HALF = 512
EPS, GN_EPS = 1e-6, 1e-5
SCALE = float(QK) ** -0.5
MASKED = -3.0e38
TWO_PI = 2.0 * np.pi
PI_A = 6.28125
PI_B = float(np.float32(np.floor((TWO_PI - PI_A) * 2.0 ** 18) / 2.0 ** 18))
PI_C = float(TWO_PI - PI_A - PI_B)
ROUND = 1.5 * 2.0 ** 23

C_IDENT, C_INV, C_DEC = 0, P, P + 64
C_KDEC = C_DEC + HEADS * P
C_CDEC = C_KDEC + HEADS
C_END = C_CDEC + HEADS


def shape_tables():
    table = np.zeros((P, C_END), np.float32)
    table[:, C_IDENT:C_IDENT + P] = np.eye(P)
    half = HD // 2
    scaled = np.float32(-np.log(10000.0)) * np.arange(half, dtype=np.float32) / np.float32(half)
    table[:, C_INV:C_INV + half] = np.exp(scaled)
    log_g = np.log1p(-np.exp2(-5.0 - np.arange(HEADS)))
    i = np.arange(P)
    query_decay = np.zeros((P, HEADS * P), np.float32)
    for h in range(HEADS):
        seen = (i[:, None] // CHUNK) <= (i[None, :] // CHUNK)
        decay = np.exp(log_g[h] * np.abs(i[:, None] - i[None, :])) * seen * HD ** -0.5
        table[:, C_DEC + h * P:C_DEC + (h + 1) * P] = decay
        table[:, C_KDEC + h] = np.exp(log_g[h] * (P - 1.0 - i)) * HD ** -0.5
        table[:, C_CDEC + h] = np.exp(log_g[h] * P)
        query_decay[:, h * P:(h + 1) * P] = np.exp(log_g[h] * (i + 1.0))[None, :]
    return table, query_decay


def build(nc, t_in, out):
    ctx = ExitStack()
    with ctx:
        def sb(name, shape, dt=F32):
            return ctx.enter_context(nc.sbuf_tensor(name, shape, dt))

        def sem(name):
            return ctx.enter_context(nc.semaphore(name))

        X = sb("X", [P, T * D])
        HTH = sb("HTH", [P, K, S], F32R)
        HTL = sb("HTL", [P, K, S], F32R)
        WF = sb("WF", [P, 20480], F32R)
        RAW = sb("RAW", [P, 4096])
        TMP = sb("TMP", [P, 4096])
        TAB = sb("TAB", [P, 2, T, 64])
        CST = sb("CST", [P, C_END])
        GB = sb("GB", [P, D])
        GC = sb("GC", [P, QL + KVL])
        POS = sb("POS", [P, T], I32)
        POSF = sb("POSF", [P, T])
        NEGH = sb("NEGH", [P, 16])
        PIH = sb("PIH", [P, 1])
        GNE = sb("GNE", [P, 1])
        ST = sb("ST", [P, 128])
        PS = ctx.enter_context(nc.psum_tensor("PS", [P, 8, HALF], F32))

        ident = CST[:, C_IDENT:C_IDENT + P]
        X3 = X[:, :].rearrange("p (t n) -> p t n", t=T)
        COS, SIN = TAB[:, 0], TAB[:, 1]
        JUNK = TAB[:, :, :, :].rearrange("p a t n -> p (a t n)")
        RET = X[:, 0:T * HALF].rearrange("p (t n) -> p t n", t=T)
        CKV = X[:, 4096:4096 + T * MLA_IN].rearrange("p (t n) -> p t n", t=T)
        QDEC = X[:, 4096 + T * MLA_IN:8192]

        def tmp(a, n):
            return TMP[:, a:a + n]

        def bank(b, n=HALF):
            return PS[:, b, 0:n]

        class Norm:
            def __init__(self, name):
                self.squares = sem(name + "_squares")
                self.mean = sem(name + "_mean")
                self.rstd = sem(name + "_rstd")
                self.normed = sem(name + "_normed")
                self.turned = sem(name + "_turned")
                self.hi = sem(name + "_hi")
                self.lo = sem(name + "_lo")

        n_mix, n_ffn, n_ple, n_out = Norm("mix"), Norm("ffn"), Norm("ple"), Norm("final")
        s_att = sem("s_att")
        s_const, s_gain = sem("s_const"), sem("s_gain")
        s_x = [sem(f"s_x{i}") for i in range(4)]
        s_raw = [sem(f"s_raw{i}") for i in range(4)]
        s_rawb = [sem(f"s_rawb{i}") for i in range(4)]
        w_hi, w_lo = sem("w_hi"), sem("w_lo")
        s_setup, s_tab, s_sin = sem("s_setup"), sem("s_tab"), sem("s_sin")
        lat_done, ckv_out = sem("lat_done"), sem("ckv_out")

        def big(slot, part, k, n=HALF):
            a = slot * 8192 + part * 4096 + k * HALF
            return WF[:, a:a + n]

        def raw(m):
            return RAW[:, (m % 4) * 1024:(m % 4) * 1024 + 1024]

        M_LAT, M_RET, M_WO0, M_WO1, M_FFN = 0, 4, 20, 24, 28
        M_PLE = M_FFN + NG * 6

        def arrived(eng, m, more=0):
            eng.wait_ge(s_raw[m % 4], 16 * (m // 4 + 1) + more)

        def split_hi(e, m, dst, src, more=0):
            arrived(e, m, more * 4)
            nc.scalar.copy(dst, src).then_inc(w_hi, 1)

        def split_lo(e, m, dst, hi, src, more=0):
            e.wait_ge(w_hi, m + 1 + more)
            nc.vector.tensor_tensor(dst, src, hi.bitcast(F32), ALU.subtract).then_inc(w_lo, 1)

        def granule_hi(e, g, c, m, n=HALF, more=0):
            a = g * 8192 + c * 1024
            src, dst = raw(m), WF[:, a:a + 1024]
            if n < HALF:
                src = src[:, 0:2 * n].rearrange("p (k n) -> p k n", k=2)
                dst = dst.rearrange("p (k n) -> p k n", k=2)[:, :, 0:n]
            split_hi(e, m, dst, src, more)

        def granule_lo(e, g, c, m, n=HALF, more=0):
            a = g * 8192 + c * 1024
            src, hi, dst = raw(m), WF[:, a:a + 1024], WF[:, a + 4096:a + 5120]
            if n < HALF:
                src = src[:, 0:2 * n].rearrange("p (k n) -> p k n", k=2)
                hi = hi.rearrange("p (k n) -> p k n", k=2)[:, :, 0:n]
                dst = dst.rearrange("p (k n) -> p k n", k=2)[:, :, 0:n]
            split_lo(e, m, dst, hi, src, more)

        def product(dst, tile, slot, n=HALF):
            tok = slice(tile * P, tile * P + P)
            for k in range(K):
                w_h, w_l = big(slot, 0, k, n), big(slot, 1, k, n)
                nc.tensor.matmul(dst, HTH[:, k, tok], w_h, start=(k == 0), stop=False)
                nc.tensor.matmul(dst, HTH[:, k, tok], w_l, start=False, stop=False)
                last = nc.tensor.matmul(dst, HTL[:, k, tok], w_h, start=False, stop=(k == K - 1))
            return last

        def norm_squares(e, s, t, col, src, junk):
            nc.scalar.activation(junk, src, ACT.Square, accum_out=ST[:, col + t:col + t + 1]).then_inc(s.squares, 1)

        def norm_rstd(e, s, t, col):
            e.wait_ge(s.squares, t + 1)
            c = ST[:, col + t:col + t + 1]
            r = ST[:, col + 8 + t:col + 9 + t]
            nc.gpsimd.tensor_scalar(c, c, 1.0 / D, EPS, ALU.mult, ALU.add).then_inc(s.mean, 1)
            e.wait_ge(s.mean, t + 1)
            nc.gpsimd.tensor_tensor(r, c, NEGH[:, 0:1], ALU.pow).then_inc(s.rstd, 1)

        def norm_rows(e, s, t, col, src, dst):
            e.wait_ge(s.rstd, t + 1)
            r = ST[:, col + 8 + t:col + 9 + t]
            nc.vector.scalar_tensor_tensor(dst, src, r, GB[:, :], ALU.mult, ALU.mult).then_inc(s.normed, 1)

        def norm_turn(e, s, t):
            e.wait_ge(s.normed, t + 1)
            if t >= 2:
                e.wait_ge(s.lo, 2 * t - 2)
            b = 2 * (t % 2)
            for k in range(K):
                last = nc.tensor.transpose(PS[:, b + k // 4, (k % 4) * P:(k % 4) * P + P],
                                           tmp(2048 + (t % 2) * 1024 + k * P, P), ident)
            last.then_inc(s.turned, 1)

        def turned_hi(e, s, t):
            e.wait_ge(s.turned, t + 1)
            for j in range(2):
                src = bank(2 * (t % 2) + j).rearrange("p (k n) -> p k n", k=4)
                nc.scalar.copy(HTH[:, 4 * j:4 * j + 4, t * P:t * P + P], src).then_inc(s.hi, 1)

        def turned_lo(e, s, t):
            for j in range(2):
                e.wait_ge(s.hi, 2 * t + j + 1)
                src = bank(2 * (t % 2) + j).rearrange("p (k n) -> p k n", k=4)
                d = slice(t * P, t * P + P)
                nc.vector.tensor_tensor(HTL[:, 4 * j:4 * j + 4, d], src,
                                        HTH[:, 4 * j:4 * j + 4, d].bitcast(F32), ALU.subtract).then_inc(s.lo, 1)

        def sp_1(e):
            e.dma_start(X3[:, 0, :], t_in["x"][0:P, :]).then_inc(s_x[0], 16)
            e.dma_start(CST[:, :], t_in["table"]).then_inc(s_const, 16)
            e.dma_start(GB[:, :], t_in["mix_norm_g"].partition_broadcast(P)).then_inc(s_gain, 16)
            w = t_in["w_in"].rearrange("(k p) n -> p k n", p=P)
            for m in range(4):
                e.dma_start(raw(m)[:, 0:2 * MLA_IN].rearrange("p (k n) -> p k n", k=2),
                            w[:, 2 * m:2 * m + 2, 4 * HALF:4 * HALF + MLA_IN]).then_inc(s_raw[m % 4], 16)
                if m < 3:
                    e.dma_start(X3[:, m + 1, :], t_in["x"][(m + 1) * P:(m + 2) * P, :]).then_inc(s_x[m + 1], 16)
            e.dma_start(POS[:, :], t_in["positions"]).then_inc(s_const, 16)
            e.dma_start(QDEC, t_in["query_decay"]).then_inc(s_const, 16)
            e.dma_start(GC[:, 0:QL], t_in["q_norm_g"].partition_broadcast(P)).then_inc(s_const, 16)
            e.dma_start(GC[:, QL:QL + KVL], t_in["kv_norm_g"].partition_broadcast(P)).then_inc(s_const, 16)
            for t in range(4, T):
                e.wait_ge(n_mix.normed, t - 3)
                e.dma_start(X3[:, t % 4, :], t_in["x"][t * P:(t + 1) * P, :]).then_inc(s_x[t % 4], 16)

        def pool_setup(e):
            nc.gpsimd.memset(NEGH[:, :], -0.5).then_inc(s_setup, 1)
            nc.gpsimd.memset(PIH[:, :], float(np.pi / 2)).then_inc(s_setup, 1)
            nc.gpsimd.memset(GNE[:, :], GN_EPS).then_inc(s_setup, 1)
            e.wait_ge(s_setup, 3)

        def pool_1(e):
            pool_setup(e)
            for t in range(T):
                norm_rstd(e, n_mix, t, 0)
            e.wait_ge(ckv_out, 3 * T)
            q, kv = ST[:, 16:24], ST[:, 24:32]
            nc.gpsimd.tensor_scalar(q, q, 1.0 / QL, EPS, ALU.mult, ALU.add).then_inc(s_setup, 1)
            nc.gpsimd.tensor_scalar(kv, kv, 1.0 / KVL, EPS, ALU.mult, ALU.add).then_inc(s_setup, 1)
            e.wait_ge(s_setup, 5)
            nc.gpsimd.tensor_tensor(ST[:, 32:48], ST[:, 16:32], NEGH[:, :], ALU.pow).then_inc(s_setup, 1)

        def act_1(e):
            def squares(t):
                e.wait_ge(s_x[t % 4], 16 * (t // 4 + 1))
                if t:
                    e.wait_ge(n_mix.squares, t)
                norm_squares(e, n_mix, t, 0, X3[:, t % 4, :], tmp(0, 1024))
            squares(0)
            for c in range(4):
                granule_hi(e, 0, c, c, MLA_IN)
            squares(1)
            for t in range(T):
                turned_hi(e, n_mix, t)
                if t + 2 < T:
                    squares(t + 2)
                if t >= 1:
                    latent_out(e, t - 1)
                if t >= 4:
                    e.wait_ge(s_rawb[t - 4], 16)
                    granule_hi(e, 1, t - 4, M_RET + t - 4)
                if t == 3:
                    tables_act(e)
            latent_out(e, T - 1)

        def latent_out(e, t):
            e.wait_ge(lat_done, t + 1)
            b = PS[:, 4 + t % 2]
            if t:
                e.wait_ge(ckv_out, 3 * t)
            nc.scalar.activation(GC2, b[:, 0:QL], ACT.Square, accum_out=ST[:, 16 + t:17 + t]).then_inc(ckv_out, 1)
            nc.scalar.activation(GC3, b[:, QL:QL + KVL], ACT.Square, accum_out=ST[:, 24 + t:25 + t]).then_inc(ckv_out, 1)
            nc.scalar.copy(CKV[:, t, :], b[:, 0:MLA_IN]).then_inc(ckv_out, 1)

        GC2, GC3 = tmp(1024, QL), tmp(1280, KVL)

        def tables_dve(e):
            n = [0]
            ang = COS
            turns = tmp(1536, 512).rearrange("p (t n) -> p t n", t=T)

            def link(i):
                n[0] += 1
                i.then_inc(s_tab, 1)
                e.wait_ge(s_tab, n[0])

            e.wait_ge(s_const, 16 * 5)
            e.wait_ge(s_setup, 2)
            link(nc.vector.tensor_copy(POSF[:, :], POS[:, :]))
            link(nc.vector.tensor_tensor(ang, POSF[:, :].unsqueeze(2).to_broadcast([P, T, 64]),
                                         CST[:, C_INV:C_INV + 64].unsqueeze(1).to_broadcast([P, T, 64]), ALU.mult))
            link(nc.vector.tensor_scalar(turns, ang, 1.0 / TWO_PI, ROUND, ALU.mult, ALU.add))
            link(nc.vector.tensor_scalar(turns, turns, ROUND, None, ALU.subtract))
            for part in (PI_A, PI_B, PI_C):
                link(nc.vector.scalar_tensor_tensor(ang, turns, -part, ang, ALU.mult, ALU.add))
            link(nc.vector.tensor_scalar(ang, ang, 3.1415925, -3.1415925, ALU.min, ALU.max))
            link(nc.vector.scalar_tensor_tensor(turns, ang, -1.0, ang, ALU.mult, ALU.max))

        N_TAB = 9

        def tables_act(e):
            e.wait_ge(s_tab, N_TAB)
            turns = tmp(1536, 512).rearrange("p (t n) -> p t n", t=T)
            nc.scalar.activation(SIN, COS, ACT.Sin).then_inc(s_sin, 1)
            e.wait_ge(s_sin, 1)
            nc.scalar.activation(COS, turns, ACT.Sin, bias=PIH[:, 0:1], scale=-1.0).then_inc(s_sin, 1)

        def dve_1(e):
            def rows(t):
                if t == 0:
                    e.wait_ge(s_gain, 16)
                if t >= 2:
                    e.wait_ge(n_mix.turned, t - 1)
                norm_rows(e, n_mix, t, 0, X3[:, t % 4, :], tmp(2048 + (t % 2) * 1024, 1024))
            rows(0)
            for c in range(4):
                granule_lo(e, 0, c, c, MLA_IN)
            rows(1)
            for t in range(T):
                turned_lo(e, n_mix, t)
                if t + 2 < T:
                    rows(t + 2)
                if t >= 4:
                    granule_lo(e, 1, t - 4, M_RET + t - 4)
                if t == 2:
                    tables_dve(e)

        def pe_1(e):
            e.wait_ge(s_const, 16)
            norm_turn(e, n_mix, 0)
            for t in range(T):
                if t + 1 < T:
                    norm_turn(e, n_mix, t + 1)
                if t == 0:
                    e.wait_ge(w_lo, 4)
                e.wait_ge(n_mix.lo, 2 * t + 2)
                if t >= 2:
                    e.wait_ge(ckv_out, 3 * (t - 1))
                product(bank(4 + t % 2, MLA_IN), t, 0, MLA_IN).then_inc(lat_done, 1)

        z_proj, z_out = sem("z_proj"), sem("z_out")
        rot_ab, rot = sem("rot_ab"), sem("rot")
        qk_turned, qk_out, qd_out = sem("qk_turned"), sem("qk_out"), sem("qd_out")
        r_scores, r_probs, r_okv = sem("r_scores"), sem("r_probs"), sem("r_okv")
        r_state = sem("r_state")
        gn_stats, gn_mean, gn_rstd, gn_rows, r_done = (sem("gn_stats"), sem("gn_mean"), sem("gn_rstd"),
                                                       sem("gn_rows"), sem("r_done"))
        UNITS = 16

        def Z(u):
            return tmp((u % 4) * 512, 512)

        AB = tmp(2048, 512)
        PT2 = [tmp(2560, 128), tmp(2688, 128)]
        ON = [tmp(2816, 128), tmp(2944, 128)]
        QKT = [tmp(3072, 256), tmp(3328, 256)]
        QDT = [tmp(3584, 128), tmp(3712, 128)]
        STATE = tmp(3840, 128)
        KD = [GB[:, c * P:c * P + P] for c in range(4)]
        B_T, B_S, B_O, B_KV = 0, 1, 2, 3

        def sp_retention(e):
            w = t_in["w_in"][:, 0:4 * HALF].rearrange("(k p) (s c) -> p k s c", p=P, s=4)
            with e.Fori(0, HEADS) as h:
                for c in range(4):
                    e.wait_ge(w_lo, M_RET + c - 3 + 4 * h)
                    for k in range(2):
                        e.dma_start(RAW[:, c * 1024 + k * HALF:c * 1024 + (k + 1) * HALF].rearrange("p (s c) -> p s c", s=4),
                                    w[:, 2 * c + k, :, bass.ds(h * HD, HD)]).then_inc((s_rawb if k else s_raw)[c], 16)

        def sp_out_weights(e, half, m0):
            w = t_in["w_o"].rearrange("(k p) n -> p k n", p=P)
            for c in range(4):
                e.wait_ge(w_lo, m0 + c - 3)
                for k in range(2):
                    e.dma_start(raw(m0 + c)[:, k * HALF:(k + 1) * HALF],
                                w[:, 2 * c + k, half * HALF:(half + 1) * HALF]).then_inc((s_rawb if k else s_raw)[c], 16)

        def pe_2(e):
            e.wait_ge(ckv_out, 3 * T)
            with e.Fori(0, HEADS * T // UNITS) as i:
                B = i * UNITS
                for s in range(UNITS + 3):
                    if s < UNITS:
                        if s % T == 0:
                            e.wait_ge(w_lo, M_RET + 4 * (s // T + 1) + i * 8)
                        e.wait_ge(z_out, B * 2 + 2 * max(0, s - 1))
                        product(bank(4 + s % 2), s % T, 1 - s // T).then_inc(z_proj, 1)
                    u = s - 1
                    if 0 <= u < UNITS:
                        e.wait_ge(rot, B * 3 + 3 * u + 2)
                        e.wait_ge(qk_out, B + u)
                        nc.tensor.transpose(PS[:, B_T, 0:P], Z(u)[:, 0:P], ident)
                        nc.tensor.transpose(PS[:, B_T, P:2 * P], Z(u)[:, P:2 * P], ident).then_inc(qk_turned, 1)
                    u = s - 2
                    if 0 <= u < UNITS:
                        e.wait_ge(qk_out, B + u + 1)
                        e.wait_ge(r_probs, B + u)
                        nc.tensor.matmul(bank(B_S, P), QKT[u % 2][:, P:2 * P], QKT[u % 2][:, 0:P],
                                         start=True, stop=True).then_inc(r_scores, 1)
                    u = s - 3
                    if 0 <= u < UNITS:
                        e.wait_ge(r_probs, B + u + 1)
                        e.wait_ge(qd_out, B + u + 1)
                        e.wait_ge(rot, B * 3 + 3 * u + 3)
                        e.wait_ge(r_state, B + u)
                        e.wait_ge(gn_rows, B + u)
                        V = Z(u)[:, 2 * P:3 * P]
                        nc.tensor.matmul(bank(B_O, P), PT2[u % 2], V, start=True, stop=(u % T == 0))
                        if u % T:
                            nc.tensor.matmul(bank(B_O, P), QDT[u % 2], STATE, start=False, stop=True)
                        nc.tensor.matmul(bank(B_KV, P), KD[u % 4], V, start=True, stop=True).then_inc(r_okv, 1)

        def act_2(e):
            with e.Fori(0, HEADS * T // UNITS) as i:
                B = i * UNITS
                for s in range(UNITS + 3):
                    if s < UNITS:
                        e.wait_ge(z_proj, B + s + 1)
                        e.wait_ge(r_done, B + max(0, s - 3))
                        e.wait_ge(r_okv, B + max(0, s - 3))
                        b = PS[:, 4 + s % 2]
                        nc.scalar.copy(Z(s)[:, 0:3 * P], b[:, 0:3 * P]).then_inc(z_out, 1)
                        nc.scalar.activation(Z(s)[:, 3 * P:4 * P], b[:, 3 * P:4 * P], ACT.Silu).then_inc(z_out, 1)
                    u = s - 1
                    if 0 <= u < UNITS:
                        e.wait_ge(qk_turned, B + u + 1)
                        e.wait_ge(r_scores, B + max(0, u - 1))
                        e.wait_ge(qd_out, B + max(0, u - 1))
                        nc.scalar.copy(QKT[u % 2], bank(B_T, 2 * P)).then_inc(qk_out, 1)
                    if s < UNITS and s % 2 == 0:
                        hh, c = s // T, s % T // 2
                        e.wait_ge(z_proj, B + hh * T)
                        piece_m = M_RET + 4 + 4 * hh + c
                        e.wait_ge(s_raw[c], 16 * (piece_m // 4 + 1) + i * 32)
                        e.wait_ge(s_rawb[c], 16 * (hh + 2) + i * 32)
                        a = hh * 8192 + c * 1024
                        nc.scalar.copy(WF[:, a:a + 1024], RAW[:, c * 1024:(c + 1) * 1024]).then_inc(w_hi, 1)

        def pool_2(e):
            e.wait_ge(s_const, 16 * 5)
            with e.Fori(0, HEADS * T // UNITS) as i:
                B = i * UNITS
                for s in range(UNITS + 3):
                    if s < UNITS:
                        z = Z(s)[:, 0:2 * P].rearrange("p (q h n) -> p q h n", q=2, h=2)
                        ab = AB.rearrange("p (x q h n) -> p x q h n", x=2, q=2, h=2)
                        e.wait_ge(rot_ab, B * 2 + 2 * s + 2)
                        nc.gpsimd.tensor_tensor(z[:, :, 0], ab[:, 0, :, 0], ab[:, 1, :, 1], ALU.subtract).then_inc(rot, 1)
                        nc.gpsimd.tensor_tensor(z[:, :, 1], ab[:, 0, :, 1], ab[:, 1, :, 0], ALU.add).then_inc(rot, 1)
                        e.wait_ge(rot, B * 3 + 3 * s + 2)
                        e.wait_ge(r_okv, B + max(0, s - 3))
                        dec = HDEC[s // T]
                        nc.gpsimd.tensor_tensor(KD[s % 4], Z(s)[:, P:2 * P], dec.to_broadcast([P, P]),
                                                ALU.mult).then_inc(rot, 1)
                    u = s - 3
                    if 0 <= u < UNITS:
                        e.wait_ge(gn_stats, B * 2 + 2 * u + 2)
                        var, r = ST[:, 65:66], ST[:, 66:67]
                        nc.gpsimd.tensor_tensor(r, var, GNE[:, 0:1], ALU.add).then_inc(gn_mean, 1)
                        e.wait_ge(gn_mean, B + u + 1)
                        nc.gpsimd.tensor_tensor(r, r, NEGH[:, 0:1], ALU.pow).then_inc(gn_rstd, 1)
                        e.wait_ge(gn_rows, B + u + 1)
                        hcol = i * 2 * HD + (u // T) * HD
                        nc.gpsimd.tensor_tensor(RET[:, u % T, bass.ds(hcol, HD)], ON[u % 2],
                                                Z(u)[:, 3 * P:4 * P], ALU.mult).then_inc(r_done, 1)

        HCON = sb("HCON", [P, 2 * 2])
        HDEC = [HCON[:, 0:1], HCON[:, 1:2]]
        HCD = [HCON[:, 2:3], HCON[:, 3:4]]
        s_hcon = sem("s_hcon")

        def dve_2(e):
            with e.Fori(0, HEADS * T // UNITS) as i:
                B = i * UNITS
                e.wait_ge(rot, B * 3)
                e.wait_ge(r_state, B)
                nc.vector.tensor_copy(HCON[:, 0:2], CST[:, bass.ds(i * 2 + C_KDEC, 2)]).then_inc(s_hcon, 1)
                nc.vector.tensor_copy(HCON[:, 2:4], CST[:, bass.ds(i * 2 + C_CDEC, 2)]).then_inc(s_hcon, 1)
                e.wait_ge(s_hcon, i * 2 + 2)
                for s in range(UNITS + 3):
                    if s < UNITS:
                        z = Z(s)[:, 0:2 * P].rearrange("p (g n) -> p g n", g=4)
                        ab = AB.rearrange("p (x g n) -> p x g n", x=2, g=4)
                        if s == 0:
                            e.wait_ge(s_sin, 2)
                        e.wait_ge(z_out, B * 2 + 2 * s + 2)
                        e.wait_ge(rot, B * 3 + (3 * s - 1 if s else 0))
                        for x, table in enumerate((COS, SIN)):
                            w = table[:, s % T].unsqueeze(1).to_broadcast([P, 4, 64])
                            nc.vector.tensor_tensor(ab[:, x], z, w, ALU.mult).then_inc(rot_ab, 1)
                    u = s - 1
                    if 0 <= u < UNITS:
                        e.wait_ge(qk_out, B + u + 1)
                        e.wait_ge(r_okv, B + max(0, u - 1))
                        col = i * 2 * P + (u // T) * P
                        nc.vector.tensor_tensor(QDT[u % 2], QKT[u % 2][:, 0:P], QDEC[:, bass.ds(col, P)],
                                                ALU.mult).then_inc(qd_out, 1)
                    u = s - 2
                    if 0 <= u < UNITS:
                        e.wait_ge(r_scores, B + u + 1)
                        e.wait_ge(r_okv, B + max(0, u - 1))
                        col = i * 2 * P + ((u // T) * P + C_DEC)
                        nc.vector.tensor_tensor(PT2[u % 2], bank(B_S, P), CST[:, bass.ds(col, P)],
                                                ALU.mult).then_inc(r_probs, 1)
                    u = s - 3
                    if 0 <= u < UNITS:
                        e.wait_ge(r_okv, B + u + 1)
                        nc.vector.bn_stats(ST[:, 68:74], bank(B_O, P)).then_inc(gn_stats, 1)
                        e.wait_ge(r_state, B + u)
                        e.wait_ge(gn_stats, B * 2 + 2 * u + 1)
                        if u % T:
                            nc.vector.scalar_tensor_tensor(STATE, STATE, HCD[u // T], bank(B_KV, P),
                                                           ALU.mult, ALU.add).then_inc(r_state, 1)
                        else:
                            nc.vector.tensor_copy(STATE, bank(B_KV, P)).then_inc(r_state, 1)
                        nc.vector.bn_aggr(ST[:, 64:66], ST[:, 68:74]).then_inc(gn_stats, 1)
                        e.wait_ge(gn_rstd, B + u + 1)
                        e.wait_ge(r_done, B + max(0, u - 1))
                        nc.vector.tensor_scalar(ON[u % 2], bank(B_O, P), ST[:, 64:65], ST[:, 66:67],
                                                ALU.subtract, ALU.mult).then_inc(gn_rows, 1)
                    if s < UNITS and s % 2 == 0:
                        hh, c = s // T, s % T // 2
                        e.wait_ge(z_proj, B + hh * T)
                        e.wait_ge(w_hi, M_RET + 4 + 4 * hh + c + 1 + i * 8)
                        a = hh * 8192 + c * 1024
                        nc.vector.tensor_tensor(WF[:, a + 4096:a + 5120], RAW[:, c * 1024:(c + 1) * 1024],
                                                WF[:, a:a + 1024].bitcast(F32), ALU.subtract).then_inc(w_lo, 1)

        lat_rows, lat_rope, lat_turned, lat_hi, lat_lo = (sem("lat_rows"), sem("lat_rope"), sem("lat_turned"),
                                                          sem("lat_hi"), sem("lat_lo"))
        a_w, a_w_lo = sem("a_w"), sem("a_w_lo")
        a_proj, a_hi, a_lo = sem("a_proj"), sem("a_hi"), sem("a_lo")
        a_rope, a_qturn, a_qr = sem("a_rope"), sem("a_qturn"), sem("a_qr")
        a_scores, a_mask, a_max, a_bias = sem("a_scores"), sem("a_mask"), sem("a_max"), sem("a_bias")
        a_exp, a_rec, a_prob, a_turn = sem("a_exp"), sem("a_rec"), sem("a_prob"), sem("a_turn")
        a_pt_hi, a_pt_lo, a_pv, a_o_hi, a_o_lo = (sem("a_pt_hi"), sem("a_pt_lo"), sem("a_pv"),
                                                  sem("a_o_hi"), sem("a_o_lo"))
        CT = [WF[:, 0:4096].rearrange("p (k n) -> p k n", k=4), WF[:, 4096:8192].rearrange("p (k n) -> p k n", k=4)]
        WS = 16384
        WQ = [WF[:, WS + p * 640:WS + p * 640 + 384].rearrange("p (k n) -> p k n", k=2) for p in range(2)]
        WKV = [WF[:, WS + p * 640 + 384:WS + p * 640 + 640] for p in range(2)]
        QR = WF[:, WS + 1280:WS + 2304]
        HT = [HTH, HTL]
        QT, KT, VV, PTT = 0, 1, 2, 3
        CN = [tmp(0, 384), tmp(384, 384)]
        KR = tmp(1024, 1024).rearrange("p (t n) -> p t n", t=T)
        QS = tmp(2560, 1024).rearrange("p (t n) -> p t n", t=T)
        QRF = tmp(2048, 512)
        RA = tmp(3584, 512)
        RB = GB[:, 512:1024]

        def sp_3(e):
            e.wait_ge(w_lo, M_WO1)
            for k in range(2):
                e.dma_start(RAW[:, k * 1024:k * 1024 + 768], t_in["w_uq"][k * P:(k + 1) * P, :]).then_inc(s_att, 16)
            for k in range(2):
                e.dma_start(RAW[:, 2560 + k * 512:3072 + k * 512],
                            t_in["w_ukv"][:, k * 512:(k + 1) * 512]).then_inc(s_att, 16)
            e.wait_ge(lat_rows, 2 * T)
            e.wait_ge(lat_rope, 2)
            for t in range(4, T):
                e.dma_start(X3[:, t, :], t_in["x"][t * P:(t + 1) * P, :]).then_inc(s_x[t % 4], 16)

        def rope64(e, s, base, z, a, b, dst):
            a4, b4 = (x.rearrange("p (t h n) -> p t h n", t=T, h=2) for x in (a, b))
            for x, table in ((a4, COS), (b4, SIN)):
                w = table[:, :, 0:64:2].unsqueeze(2).to_broadcast([P, T, 2, 32])
                nc.vector.tensor_tensor(x, z, w, ALU.mult).then_inc(s, 1)
            e.wait_ge(s, base + 2)
            nc.vector.tensor_tensor(dst[:, :, 0:32], a4[:, :, 0], b4[:, :, 1], ALU.subtract).then_inc(s, 1)
            nc.vector.tensor_tensor(dst[:, :, 32:64], a4[:, :, 1], b4[:, :, 0], ALU.add).then_inc(s, 1)
            e.wait_ge(s, base + 4)

        NU = HEADS * T // UNITS * UNITS

        def dve_3a(e):
            e.wait_ge(s_setup, 6)
            e.wait_ge(r_done, NU)
            e.wait_ge(gn_rows, NU)
            z = CKV[:, :, QL + KVL:MLA_IN].rearrange("p t (h n) -> p t h n", h=2)
            rope64(e, lat_rope, 0, z, RA, RB, KR[:, :, 0:64])
            nc.vector.tensor_copy(KR[:, :, 64:128], KR[:, :, 0:64]).then_inc(lat_rope, 1)
            for t in range(T):
                if t >= 2:
                    e.wait_ge(lat_turned, t - 1)
                c = CN[t % 2]
                nc.vector.scalar_tensor_tensor(c[:, 0:QL], CKV[:, t, 0:QL], ST[:, 32 + t:33 + t], GC[:, 0:QL],
                                               ALU.mult, ALU.mult).then_inc(lat_rows, 1)
                nc.vector.scalar_tensor_tensor(c[:, QL:QL + KVL], CKV[:, t, QL:QL + KVL], ST[:, 40 + t:41 + t],
                                               GC[:, QL:QL + KVL], ALU.mult, ALU.mult).then_inc(lat_rows, 1)
                if t >= 1:
                    lat_lo_tile(e, t - 1)
            lat_lo_tile(e, T - 1)

        def lat_lo_tile(e, t):
            e.wait_ge(lat_hi, t + 1)
            d = slice(t * P, t * P + P)
            nc.vector.tensor_tensor(CT[1][:, :, d], bank(t % 4).rearrange("p (k n) -> p k n", k=4),
                                    CT[0][:, :, d].bitcast(F32), ALU.subtract).then_inc(lat_lo, 1)

        def act_3a(e):
            for t in range(T):
                e.wait_ge(lat_turned, t + 1)
                nc.scalar.copy(CT[0][:, :, t * P:t * P + P],
                               bank(t % 4).rearrange("p (k n) -> p k n", k=4)).then_inc(lat_hi, 1)

        def pe_3a(e):
            e.wait_ge(gn_rows, NU)
            e.wait_ge(r_state, NU)
            e.wait_ge(lat_rope, 5)
            for t in range(T):
                e.wait_ge(lat_rows, 2 * t + 2)
                if t >= 4:
                    e.wait_ge(lat_lo, t - 3)
                for k in range(4):
                    src = CN[t % 2][:, k * P:k * P + P] if k < 3 else KR[:, t, :]
                    last = nc.tensor.transpose(PS[:, t % 4, k * P:k * P + P], src, ident)
                last.then_inc(lat_turned, 1)

        def pe_3b(e):
            e.wait_ge(lat_lo, T)
            with e.Fori(0, HEADS) as h:
                e.wait_ge(a_w_lo, h * 2 + 2)
                e.wait_ge(a_o_lo, h * T)
                for b in range(2):
                    blk = slice(b * HALF, (b + 1) * HALF)
                    for n, (x, y) in enumerate(((0, 0), (0, 1), (1, 0))):
                        last = nc.tensor.matmul(bank(b), WKV[x][:, 0:P], CT[y][:, 2, blk], start=(n == 0), stop=(n == 2))
                    last.then_inc(a_proj, 1)
                for b in range(2):
                    blk = slice(b * HALF, (b + 1) * HALF)
                    for k in range(2):
                        for n, (x, y) in enumerate(((0, 0), (0, 1), (1, 0))):
                            last = nc.tensor.matmul(bank(2 + b), WQ[x][:, k, 0:P], CT[y][:, k, blk],
                                                    start=(k + n == 0), stop=(k * n == 2))
                    last.then_inc(a_proj, 1)
                for t in range(T):
                    tok = slice(t * P, t * P + P)
                    for k in range(2):
                        for n, (x, y) in enumerate(((0, 0), (0, 1), (1, 0))):
                            last = nc.tensor.matmul(PS[:, 6, t * 64:t * 64 + 64], CT[x][:, k, tok],
                                                    WQ[y][:, k, P:QK], start=(k + n == 0), stop=(k * n == 2))
                last.then_inc(a_proj, 1)
                for t in range(T):
                    tok = slice(t * P, t * P + P)
                    for n, (x, y) in enumerate(((0, 0), (0, 1), (1, 0))):
                        last = nc.tensor.matmul(PS[:, 4 + t // 4, (t % 4) * P:(t % 4) * P + P], CT[x][:, 2, tok],
                                                WKV[y][:, P:2 * P], start=(n == 0), stop=(n == 2))
                    if t % 4 == 3:
                        last.then_inc(a_proj, 1)
                e.wait_ge(a_lo, h * 6 + 2)
                e.wait_ge(a_rope, h * 6 + 6)
                for t in range(T):
                    last = nc.tensor.transpose(PS[:, t // 4, (t % 4) * P:(t % 4) * P + P], QS[:, t, :], ident)
                last.then_inc(a_qturn, 1)

                def scores(t):
                    if t == 0:
                        e.wait_ge(a_lo, h * 6 + 6)
                        e.wait_ge(a_qr, h + 1)
                    if t >= 2:
                        e.wait_ge(a_exp, h * T + t - 1)
                    tok = slice(t * P, t * P + P)
                    n = (t + 1) * P
                    for c in range(0, n, HALF):
                        blk = slice(c, min(n, c + HALF))
                        dst = bank(2 * ((t + 1) % 2) + c // HALF, blk.stop - c)
                        nc.tensor.matmul(dst, HTH[:, QT, tok], HTH[:, KT, blk], start=True, stop=False)
                        nc.tensor.matmul(dst, HTH[:, QT, tok], HTL[:, KT, blk], start=False, stop=False)
                        nc.tensor.matmul(dst, HTL[:, QT, tok], HTH[:, KT, blk], start=False, stop=False)
                        nc.tensor.matmul(dst, QR[:, tok], CT[0][:, 3, blk], start=False, stop=False)
                        last = nc.tensor.matmul(dst, QR[:, tok], CT[1][:, 3, blk], start=False, stop=True)
                    last.then_inc(a_scores, 1)

                def turn(t):
                    e.wait_ge(a_prob, h * T + t + 1)
                    if t >= 1:
                        e.wait_ge(a_pt_lo, h * T + t)
                    for j in range(t + 1):
                        last = nc.tensor.transpose(PS[:, 4 + j // 4, (j % 4) * P:(j % 4) * P + P],
                                                   tmp((t % 2) * 1024 + j * P, P), ident)
                    last.then_inc(a_turn, 1)

                def values(t):
                    e.wait_ge(a_pt_lo, h * T + t + 1)
                    if t >= 2:
                        e.wait_ge(a_o_lo, h * T + t - 1)
                    for j in range(t + 1):
                        key = slice(j * P, j * P + P)
                        for n, (x, y) in enumerate(((0, 0), (0, 1), (1, 0))):
                            last = nc.tensor.matmul(bank(6 + t % 2, P), HT[x][:, VV, key], HT[y][:, PTT, key],
                                                    start=(j + n == 0), stop=(j == t and n == 2))
                    last.then_inc(a_pv, 1)

                scores(0)
                for t in range(T):
                    if t + 1 < T:
                        scores(t + 1)
                    if t >= 1:
                        values(t - 1)
                    turn(t)
                values(T - 1)

        def act_3b(e):
            with e.Fori(0, HEADS) as h:
                e.wait_ge(s_att, 64)
                e.wait_ge(a_proj, h * 7)
                wq = RAW[:, 0:2048].rearrange("p (k n) -> p k n", k=2)[:, :, bass.ds(h * QK, QK)]
                nc.scalar.copy(WQ[0], wq).then_inc(a_w, 1)
                nc.scalar.copy(WKV[0], RAW[:, bass.ds(h * 2 * HD + 2560, 2 * HD)]).then_inc(a_w, 1)
                for n, (where, b) in enumerate(((KT, 0), (KT, 1), (QT, 2), (QT, 3), (VV, 4), (VV, 5))):
                    if n == 0:
                        e.wait_ge(a_pv, h * T)
                    e.wait_ge(a_proj, h * 7 + n + 1 + (n >= 4))
                    blk = slice((b % 2) * HALF, (b % 2 + 1) * HALF)
                    nc.scalar.copy(HTH[:, where, blk], bank(b)).then_inc(a_hi, 1)
                e.wait_ge(a_qturn, h + 1)
                nc.scalar.copy(QR.rearrange("p (b n) -> p b n", b=2), PS[:, 0:2, :]).then_inc(a_qr, 1)

                def exp(t):
                    e.wait_ge(a_bias, h * T + t + 1)
                    if t >= 2:
                        e.wait_ge(a_turn, h * T + t - 1)
                    n = (t + 1) * P
                    src = PS[:, 2 * ((t + 1) % 2):2 * ((t + 1) % 2) + 2, :].rearrange("p b n -> p (b n)")[:, 0:n]
                    nc.scalar.activation(tmp((t % 2) * 1024, n), src, ACT.Exp, bias=ST[:, 76 + t % 2:77 + t % 2],
                                         scale=SCALE, accum_out=ST[:, 78 + t % 2:79 + t % 2]).then_inc(a_exp, 1)

                def out_hi(t):
                    e.wait_ge(a_pv, h * T + t + 1)
                    nc.scalar.copy(HTH[:, bass.ds(h + 4, 1), t * P:t * P + P],
                                   bank(6 + t % 2, P).unsqueeze(1)).then_inc(a_o_hi, 1)

                exp(0)
                for t in range(T):
                    if t + 1 < T:
                        exp(t + 1)
                    if t >= 1:
                        out_hi(t - 1)
                    e.wait_ge(a_turn, h * T + t + 1)
                    n = (t + 1) * P
                    if t >= 1:
                        e.wait_ge(a_pv, h * T + t)
                    src = PS[:, 4:6, :].rearrange("p b n -> p (b n)")[:, 0:n]
                    nc.scalar.copy(HTH[:, PTT, 0:n], src).then_inc(a_pt_hi, 1)
                out_hi(T - 1)

        def dve_3b(e):
            with e.Fori(0, HEADS) as h:
                e.wait_ge(a_w, h * 2 + 2)
                wq = RAW[:, 0:2048].rearrange("p (k n) -> p k n", k=2)[:, :, bass.ds(h * QK, QK)]
                nc.vector.tensor_tensor(WQ[1], wq, WQ[0].bitcast(F32), ALU.subtract).then_inc(a_w_lo, 1)
                nc.vector.tensor_tensor(WKV[1], RAW[:, bass.ds(h * 2 * HD + 2560, 2 * HD)], WKV[0].bitcast(F32),
                                        ALU.subtract).then_inc(a_w_lo, 1)
                for n, (where, b) in enumerate(((KT, 0), (KT, 1), (QT, 2), (QT, 3), (VV, 4), (VV, 5))):
                    if n == 4:
                        e.wait_ge(a_proj, h * 7 + 5)
                        e.wait_ge(a_qturn, h)
                        z = bank(6).rearrange("p (t h n) -> p t h n", t=T, h=2)
                        qrf = QRF.rearrange("p (t n) -> p t n", t=T)
                        rope64(e, a_rope, h * 6, z, RA, RB, qrf)
                        qs = QS[:, :, 0:64]
                        nc.vector.tensor_copy(qs.bitcast(F32R), qrf).then_inc(a_rope, 1)
                        e.wait_ge(a_rope, h * 6 + 5)
                        nc.vector.tensor_tensor(QS[:, :, 64:128], qrf, qs, ALU.subtract).then_inc(a_rope, 1)
                    e.wait_ge(a_hi, h * 6 + n + 1)
                    blk = slice((b % 2) * HALF, (b % 2 + 1) * HALF)
                    nc.vector.tensor_tensor(HTL[:, where, blk], bank(b), HTH[:, where, blk].bitcast(F32),
                                            ALU.subtract).then_inc(a_lo, 1)

                def biggest(t):
                    e.wait_ge(a_scores, h * T + t + 1)
                    if t >= 2:
                        e.wait_ge(a_exp, h * T + t - 1)
                    n = (t + 1) * P
                    src = PS[:, 2 * ((t + 1) % 2):2 * ((t + 1) % 2) + 2, :].rearrange("p b n -> p (b n)")
                    nc.vector.memset(src[0:CHUNK, n - CHUNK:n], MASKED).then_inc(a_mask, 1)
                    e.wait_ge(a_mask, h * T + t + 1)
                    nc.vector.tensor_reduce(ST[:, 74 + t % 2:75 + t % 2], src[:, 0:n], AXX, ALU.max).then_inc(a_max, 1)
                    e.wait_ge(a_max, h * T + t + 1)
                    nc.vector.tensor_scalar(ST[:, 76 + t % 2:77 + t % 2], ST[:, 74 + t % 2:75 + t % 2], -SCALE, None,
                                            ALU.mult).then_inc(a_bias, 1)

                def out_lo(t):
                    e.wait_ge(a_o_hi, h * T + t + 1)
                    d = slice(t * P, t * P + P)
                    nc.vector.tensor_tensor(HTL[:, bass.ds(h + 4, 1), d], bank(6 + t % 2, P).unsqueeze(1),
                                            HTH[:, bass.ds(h + 4, 1), d].bitcast(F32), ALU.subtract).then_inc(a_o_lo, 1)

                def divide(t):
                    e.wait_ge(a_exp, h * T + t + 1)
                    n = (t + 1) * P
                    nc.vector.reciprocal(ST[:, 80 + t % 2:81 + t % 2], ST[:, 78 + t % 2:79 + t % 2]).then_inc(a_rec, 1)
                    e.wait_ge(a_rec, h * T + t + 1)
                    p = tmp((t % 2) * 1024, n)
                    nc.vector.tensor_scalar(p, p, ST[:, 80 + t % 2:81 + t % 2], None, ALU.mult).then_inc(a_prob, 1)

                biggest(0)
                divide(0)
                for t in range(T):
                    if t + 1 < T:
                        biggest(t + 1)
                    if t >= 1:
                        out_lo(t - 1)
                    n = (t + 1) * P
                    e.wait_ge(a_pt_hi, h * T + t + 1)
                    src = PS[:, 4:6, :].rearrange("p b n -> p (b n)")[:, 0:n]
                    nc.vector.tensor_tensor(HTL[:, PTT, 0:n], src, HTH[:, PTT, 0:n].bitcast(F32),
                                            ALU.subtract).then_inc(a_pt_lo, 1)
                    if t + 1 < T:
                        divide(t + 1)
                out_lo(T - 1)

        def act_3c(e):
            pass

        rt_turned, rt_hi, rt_lo = sem("rt_turned"), sem("rt_hi"), sem("rt_lo")
        o_done, o_added = sem("o_done"), sem("o_added")
        NA = HEADS * T

        def sp_4(e):
            e.wait_ge(a_w_lo, 2 * HEADS)
            sp_out_weights(e, 1, M_WO1)
            e.wait_ge(a_rope, 6 * HEADS)
            e.dma_start(GB[:, :], t_in["ffn_norm_g"].partition_broadcast(P)).then_inc(s_gain, 16)
            e.wait_ge(rt_turned, T)
            for t in range(4):
                e.dma_start(X3[:, t, :], t_in["x"][t * P:(t + 1) * P, :]).then_inc(s_x[t], 16)

        def pe_4(e):
            e.wait_ge(r_done, NU)
            for t in range(T):
                if t < 4:
                    e.wait_ge(a_exp, NA)
                else:
                    e.wait_ge(rt_lo, t - 3)
                for k in range(4):
                    last = nc.tensor.transpose(PS[:, t % 4, k * P:k * P + P], RET[:, t, k * P:k * P + P], ident)
                last.then_inc(rt_turned, 1)
            e.wait_ge(a_o_lo, NA)
            e.wait_ge(a_pt_lo, NA)
            for half in range(2):
                if half == 1:
                    e.wait_ge(w_lo, M_WO1 + 4)
                for t in range(T):
                    n = half * T + t
                    e.wait_ge(rt_lo, t + 1)
                    if n >= 4:
                        e.wait_ge(o_added, n - 3)
                    product(bank(4 + n % 4), t, 1 - half).then_inc(o_done, 1)
                    if half == 1 and t >= 2:
                        norm_turn(e, n_ffn, t - 2)
            norm_turn(e, n_ffn, T - 2)
            norm_turn(e, n_ffn, T - 1)

        def act_4(e):
            for t in range(T):
                e.wait_ge(rt_turned, t + 1)
                nc.scalar.copy(HTH[:, 0:4, t * P:t * P + P],
                               bank(t % 4).rearrange("p (k n) -> p k n", k=4)).then_inc(rt_hi, 1)
            for c in range(4):
                e.wait_ge(s_rawb[c], 16 * (HEADS + 2))
                granule_hi(e, 0, c, M_WO1 + c)
            for t in range(T):
                squares_x(e, n_ffn, t, 48, o_added, T + t + 1)
                if t >= 2:
                    turned_hi(e, n_ffn, t - 2)
                if t in (2, 4):
                    for c in range(2):
                        ffn_hi(e, (M_FFN + c + t - 2), 8192 + (t - 2) // 2 * 4096 + c * 2048)
            turned_hi(e, n_ffn, T - 2)
            turned_hi(e, n_ffn, T - 1)

        def squares_x(e, s, t, col, ready, count):
            e.wait_ge(ready, count)
            if t:
                e.wait_ge(s.squares, t)
            norm_squares(e, s, t, col, X3[:, t, :], JUNK)

        def rows_x(e, s, t, col):
            if t >= 2:
                e.wait_ge(s.turned, t - 1)
            norm_rows(e, s, t, col, X3[:, t, :], tmp(2048 + (t % 2) * 1024, 1024))

        def add_x(e, src, t, lo, n, done):
            x = X3[:, t, lo:lo + n]
            nc.vector.tensor_tensor(x, x, src, ALU.add).then_inc(done, 1)

        def dve_4(e):
            for t in range(T):
                e.wait_ge(rt_hi, t + 1)
                d = slice(t * P, t * P + P)
                nc.vector.tensor_tensor(HTL[:, 0:4, d], bank(t % 4).rearrange("p (k n) -> p k n", k=4),
                                        HTH[:, 0:4, d].bitcast(F32), ALU.subtract).then_inc(rt_lo, 1)
            for c in range(4):
                granule_lo(e, 0, c, M_WO1 + c)
            for half in range(2):
                for t in range(T):
                    n = half * T + t
                    e.wait_ge(o_done, n + 1)
                    if half == 0:
                        e.wait_ge(s_x[t % 4], 16 * (3 if t >= 4 else 4))
                    add_x(e, bank(4 + n % 4), t, half * HALF, HALF, o_added)
                    if half == 1:
                        if t >= 1:
                            if t == 1:
                                e.wait_ge(s_gain, 32)
                            rows_x(e, n_ffn, t - 1, 48)
                        if t >= 3:
                            turned_lo(e, n_ffn, t - 3)
                        if t in (2, 4):
                            for c in range(2):
                                ffn_lo(e, (M_FFN + c + t - 2), 8192 + (t - 2) // 2 * 4096 + c * 2048)
            rows_x(e, n_ffn, T - 1, 48)
            for t in range(T - 3, T):
                turned_lo(e, n_ffn, t)

        def pool_4(e):
            for t in range(T):
                norm_rstd(e, n_ffn, t, 48)

        f_gu, f_silu, f_hid, f_hi, f_lo = sem("f_gu"), sem("f_silu"), sem("f_hid"), sem("f_hi"), sem("f_lo")
        f_down, f_added = sem("f_down"), sem("f_added")

        def ffn_hi(e, m, a, more=0):
            arrived(e, m, more * 4)
            nc.scalar.copy(WF[:, a:a + 1024], raw(m)).then_inc(w_hi, 1)

        def ffn_lo(e, m, a, more=0):
            e.wait_ge(w_hi, m + 1 + more)
            nc.vector.tensor_tensor(WF[:, a + 1024:a + 2048], raw(m), WF[:, a:a + 1024].bitcast(F32),
                                    ALU.subtract).then_inc(w_lo, 1)

        def m_block(g):
            return M_FFN + 8 + 6 * (g - 1)

        def sp_ffn_gu(e, m, g, jj, more=0, col=0):
            for n, name in enumerate(("w_ffn_gate", "w_ffn_up")):
                w = t_in[name].rearrange("(k p) n -> p k n", p=P)
                e.wait_ge(w_lo, m + n - 3 + more)
                e.dma_start(raw(m + n).rearrange("p (k n) -> p k n", k=K),
                            w[:, :, bass.ds(col + (g * GROUP + jj) * P, P)]).then_inc(s_raw[(m + n) % 4], 16)

        def sp_ffn_down(e, m, g, more=0, row=0):
            for jj in range(GROUP):
                e.wait_ge(w_lo, m + jj - 3 + more)
                w = t_in["w_ffn_down"]
                e.dma_start(raw(m + jj), w[bass.ds(row + (g * GROUP + jj) * P, P), :]).then_inc(s_raw[(m + jj) % 4], 16)

        def sp_5(e):
            for g in range(2):
                for jj in range(2):
                    sp_ffn_gu(e, M_FFN + 4 * g + 2 * jj, g, jj)

            def block(g, i=0, last=False):
                m = m_block(g)
                sp_ffn_down(e, m, g - 1, i * 12, i * (2 * GROUP * P))
                if not last:
                    for jj in range(2):
                        sp_ffn_gu(e, m + 2 + 2 * jj, g + 1, jj, i * 12, i * (2 * GROUP * P))
            with e.Fori(0, (NG - 3) // 2) as i:
                block(1, i)
                block(2, i)
            block(NG - 2)
            block(NG - 1, last=True)
            sp_ffn_down(e, m_block(NG - 1) + 2, NG - 1)

        def pe_gu(e, g, i=0):
            for jj in range(GROUP):
                for b in range(2):
                    u = 4 * g + 2 * jj + b
                    if b == 0:
                        m = M_FFN + 2 * jj + 2 if g == 0 else (M_FFN + 4 + 2 * jj + 2 if g == 1 else m_block(g - 1) + 4 + 2 * jj)
                        e.wait_ge(w_lo, m + i * 12)
                    if g == 0:
                        e.wait_ge(n_ffn.lo, 2 * T - 2 + 2 * b)
                    if u >= 2:
                        e.wait_ge(f_hid, u - 1 + i * 8)
                    blk = slice(b * HALF, (b + 1) * HALF)
                    for x in range(2):
                        a = 8192 + 4096 * jj + 2048 * x
                        dst = bank(2 * (u % 2) + x)
                        for k in range(K):
                            w_h, w_l = WF[:, a + k * P:a + k * P + P], WF[:, a + 1024 + k * P:a + 1024 + k * P + P]
                            nc.tensor.matmul(dst, w_h, HTH[:, k, blk], start=(k == 0), stop=False)
                            nc.tensor.matmul(dst, w_h, HTL[:, k, blk], start=False, stop=False)
                            last = nc.tensor.matmul(dst, w_l, HTH[:, k, blk], start=False, stop=(k == K - 1))
                    last.then_inc(f_gu, 1)

        def pe_down(e, g, i=0, more=None):
            e.wait_ge(f_lo, 4 * (g + 1) + i * 8)
            m = m_block(g + 1) + 2 if g < NG - 1 else m_block(NG - 1) + 4
            e.wait_ge(w_lo, m + i * 12)
            for t in range(T):
                for half in range(2):
                    n = 16 * g + 2 * t + half
                    if n >= 4:
                        e.wait_ge(f_added, n - 3 + i * 32)
                    dst = bank(4 + n % 4)
                    for jj in range(GROUP):
                        hid = (g % 2) * 4096 + 2048 * jj + t * P
                        w = 16384 + 2048 * jj + half * HALF
                        nc.tensor.matmul(dst, WF[:, hid:hid + P], WF[:, w:w + HALF], start=(jj == 0), stop=False)
                        nc.tensor.matmul(dst, WF[:, hid:hid + P], WF[:, w + 1024:w + 1024 + HALF], start=False, stop=False)
                        last = nc.tensor.matmul(dst, WF[:, hid + 1024:hid + 1024 + P], WF[:, w:w + HALF],
                                                start=False, stop=(jj == GROUP - 1))
                    last.then_inc(f_down, 1)
                if more:
                    more(t)

        def pe_5(e):
            e.wait_ge(o_added, 2 * T)
            pe_gu(e, 0)
            with e.Fori(0, (NG - 3) // 2) as i:
                for g in (1, 2):
                    pe_gu(e, g, i)
                    pe_down(e, g - 1, i)
            for g in (NG - 2, NG - 1):
                pe_gu(e, g)
                pe_down(e, g - 1)

            def turn(t):
                if t == 0:
                    pt_turn(e)
                if t >= 2:
                    norm_turn(e, n_ple, t - 2)
            pe_down(e, NG - 1, more=turn)
            norm_turn(e, n_ple, T - 2)
            norm_turn(e, n_ple, T - 1)

        def act_hidden(e, g, jj, b, i=0):
            u = 4 * g + 2 * jj + b
            e.wait_ge(f_gu, u + 1 + i * 8)
            if u >= 2:
                e.wait_ge(f_hid, u - 1 + i * 8)
            nc.scalar.activation(tmp((u % 2) * HALF, HALF), bank(2 * (u % 2)), ACT.Silu).then_inc(f_silu, 1)
            e.wait_ge(f_hid, u + 1 + i * 8)
            if g >= 2 and b == 0:
                e.wait_ge(f_down, 16 * (g - 1) + i * 32)
            a = (g % 2) * 4096 + 2048 * jj + b * HALF
            nc.scalar.copy(WF[:, a:a + HALF], tmp(1024 + (u % 2) * HALF, HALF)).then_inc(f_hi, 1)

        def dve_hidden(e, g, jj, b, i=0):
            u = 4 * g + 2 * jj + b
            e.wait_ge(f_silu, u + 1 + i * 8)
            if u >= 2:
                e.wait_ge(f_lo, u - 1 + i * 8)
            h = tmp(1024 + (u % 2) * HALF, HALF)
            nc.vector.tensor_tensor(h, tmp((u % 2) * HALF, HALF), bank(2 * (u % 2) + 1), ALU.mult).then_inc(f_hid, 1)
            e.wait_ge(f_hi, u + 1 + i * 8)
            a = (g % 2) * 4096 + 2048 * jj + b * HALF
            nc.vector.tensor_tensor(WF[:, a + 1024:a + 1024 + HALF], h, WF[:, a:a + HALF].bitcast(F32),
                                    ALU.subtract).then_inc(f_lo, 1)

        def ffn_block(e, g, i, hidden, piece, adds, last=False):
            m = m_block(g)
            hidden(e, g, 0, 0, i)
            if g >= 2:
                e.wait_ge(f_down, 16 * (g - 1) + i * 32)
            for jj in range(2):
                piece(e, m + jj, 16384 + 2048 * jj, i * 12)
            hidden(e, g, 0, 1, i)
            for b in range(2):
                hidden(e, g, 1, b, i)
                if not last:
                    e.wait_ge(f_gu, 4 * g + 2 + i * 8)
                    piece(e, m + 2 + b, 8192 + 2048 * b, i * 12)
            for n in range(16):
                if adds:
                    adds(e, g - 1, n, i)
                if not last and n in (2, 6):
                    e.wait_ge(f_gu, 4 * g + 4 + i * 8)
                    piece(e, m + 4 + n // 4, 12288 + 2048 * (n // 4), i * 12)

        def add_down(e, g, n, i=0):
            e.wait_ge(f_down, 16 * g + n + 1 + i * 32)
            if g >= 1:
                e.wait_ge(f_added, 16 * (g - 1) + n + 1 + i * 32)
            add_x(e, bank(4 + (16 * g + n) % 4), n // 2, (n % 2) * HALF, HALF, f_added)

        def ffn_5(e, hidden, piece, adds, first):
            for jj in range(2):
                for b in range(2):
                    hidden(e, 0, jj, b)
                e.wait_ge(f_gu, 2 * jj + 2)
                for n in range(2):
                    piece(e, M_FFN + 4 + 2 * jj + n, 8192 + 4096 * jj + 2048 * n, 0)
            with e.Fori(0, (NG - 3) // 2) as i:
                ffn_block(e, 1, i, hidden, piece, adds)
                ffn_block(e, 2, i, hidden, piece, adds)
            ffn_block(e, NG - 2, 0, hidden, piece, adds)
            ffn_block(e, NG - 1, 0, hidden, piece, adds, last=True)
            e.wait_ge(f_down, 16 * (NG - 1))
            for jj in range(2):
                piece(e, m_block(NG - 1) + 2 + jj, 16384 + 2048 * jj, 0)

        def act_5(e):
            ffn_5(e, act_hidden, ffn_hi, None, 0)

        def dve_5(e):
            ffn_5(e, dve_hidden, ffn_lo, add_down, 0)

        s_p, p_turned, p_hi, p_lo = sem("s_p"), sem("p_turned"), sem("p_hi"), sem("p_lo")
        g_done, g_sig, g_mul, g_added, s_out = sem("g_done"), sem("g_sig"), sem("g_mul"), sem("g_added"), [sem("s_out0"), sem("s_out1")]
        M6 = M_PLE
        QC = 256
        PTP = [WF[:, 4096:6144].rearrange("p (k n) -> p k n", k=2), WF[:, 6144:8192].rearrange("p (k n) -> p k n", k=2)]
        PW = 8192
        GQ = [12288, 0]
        PIN = tmp(0, 2048).rearrange("p (t n) -> p t n", t=T)

        def sp_6(e):
            e.wait_ge(f_lo, 4 * NG)
            e.dma_start(PIN, t_in["p"].rearrange("(t p) n -> p t n", p=P)).then_inc(s_p, 16)
            e.wait_ge(n_ffn.normed, T)
            e.dma_start(GB[:, :], t_in["ple_norm_g"].partition_broadcast(P)).then_inc(s_gain, 16)
            for k in range(2):
                e.wait_ge(w_lo, M6 + k - 3)
                e.dma_start(raw(M6 + k), t_in["w_ple_proj"][k * P:(k + 1) * P, :]).then_inc(s_raw[(M6 + k) % 4], 16)
            w = t_in["w_ple_gate"].rearrange("(k p) n -> p k n", p=P)
            for q in range(4):
                for c in range(2):
                    m = M6 + 2 + 2 * q + c
                    e.wait_ge(w_lo, m - 3)
                    e.dma_start(raw(m).rearrange("p (k n) -> p k n", k=4),
                                w[:, 4 * c:4 * c + 4, q * QC:(q + 1) * QC]).then_inc(s_raw[m % 4], 16)
                if q == 1:
                    e.wait_ge(n_ple.normed, T)
                    e.dma_start(GB[:, :], t_in["final_norm_g"].partition_broadcast(P)).then_inc(s_gain, 16)
            for t in range(T):
                e.wait_ge(n_out.normed, t + 1)
                e.dma_start(out[t * P:(t + 1) * P, :], tmp(2048 + (t % 2) * 1024, 1024)).then_inc(s_out[t % 2], 16)
            for c in range(2):
                e.wait_ge(s_out[c], 16 * T // 2)

        def pt_turn(e):
            e.wait_ge(s_p, 16)
            e.wait_ge(f_hid, 4 * NG)
            for t in range(T):
                for k in range(2):
                    last = nc.tensor.transpose(PS[:, t // 2, (t % 2) * QC + k * P:(t % 2) * QC + k * P + P],
                                               PIN[:, t, k * P:k * P + P], ident)
            last.then_inc(p_turned, 1)

        def p_halves(e, s, f):
            for t in range(T):
                src = PS[:, t // 2, (t % 2) * QC:(t % 2) * QC + QC].rearrange("p (k n) -> p k n", k=2)
                f(t, src, PTP[0][:, :, t * P:t * P + P], PTP[1][:, :, t * P:t * P + P]).then_inc(s, 1)

        def act_6(e):
            e.wait_ge(p_turned, 1)
            e.wait_ge(f_down, 16 * (NG - 1))
            p_halves(e, p_hi, lambda t, src, hi, lo: nc.scalar.copy(hi, src))
            for k in range(2):
                ffn_hi(e, M6 + k, PW + 2048 * k)
            gate_hi(e, 0)
            for t in range(T):
                squares_x(e, n_ple, t, 48, f_added, 16 * (NG - 1) + 2 * t + 2)
                if t == 3:
                    pass
                if t >= 2:
                    turned_hi(e, n_ple, t - 2)
            turned_hi(e, n_ple, T - 2)
            turned_hi(e, n_ple, T - 1)
            gate_hi(e, 1)
            for q in range(4):
                for t in range(T):
                    u = q * T + t
                    e.wait_ge(g_done, u + 1)
                    if u >= 4:
                        e.wait_ge(g_mul, u - 3)
                    nc.scalar.activation(tmp((u % 4) * QC, QC), PS[:, u % 8, 0:QC], ACT.Sigmoid).then_inc(g_sig, 1)
                    if t == 0 and 1 <= q < 3:
                        gate_hi(e, q + 1)
                    if q == 3 and t >= 1:
                        squares_x(e, n_out, t - 1, 96, g_added, 3 * T + t)
            squares_x(e, n_out, T - 1, 96, g_added, 4 * T)

        def gate_hi(e, q):
            if q == 1:
                e.wait_ge(f_down, 16 * NG)
            if q >= 2:
                e.wait_ge(g_done, (q - 1) * T)
            for c in range(2):
                m, a = M6 + 2 + 2 * q + c, GQ[q % 2] + 1024 * c
                arrived(e, m)
                nc.scalar.copy(WF[:, a:a + 1024], raw(m)).then_inc(w_hi, 1)

        def gate_lo(e, q):
            for c in range(2):
                m, a = M6 + 2 + 2 * q + c, GQ[q % 2] + 1024 * c
                e.wait_ge(w_hi, m + 1)
                nc.vector.tensor_tensor(WF[:, a + 2048:a + 3072], raw(m), WF[:, a:a + 1024].bitcast(F32),
                                        ALU.subtract).then_inc(w_lo, 1)

        def dve_6(e):
            e.wait_ge(p_hi, T)
            p_halves(e, p_lo, lambda t, src, hi, lo: nc.vector.tensor_tensor(lo, src, hi.bitcast(F32), ALU.subtract))
            for k in range(2):
                ffn_lo(e, M6 + k, PW + 2048 * k)
            gate_lo(e, 0)
            e.wait_ge(s_gain, 48)
            for t in range(T):
                add_down(e, NG - 1, 2 * t)
                add_down(e, NG - 1, 2 * t + 1)
                if t >= 1:
                    rows_x(e, n_ple, t - 1, 48)
                if t >= 3:
                    turned_lo(e, n_ple, t - 3)
            rows_x(e, n_ple, T - 1, 48)
            for t in range(T - 3, T):
                turned_lo(e, n_ple, t)
            gate_lo(e, 1)
            for q in range(4):
                for t in range(T):
                    u = q * T + t
                    e.wait_ge(g_sig, u + 1)
                    if u >= 4:
                        e.wait_ge(g_added, u - 3)
                    m = tmp(1024 + (u % 4) * QC, QC)
                    nc.vector.tensor_tensor(m, tmp((u % 4) * QC, QC), PS[:, u % 8, QC:2 * QC], ALU.mult).then_inc(g_mul, 1)
                    if t == 0 and 1 <= q < 3:
                        gate_lo(e, q + 1)
                    if q == 3 and t >= 2:
                        out_rows(e, t - 2)
            out_rows(e, T - 2)
            out_rows(e, T - 1)

        def out_rows(e, t):
            if t == 0:
                e.wait_ge(s_gain, 64)
            if t >= 2:
                e.wait_ge(s_out[t % 2], 16 * (t // 2))
            norm_rows(e, n_out, t, 96, X3[:, t, :], tmp(2048 + (t % 2) * 1024, 1024))

        def pool_6(e):
            for t in range(T):
                norm_rstd(e, n_ple, t, 48)
            for q in range(4):
                for t in range(T):
                    u = q * T + t
                    e.wait_ge(g_mul, u + 1)
                    x = X3[:, t, q * QC:(q + 1) * QC]
                    nc.gpsimd.tensor_tensor(x, x, tmp(1024 + (u % 4) * QC, QC), ALU.add).then_inc(g_added, 1)
                    if q == 3 and t >= 1:
                        norm_rstd(e, n_out, t - 1, 96)
            norm_rstd(e, n_out, T - 1, 96)

        def pe_6(e):
            e.wait_ge(n_ple.lo, 2 * T)
            e.wait_ge(f_added, 16 * NG)
            e.wait_ge(p_lo, T)
            with e.Fori(0, 2) as j:
                for q in range(2):
                    e.wait_ge(w_lo, M6 + 4 + 2 * q + j * 4)
                    for t in range(T):
                        u = q * T + t
                        e.wait_ge(g_mul, j * 16 + max(0, u - 7))
                        tok = slice(t * P, t * P + P)
                        gate, emb = PS[:, u % 8, 0:QC], PS[:, u % 8, QC:2 * QC]
                        for k in range(K):
                            a = GQ[q] + k * QC
                            nc.tensor.matmul(gate, HTH[:, k, tok], WF[:, a:a + QC], start=(k == 0), stop=False)
                            nc.tensor.matmul(gate, HTH[:, k, tok], WF[:, a + 2048:a + 2048 + QC], start=False, stop=False)
                            nc.tensor.matmul(gate, HTL[:, k, tok], WF[:, a:a + QC], start=False, stop=(k == K - 1))
                        for k in range(2):
                            for n, (x, y) in enumerate(((0, 0), (0, 1), (1, 0))):
                                a = j * 512 + (PW + 2048 * k + 1024 * y + q * QC)
                                last = nc.tensor.matmul(emb, PTP[x][:, k, tok], WF[:, bass.ds(a, QC)],
                                                        start=(k + n == 0), stop=(k * n == 2))
                        last.then_inc(g_done, 1)

        block = ctx.enter_context(nc.Block())

        @block.sync
        def _(sp):
            sp_1(sp)
            sp_retention(sp)
            sp_out_weights(sp, 0, M_WO0)
            sp_3(sp)
            sp_4(sp)
            sp_5(sp)
            sp_6(sp)

        @block.gpsimd
        def _(pool):
            pool_1(pool)
            pool_2(pool)
            pool_4(pool)
            pool_6(pool)

        @block.scalar
        def _(act):
            act_1(act)
            act_2(act)
            act_3a(act)
            act_3b(act)
            act_4(act)
            act_5(act)
            act_6(act)

        @block.vector
        def _(dve):
            dve_1(dve)
            dve_2(dve)
            dve_3a(dve)
            dve_3b(dve)
            dve_4(dve)
            dve_5(dve)
            dve_6(dve)

        @block.tensor
        def _(pe):
            pe_1(pe)
            pe_2(pe)
            pe_3a(pe)
            pe_3b(pe)
            pe_4(pe)
            pe_5(pe)
            pe_6(pe)


def kernel(x, p, positions, mix_norm_g, w_in, q_norm_g, w_uq, kv_norm_g, w_ukv, w_o,
           ffn_norm_g, w_ffn_gate, w_ffn_up, w_ffn_down, ple_norm_g, w_ple_gate,
           w_ple_proj, final_norm_g):
    import concourse.bacc as bacc
    from concourse.bass_utils import run_bass_kernel_spmd

    table, query_decay = shape_tables()
    arrays = {
        "x": np.asarray(x)[0],
        "p": np.asarray(p)[0, 0],
        "positions": np.asarray(positions).reshape(T, P).T,
        "w_in": np.asarray(w_in)[0], "w_uq": np.asarray(w_uq)[0], "w_ukv": np.asarray(w_ukv)[0],
        "w_o": np.asarray(w_o)[0], "w_ffn_gate": np.asarray(w_ffn_gate)[0],
        "w_ffn_up": np.asarray(w_ffn_up)[0], "w_ffn_down": np.asarray(w_ffn_down)[0],
        "w_ple_gate": np.asarray(w_ple_gate)[0], "w_ple_proj": np.asarray(w_ple_proj)[0],
        "mix_norm_g": np.asarray(mix_norm_g)[0], "q_norm_g": np.asarray(q_norm_g)[0],
        "kv_norm_g": np.asarray(kv_norm_g)[0], "ffn_norm_g": np.asarray(ffn_norm_g)[0],
        "ple_norm_g": np.asarray(ple_norm_g)[0], "final_norm_g": np.asarray(final_norm_g),
        "table": table, "query_decay": query_decay,
    }
    nc = bacc.Bacc("TRN2", target_bir_lowering=False, num_devices=1, dynamic_dma_scratch_size=1024)
    maps, t_in = {}, {}
    for name, a in arrays.items():
        a = np.ascontiguousarray(a)
        maps["in_" + name] = a
        t_in[name] = nc.dram_tensor("in_" + name, a.shape, mybir.dt.from_np(a.dtype), kind="ExternalInput").ap()
    out = nc.dram_tensor("out_rows", (S, D), F32, kind="ExternalOutput").ap()
    build(nc, t_in, out)
    r = run_bass_kernel_spmd(nc, [maps], core_ids=[0])
    return r.results[0]["out_rows"].reshape(1, S, D)
```

```python
from contextlib import ExitStack

import numpy as np

import concourse.bass as bass
from concourse import mybir

F32 = mybir.dt.float32
F32R = mybir.dt.float32r
I32 = mybir.dt.int32
ALU = mybir.AluOpType
ACT = mybir.ActivationFunctionType
AXX = mybir.AxisListType.X

P = 128
S = 1024
D = 1024
T = S // P
K = D // P
CHUNK = 64
HEADS = 4
HD = 128
ROPE = 64
QL, KVL = 256, 128
MLA_IN = QL + KVL + ROPE
QK = HD + ROPE
FF = 2816
GROUP = 2
NG = FF // P // GROUP
PLE = 256
HALF = 512
EPS, GN_EPS = 1e-6, 1e-5
SCALE = float(QK) ** -0.5
MASKED = -3.0e38
TWO_PI = 2.0 * np.pi
PI_A = 6.28125
PI_B = float(np.float32(np.floor((TWO_PI - PI_A) * 2.0 ** 18) / 2.0 ** 18))
PI_C = float(TWO_PI - PI_A - PI_B)
ROUND = 1.5 * 2.0 ** 23

C_IDENT, C_INV, C_DEC = 0, P, P + 64
C_KDEC = C_DEC + HEADS * P
C_CDEC = C_KDEC + HEADS
C_END = C_CDEC + HEADS


def shape_tables():
    table = np.zeros((P, C_END), np.float32)
    table[:, C_IDENT:C_IDENT + P] = np.eye(P)
    half = HD // 2
    scaled = np.float32(-np.log(10000.0)) * np.arange(half, dtype=np.float32) / np.float32(half)
    table[:, C_INV:C_INV + half] = np.exp(scaled)
    log_g = np.log1p(-np.exp2(-5.0 - np.arange(HEADS)))
    i = np.arange(P)
    query_decay = np.zeros((P, HEADS * P), np.float32)
    for h in range(HEADS):
        seen = (i[:, None] // CHUNK) <= (i[None, :] // CHUNK)
        decay = np.exp(log_g[h] * np.abs(i[:, None] - i[None, :])) * seen * HD ** -0.5
        table[:, C_DEC + h * P:C_DEC + (h + 1) * P] = decay
        table[:, C_KDEC + h] = np.exp(log_g[h] * (P - 1.0 - i)) * HD ** -0.5
        table[:, C_CDEC + h] = np.exp(log_g[h] * P)
        query_decay[:, h * P:(h + 1) * P] = np.exp(log_g[h] * (i + 1.0))[None, :]
    return table, query_decay


def build(nc, t_in, out):
    ctx = ExitStack()
    with ctx:
        def sb(name, shape, dt=F32):
            return ctx.enter_context(nc.sbuf_tensor(name, shape, dt))

        def sem(name):
            return ctx.enter_context(nc.semaphore(name))

        X = sb("X", [P, T * D])
        HTH = sb("HTH", [P, K, S], F32R)
        HTL = sb("HTL", [P, K, S], F32R)
        WF = sb("WF", [P, 20480], F32R)
        RAW = sb("RAW", [P, 4096])
        TMP = sb("TMP", [P, 4096])
        TAB = sb("TAB", [P, 2, T, 64])
        CST = sb("CST", [P, C_END])
        GB = sb("GB", [P, D])
        GC = sb("GC", [P, QL + KVL])
        POS = sb("POS", [P, T], I32)
        POSF = sb("POSF", [P, T])
        NEGH = sb("NEGH", [P, 16])
        PIH = sb("PIH", [P, 1])
        GNE = sb("GNE", [P, 1])
        ST = sb("ST", [P, 128])
        PS = ctx.enter_context(nc.psum_tensor("PS", [P, 8, HALF], F32))

        ident = CST[:, C_IDENT:C_IDENT + P]
        X3 = X[:, :].rearrange("p (t n) -> p t n", t=T)
        COS, SIN = TAB[:, 0], TAB[:, 1]
        JUNK = TAB[:, :, :, :].rearrange("p a t n -> p (a t n)")
        RET = X[:, 0:T * HALF].rearrange("p (t n) -> p t n", t=T)
        CKV = X[:, T * HALF:2 * T * HALF].rearrange("p (t n) -> p t n", t=T)
        VALL = CKV
        QDEC = GB[:, HALF:2 * HALF]

        def tmp(a, n):
            return TMP[:, a:a + n]

        def bank(b, n=HALF):
            return PS[:, b, 0:n]

        class Norm:
            def __init__(self, name):
                self.squares = sem(name + "_squares")
                self.mean = sem(name + "_mean")
                self.rstd = sem(name + "_rstd")
                self.normed = sem(name + "_normed")
                self.turned = sem(name + "_turned")
                self.hi = sem(name + "_hi")
                self.lo = sem(name + "_lo")

        n_mix, n_ffn, n_ple, n_out = Norm("mix"), Norm("ffn"), Norm("ple"), Norm("final")
        s_decay = sem("s_decay")
        s_att = sem("s_att")
        s_const, s_gain = sem("s_const"), sem("s_gain")
        s_x = [sem(f"s_x{i}") for i in range(4)]
        s_raw = [sem(f"s_raw{i}") for i in range(4)]
        s_rawb = [sem(f"s_rawb{i}") for i in range(4)]
        w_hi, w_lo = sem("w_hi"), sem("w_lo")
        s_setup, s_tab, s_sin = sem("s_setup"), sem("s_tab"), sem("s_sin")
        lat_done, ckv_out = sem("lat_done"), sem("ckv_out")
        lat_mean, lat_rstd, lat_rows, lat_rope = sem("lat_mean"), sem("lat_rstd"), sem("lat_rows"), sem("lat_rope")

        def big(slot, part, k, n=HALF):
            a = slot * 8192 + part * 4096 + k * HALF
            return WF[:, a:a + n]

        def raw(m):
            return RAW[:, (m % 4) * 1024:(m % 4) * 1024 + 1024]

        M_LAT, M_RET, M_WO0, M_WO1, M_FFN = 0, 4, 20, 24, 28
        M_PLE = M_FFN + NG * 6

        def arrived(eng, m, more=0):
            eng.wait_ge(s_raw[m % 4], 16 * (m // 4 + 1) + more)

        def split_hi(e, m, dst, src, more=0):
            arrived(e, m, more * 4)
            nc.scalar.copy(dst, src).then_inc(w_hi, 1)

        def split_lo(e, m, dst, hi, src, more=0):
            e.wait_ge(w_hi, m + 1 + more)
            nc.vector.tensor_tensor(dst, src, hi.bitcast(F32), ALU.subtract).then_inc(w_lo, 1)

        def granule_hi(e, g, c, m, n=HALF, more=0):
            a = g * 8192 + c * 1024
            src, dst = raw(m), WF[:, a:a + 1024]
            if n < HALF:
                src = src[:, 0:2 * n].rearrange("p (k n) -> p k n", k=2)
                dst = dst.rearrange("p (k n) -> p k n", k=2)[:, :, 0:n]
            split_hi(e, m, dst, src, more)

        def granule_lo(e, g, c, m, n=HALF, more=0):
            a = g * 8192 + c * 1024
            src, hi, dst = raw(m), WF[:, a:a + 1024], WF[:, a + 4096:a + 5120]
            if n < HALF:
                src = src[:, 0:2 * n].rearrange("p (k n) -> p k n", k=2)
                hi = hi.rearrange("p (k n) -> p k n", k=2)[:, :, 0:n]
                dst = dst.rearrange("p (k n) -> p k n", k=2)[:, :, 0:n]
            split_lo(e, m, dst, hi, src, more)

        def product(dst, tile, slot, n=HALF):
            tok = slice(tile * P, tile * P + P)
            for k in range(K):
                w_h, w_l = big(slot, 0, k, n), big(slot, 1, k, n)
                nc.tensor.matmul(dst, HTH[:, k, tok], w_h, start=(k == 0), stop=False)
                nc.tensor.matmul(dst, HTH[:, k, tok], w_l, start=False, stop=False)
                last = nc.tensor.matmul(dst, HTL[:, k, tok], w_h, start=False, stop=(k == K - 1))
            return last

        def norm_squares(e, s, t, col, src, junk):
            nc.scalar.activation(junk, src, ACT.Square, accum_out=ST[:, col + t:col + t + 1]).then_inc(s.squares, 1)

        def norm_rstd(e, s, t, col):
            e.wait_ge(s.squares, t + 1)
            c = ST[:, col + t:col + t + 1]
            r = ST[:, col + 8 + t:col + 9 + t]
            nc.gpsimd.tensor_scalar(c, c, 1.0 / D, EPS, ALU.mult, ALU.add).then_inc(s.mean, 1)
            e.wait_ge(s.mean, t + 1)
            nc.gpsimd.tensor_tensor(r, c, NEGH[:, 0:1], ALU.pow).then_inc(s.rstd, 1)

        def norm_rows(e, s, t, col, src, dst):
            e.wait_ge(s.rstd, t + 1)
            r = ST[:, col + 8 + t:col + 9 + t]
            nc.vector.scalar_tensor_tensor(dst, src, r, GB[:, :], ALU.mult, ALU.mult).then_inc(s.normed, 1)

        def norm_turn(e, s, t):
            e.wait_ge(s.normed, t + 1)
            if t >= 2:
                e.wait_ge(s.lo, 2 * t - 2)
            b = 2 * (t % 2)
            for k in range(K):
                last = nc.tensor.transpose(PS[:, b + k // 4, (k % 4) * P:(k % 4) * P + P],
                                           tmp(2048 + (t % 2) * 1024 + k * P, P), ident)
            last.then_inc(s.turned, 1)

        def turned_hi(e, s, t):
            e.wait_ge(s.turned, t + 1)
            for j in range(2):
                src = bank(2 * (t % 2) + j).rearrange("p (k n) -> p k n", k=4)
                nc.scalar.copy(HTH[:, 4 * j:4 * j + 4, t * P:t * P + P], src).then_inc(s.hi, 1)

        def turned_lo(e, s, t):
            for j in range(2):
                e.wait_ge(s.hi, 2 * t + j + 1)
                src = bank(2 * (t % 2) + j).rearrange("p (k n) -> p k n", k=4)
                d = slice(t * P, t * P + P)
                nc.vector.tensor_tensor(HTL[:, 4 * j:4 * j + 4, d], src,
                                        HTH[:, 4 * j:4 * j + 4, d].bitcast(F32), ALU.subtract).then_inc(s.lo, 1)

        def sp_1(e):
            e.dma_start(X3[:, 0, :], t_in["x"][0:P, :]).then_inc(s_x[0], 16)
            e.dma_start(CST[:, :], t_in["table"]).then_inc(s_const, 16)
            e.dma_start(GB[:, :], t_in["mix_norm_g"].partition_broadcast(P)).then_inc(s_gain, 16)
            w = t_in["w_in"].rearrange("(k p) n -> p k n", p=P)
            for m in range(4):
                e.dma_start(raw(m)[:, 0:2 * MLA_IN].rearrange("p (k n) -> p k n", k=2),
                            w[:, 2 * m:2 * m + 2, 4 * HALF:4 * HALF + MLA_IN]).then_inc(s_raw[m % 4], 16)
                if m < 3:
                    e.dma_start(X3[:, m + 1, :], t_in["x"][(m + 1) * P:(m + 2) * P, :]).then_inc(s_x[m + 1], 16)
            e.dma_start(POS[:, :], t_in["positions"]).then_inc(s_const, 16)
            e.dma_start(GC[:, 0:QL], t_in["q_norm_g"].partition_broadcast(P)).then_inc(s_const, 16)
            e.dma_start(GC[:, QL:QL + KVL], t_in["kv_norm_g"].partition_broadcast(P)).then_inc(s_const, 16)
            for t in range(4, T):
                e.wait_ge(n_mix.normed, t - 3)
                e.dma_start(X3[:, t % 4, :], t_in["x"][t * P:(t + 1) * P, :]).then_inc(s_x[t % 4], 16)

        def pool_setup(e):
            nc.gpsimd.memset(NEGH[:, :], -0.5).then_inc(s_setup, 1)
            nc.gpsimd.memset(PIH[:, :], float(np.pi / 2)).then_inc(s_setup, 1)
            nc.gpsimd.memset(GNE[:, :], GN_EPS).then_inc(s_setup, 1)
            e.wait_ge(s_setup, 3)

        def pool_1(e):
            pool_setup(e)

            def latent_rstd(t):
                e.wait_ge(ckv_out, 3 * t + 2)
                q, kv = ST[:, 16 + 2 * t:17 + 2 * t], ST[:, 17 + 2 * t:18 + 2 * t]
                nc.gpsimd.tensor_scalar(q, q, 1.0 / QL, EPS, ALU.mult, ALU.add).then_inc(lat_mean, 1)
                nc.gpsimd.tensor_scalar(kv, kv, 1.0 / KVL, EPS, ALU.mult, ALU.add).then_inc(lat_mean, 1)
                e.wait_ge(lat_mean, 2 * t + 2)
                nc.gpsimd.tensor_tensor(ST[:, 32 + 2 * t:34 + 2 * t], ST[:, 16 + 2 * t:18 + 2 * t], NEGH[:, 0:2],
                                        ALU.pow).then_inc(lat_rstd, 1)
            norm_rstd(e, n_mix, 0, 0)
            norm_rstd(e, n_mix, 1, 0)
            for t in range(T):
                if t + 2 < T:
                    norm_rstd(e, n_mix, t + 2, 0)
                if t >= 1:
                    latent_rstd(t - 1)
            latent_rstd(T - 1)

        def act_1(e):
            def squares(t):
                e.wait_ge(s_x[t % 4], 16 * (t // 4 + 1))
                if t:
                    e.wait_ge(n_mix.squares, t)
                norm_squares(e, n_mix, t, 0, X3[:, t % 4, :], tmp(0, 1024))
            squares(0)
            for c in range(4):
                granule_hi(e, 0, c, c, MLA_IN)
            squares(1)
            for t in range(T):
                turned_hi(e, n_mix, t)
                if t + 2 < T:
                    squares(t + 2)
                if t >= 1:
                    latent_out(e, t - 1)
                if t >= 4:
                    e.wait_ge(s_rawb[t - 4], 16)
                    granule_hi(e, 1, t - 4, M_RET + t - 4)
                if t == 3:
                    tables_act(e)
            e.wait_ge(n_mix.normed, T)
            e.dma_start(QDEC, t_in["query_decay"]).then_inc(s_decay, 16)
            latent_out(e, T - 1)

        def latent_out(e, t):
            e.wait_ge(lat_done, t + 1)
            b = PS[:, 4 + t % 2]
            if t:
                e.wait_ge(ckv_out, 3 * t)
            nc.scalar.activation(GC2, b[:, 0:QL], ACT.Square, accum_out=ST[:, 16 + 2 * t:17 + 2 * t]).then_inc(ckv_out, 1)
            nc.scalar.activation(GC3, b[:, QL:QL + KVL], ACT.Square, accum_out=ST[:, 17 + 2 * t:18 + 2 * t]).then_inc(ckv_out, 1)
            nc.scalar.copy(CKV[:, t, 0:MLA_IN], b[:, 0:MLA_IN]).then_inc(ckv_out, 1)

        GC2, GC3 = tmp(1024, QL), tmp(1280, KVL)

        def tables_dve(e):
            n = [0]
            ang = COS
            turns = tmp(1536, 512).rearrange("p (t n) -> p t n", t=T)

            def link(i):
                n[0] += 1
                i.then_inc(s_tab, 1)
                e.wait_ge(s_tab, n[0])

            e.wait_ge(s_const, 16 * 4)
            e.wait_ge(s_setup, 2)
            link(nc.vector.tensor_copy(POSF[:, :], POS[:, :]))
            link(nc.vector.tensor_tensor(ang, POSF[:, :].unsqueeze(2).to_broadcast([P, T, 64]),
                                         CST[:, C_INV:C_INV + 64].unsqueeze(1).to_broadcast([P, T, 64]), ALU.mult))
            link(nc.vector.tensor_scalar(turns, ang, 1.0 / TWO_PI, ROUND, ALU.mult, ALU.add))
            link(nc.vector.tensor_scalar(turns, turns, ROUND, None, ALU.subtract))
            for part in (PI_A, PI_B, PI_C):
                link(nc.vector.scalar_tensor_tensor(ang, turns, -part, ang, ALU.mult, ALU.add))
            link(nc.vector.tensor_scalar(ang, ang, 3.1415925, -3.1415925, ALU.min, ALU.max))
            link(nc.vector.scalar_tensor_tensor(turns, ang, -1.0, ang, ALU.mult, ALU.max))

        N_TAB = 9

        def tables_act(e):
            e.wait_ge(s_tab, N_TAB)
            turns = tmp(1536, 512).rearrange("p (t n) -> p t n", t=T)
            nc.scalar.activation(SIN, COS, ACT.Sin).then_inc(s_sin, 1)
            e.wait_ge(s_sin, 1)
            nc.scalar.activation(COS, turns, ACT.Sin, bias=PIH[:, 0:1], scale=-1.0).then_inc(s_sin, 1)

        def dve_1(e):
            def rows(t):
                if t == 0:
                    e.wait_ge(s_gain, 16)
                if t >= 2:
                    e.wait_ge(n_mix.turned, t - 1)
                norm_rows(e, n_mix, t, 0, X3[:, t % 4, :], tmp(2048 + (t % 2) * 1024, 1024))
            rows(0)
            for c in range(4):
                granule_lo(e, 0, c, c, MLA_IN)
            rows(1)
            for t in range(T):
                turned_lo(e, n_mix, t)
                if t + 2 < T:
                    rows(t + 2)
                if t >= 4:
                    granule_lo(e, 1, t - 4, M_RET + t - 4)
                if t == 2:
                    tables_dve(e)
                if t >= 3:
                    latent_rows(e, t - 3)
            for t in range(T - 3, T):
                latent_rows(e, t)
            e.wait_ge(s_sin, 2)
            e.wait_ge(n_mix.turned, T)
            z = CKV[:, :, QL + KVL:MLA_IN].rearrange("p t (h n) -> p t h n", h=2)
            a4, b4 = (tmp(c, 512).rearrange("p (t h n) -> p t h n", t=T, h=2) for c in (3072, 3584))
            for x, table in ((a4, COS), (b4, SIN)):
                w = table[:, :, 0:64:2].unsqueeze(2).to_broadcast([P, T, 2, 32])
                nc.vector.tensor_tensor(x, z, w, ALU.mult).then_inc(lat_rope, 1)
            e.wait_ge(lat_rope, 2)
            nc.vector.tensor_tensor(z[:, :, 0], a4[:, :, 0], b4[:, :, 1], ALU.subtract).then_inc(lat_rope, 1)
            nc.vector.tensor_tensor(z[:, :, 1], a4[:, :, 1], b4[:, :, 0], ALU.add).then_inc(lat_rope, 1)
            e.wait_ge(lat_rope, 4)
            nc.vector.tensor_copy(CKV[:, :, MLA_IN:HALF], CKV[:, :, QL + KVL:MLA_IN]).then_inc(lat_rope, 1)

        def latent_rows(e, t):
            e.wait_ge(lat_rstd, t + 1)
            e.wait_ge(ckv_out, 3 * t + 3)
            for n, (a, b) in enumerate(((0, QL), (QL, QL + KVL))):
                c = CKV[:, t, a:b]
                nc.vector.scalar_tensor_tensor(c, c, ST[:, 32 + 2 * t + n:33 + 2 * t + n], GC[:, a:b],
                                               ALU.mult, ALU.mult).then_inc(lat_rows, 1)

        def pe_1(e):
            e.wait_ge(s_const, 16)
            norm_turn(e, n_mix, 0)
            for t in range(T):
                if t + 1 < T:
                    norm_turn(e, n_mix, t + 1)
                if t == 0:
                    e.wait_ge(w_lo, 4)
                e.wait_ge(n_mix.lo, 2 * t + 2)
                if t >= 2:
                    e.wait_ge(ckv_out, 3 * (t - 1))
                product(bank(4 + t % 2, MLA_IN), t, 0, MLA_IN).then_inc(lat_done, 1)

        z_proj, z_out = sem("z_proj"), sem("z_out")
        rot_ab, rot = sem("rot_ab"), sem("rot")
        qk_turned, qk_out, qd_out = sem("qk_turned"), sem("qk_out"), sem("qd_out")
        r_scores, r_probs, r_okv = sem("r_scores"), sem("r_probs"), sem("r_okv")
        r_state = sem("r_state")
        gn_stats, gn_mean, gn_rstd, gn_rows, r_done = (sem("gn_stats"), sem("gn_mean"), sem("gn_rstd"),
                                                       sem("gn_rows"), sem("r_done"))
        UNITS = 16

        def Z(u):
            return tmp((u % 4) * 512, 512)

        AB = tmp(2048, 512)
        PT2 = [tmp(2560, 128), tmp(2688, 128)]
        ON = [tmp(2816, 128), tmp(2944, 128)]
        QKT = [tmp(3072, 256), tmp(3328, 256)]
        QDT = [tmp(3584, 128), tmp(3712, 128)]
        STATE = tmp(3840, 128)
        KD = [GB[:, c * P:c * P + P] for c in range(4)]
        B_T, B_S, B_O, B_KV = 0, 1, 2, 3

        def sp_retention(e):
            w = t_in["w_in"][:, 0:4 * HALF].rearrange("(k p) (s c) -> p k s c", p=P, s=4)
            with e.Fori(0, HEADS) as h:
                for c in range(4):
                    e.wait_ge(w_lo, M_RET + c - 3 + 4 * h)
                    for k in range(2):
                        e.dma_start(RAW[:, c * 1024 + k * HALF:c * 1024 + (k + 1) * HALF].rearrange("p (s c) -> p s c", s=4),
                                    w[:, 2 * c + k, :, bass.ds(h * HD, HD)]).then_inc((s_rawb if k else s_raw)[c], 16)

        def sp_out_weights(e, half, m0):
            w = t_in["w_o"].rearrange("(k p) n -> p k n", p=P)
            for c in range(4):
                e.wait_ge(w_lo, m0 + c - 3)
                for k in range(2):
                    e.dma_start(raw(m0 + c)[:, k * HALF:(k + 1) * HALF],
                                w[:, 2 * c + k, half * HALF:(half + 1) * HALF]).then_inc((s_rawb if k else s_raw)[c], 16)

        def pe_2(e):
            e.wait_ge(ckv_out, 3 * T)
            with e.Fori(0, HEADS * T // UNITS) as i:
                B = i * UNITS
                for s in range(UNITS + 3):
                    if s < UNITS:
                        if s % T == 0:
                            e.wait_ge(w_lo, M_RET + 4 * (s // T + 1) + i * 8)
                        e.wait_ge(z_out, B * 2 + 2 * max(0, s - 1))
                        product(bank(4 + s % 2), s % T, 1 - s // T).then_inc(z_proj, 1)
                    u = s - 1
                    if 0 <= u < UNITS:
                        e.wait_ge(rot, B * 3 + 3 * u + 2)
                        e.wait_ge(qk_out, B + u)
                        nc.tensor.transpose(PS[:, B_T, 0:P], Z(u)[:, 0:P], ident)
                        nc.tensor.transpose(PS[:, B_T, P:2 * P], Z(u)[:, P:2 * P], ident).then_inc(qk_turned, 1)
                    u = s - 2
                    if 0 <= u < UNITS:
                        e.wait_ge(qk_out, B + u + 1)
                        e.wait_ge(r_probs, B + u)
                        nc.tensor.matmul(bank(B_S, P), QKT[u % 2][:, P:2 * P], QKT[u % 2][:, 0:P],
                                         start=True, stop=True).then_inc(r_scores, 1)
                    u = s - 3
                    if 0 <= u < UNITS:
                        e.wait_ge(r_probs, B + u + 1)
                        e.wait_ge(qd_out, B + u + 1)
                        e.wait_ge(rot, B * 3 + 3 * u + 3)
                        e.wait_ge(r_state, B + u)
                        e.wait_ge(gn_rows, B + u)
                        V = Z(u)[:, 2 * P:3 * P]
                        nc.tensor.matmul(bank(B_O, P), PT2[u % 2], V, start=True, stop=(u % T == 0))
                        if u % T:
                            nc.tensor.matmul(bank(B_O, P), QDT[u % 2], STATE, start=False, stop=True)
                        nc.tensor.matmul(bank(B_KV, P), KD[u % 4], V, start=True, stop=True).then_inc(r_okv, 1)

        def act_2(e):
            with e.Fori(0, HEADS * T // UNITS) as i:
                B = i * UNITS
                for s in range(UNITS + 3):
                    if s < UNITS:
                        e.wait_ge(z_proj, B + s + 1)
                        e.wait_ge(r_done, B + max(0, s - 3))
                        e.wait_ge(r_okv, B + max(0, s - 3))
                        b = PS[:, 4 + s % 2]
                        nc.scalar.copy(Z(s)[:, 0:3 * P], b[:, 0:3 * P]).then_inc(z_out, 1)
                        nc.scalar.activation(Z(s)[:, 3 * P:4 * P], b[:, 3 * P:4 * P], ACT.Silu).then_inc(z_out, 1)
                    u = s - 1
                    if 0 <= u < UNITS:
                        e.wait_ge(qk_turned, B + u + 1)
                        e.wait_ge(r_scores, B + max(0, u - 1))
                        e.wait_ge(qd_out, B + max(0, u - 1))
                        nc.scalar.copy(QKT[u % 2], bank(B_T, 2 * P)).then_inc(qk_out, 1)
                    if s < UNITS and s % 2 == 0:
                        hh, c = s // T, s % T // 2
                        e.wait_ge(z_proj, B + hh * T)
                        piece_m = M_RET + 4 + 4 * hh + c
                        e.wait_ge(s_raw[c], 16 * (piece_m // 4 + 1) + i * 32)
                        e.wait_ge(s_rawb[c], 16 * (hh + 2) + i * 32)
                        a = hh * 8192 + c * 1024
                        nc.scalar.copy(WF[:, a:a + 1024], RAW[:, c * 1024:(c + 1) * 1024]).then_inc(w_hi, 1)

        def pool_2(e):
            e.wait_ge(s_const, 16 * 4)
            with e.Fori(0, HEADS * T // UNITS) as i:
                B = i * UNITS
                for s in range(UNITS + 3):
                    if s < UNITS:
                        z = Z(s)[:, 0:2 * P].rearrange("p (q h n) -> p q h n", q=2, h=2)
                        ab = AB.rearrange("p (x q h n) -> p x q h n", x=2, q=2, h=2)
                        e.wait_ge(rot_ab, B * 2 + 2 * s + 2)
                        nc.gpsimd.tensor_tensor(z[:, :, 0], ab[:, 0, :, 0], ab[:, 1, :, 1], ALU.subtract).then_inc(rot, 1)
                        nc.gpsimd.tensor_tensor(z[:, :, 1], ab[:, 0, :, 1], ab[:, 1, :, 0], ALU.add).then_inc(rot, 1)
                        e.wait_ge(rot, B * 3 + 3 * s + 2)
                        e.wait_ge(r_okv, B + max(0, s - 3))
                        dec = HDEC[s // T]
                        nc.gpsimd.tensor_tensor(KD[s % 4], Z(s)[:, P:2 * P], dec.to_broadcast([P, P]),
                                                ALU.mult).then_inc(rot, 1)
                    u = s - 3
                    if 0 <= u < UNITS:
                        e.wait_ge(gn_stats, B * 2 + 2 * u + 2)
                        var, r = ST[:, 65:66], ST[:, 66:67]
                        nc.gpsimd.tensor_tensor(r, var, GNE[:, 0:1], ALU.add).then_inc(gn_mean, 1)
                        e.wait_ge(gn_mean, B + u + 1)
                        nc.gpsimd.tensor_tensor(r, r, NEGH[:, 0:1], ALU.pow).then_inc(gn_rstd, 1)
                        e.wait_ge(gn_rows, B + u + 1)
                        hcol = i * 2 * HD + (u // T) * HD
                        nc.gpsimd.tensor_tensor(RET[:, u % T, bass.ds(hcol, HD)], ON[u % 2],
                                                Z(u)[:, 3 * P:4 * P], ALU.mult).then_inc(r_done, 1)

        HCON = sb("HCON", [P, 2 * 2])
        HDEC = [HCON[:, 0:1], HCON[:, 1:2]]
        HCD = [HCON[:, 2:3], HCON[:, 3:4]]
        s_hcon = sem("s_hcon")

        def dve_2(e):
            with e.Fori(0, HEADS * T // UNITS) as i:
                B = i * UNITS
                e.wait_ge(rot, B * 3)
                e.wait_ge(r_state, B)
                nc.vector.tensor_copy(HCON[:, 0:2], CST[:, bass.ds(i * 2 + C_KDEC, 2)]).then_inc(s_hcon, 1)
                nc.vector.tensor_copy(HCON[:, 2:4], CST[:, bass.ds(i * 2 + C_CDEC, 2)]).then_inc(s_hcon, 1)
                e.wait_ge(s_hcon, i * 2 + 2)
                for s in range(UNITS + 3):
                    if s < UNITS:
                        z = Z(s)[:, 0:2 * P].rearrange("p (g n) -> p g n", g=4)
                        ab = AB.rearrange("p (x g n) -> p x g n", x=2, g=4)
                        if s == 0:
                            e.wait_ge(s_sin, 2)
                            e.wait_ge(s_decay, 16)
                        e.wait_ge(z_out, B * 2 + 2 * s + 2)
                        e.wait_ge(rot, B * 3 + (3 * s - 1 if s else 0))
                        for x, table in enumerate((COS, SIN)):
                            w = table[:, s % T].unsqueeze(1).to_broadcast([P, 4, 64])
                            nc.vector.tensor_tensor(ab[:, x], z, w, ALU.mult).then_inc(rot_ab, 1)
                    u = s - 1
                    if 0 <= u < UNITS:
                        e.wait_ge(qk_out, B + u + 1)
                        e.wait_ge(r_okv, B + max(0, u - 1))
                        col = i * 2 * P + (u // T) * P
                        nc.vector.tensor_tensor(QDT[u % 2], QKT[u % 2][:, 0:P], QDEC[:, bass.ds(col, P)],
                                                ALU.mult).then_inc(qd_out, 1)
                    u = s - 2
                    if 0 <= u < UNITS:
                        e.wait_ge(r_scores, B + u + 1)
                        e.wait_ge(r_okv, B + max(0, u - 1))
                        col = i * 2 * P + ((u // T) * P + C_DEC)
                        nc.vector.tensor_tensor(PT2[u % 2], bank(B_S, P), CST[:, bass.ds(col, P)],
                                                ALU.mult).then_inc(r_probs, 1)
                    u = s - 3
                    if 0 <= u < UNITS:
                        e.wait_ge(r_okv, B + u + 1)
                        nc.vector.bn_stats(ST[:, 68:74], bank(B_O, P)).then_inc(gn_stats, 1)
                        e.wait_ge(r_state, B + u)
                        e.wait_ge(gn_stats, B * 2 + 2 * u + 1)
                        if u % T:
                            nc.vector.scalar_tensor_tensor(STATE, STATE, HCD[u // T], bank(B_KV, P),
                                                           ALU.mult, ALU.add).then_inc(r_state, 1)
                        else:
                            nc.vector.tensor_copy(STATE, bank(B_KV, P)).then_inc(r_state, 1)
                        nc.vector.bn_aggr(ST[:, 64:66], ST[:, 68:74]).then_inc(gn_stats, 1)
                        e.wait_ge(gn_rstd, B + u + 1)
                        e.wait_ge(r_done, B + max(0, u - 1))
                        nc.vector.tensor_scalar(ON[u % 2], bank(B_O, P), ST[:, 64:65], ST[:, 66:67],
                                                ALU.subtract, ALU.mult).then_inc(gn_rows, 1)
                    if s < UNITS and s % 2 == 0:
                        hh, c = s // T, s % T // 2
                        e.wait_ge(z_proj, B + hh * T)
                        e.wait_ge(w_hi, M_RET + 4 + 4 * hh + c + 1 + i * 8)
                        a = hh * 8192 + c * 1024
                        nc.vector.tensor_tensor(WF[:, a + 4096:a + 5120], RAW[:, c * 1024:(c + 1) * 1024],
                                                WF[:, a:a + 1024].bitcast(F32), ALU.subtract).then_inc(w_lo, 1)

        lat_turned, lat_hi, lat_lo = sem("lat_turned"), sem("lat_hi"), sem("lat_lo")
        b_w, b_w_lo, b_v, b_v_out = sem("b_w"), sem("b_w_lo"), sem("b_v"), sem("b_v_out")
        b_q, b_ab, b_rot, b_qs, b_turn, b_qr = (sem("b_q"), sem("b_ab"), sem("b_rot"), sem("b_qs"),
                                                sem("b_turn"), sem("b_qr"))
        a_w, a_w_lo = sem("a_w"), sem("a_w_lo")
        a_proj, a_hi, a_lo, a_qr = sem("a_proj"), sem("a_hi"), sem("a_lo"), sem("a_qr")
        a_scores, a_mask, a_max, a_bias = sem("a_scores"), sem("a_mask"), sem("a_max"), sem("a_bias")
        a_exp, a_rec, a_prob, a_turn = sem("a_exp"), sem("a_rec"), sem("a_prob"), sem("a_turn")
        a_pt, a_pv, a_o_hi, a_o_lo = sem("a_pt"), sem("a_pv"), sem("a_o_hi"), sem("a_o_lo")
        a_vh = sem("a_vh")
        rt_turned, rt_hi, rt_lo = sem("rt_turned"), sem("rt_hi"), sem("rt_lo")
        NR = HEADS * T

        CT = [WF[:, 0:4096].rearrange("p (k n) -> p k n", k=4), WF[:, 4096:8192].rearrange("p (k n) -> p k n", k=4)]
        WS = 16384
        WQ = [WF[:, WS + p * 384:WS + p * 384 + 256].rearrange("p (k n) -> p k n", k=2) for p in range(2)]
        WK = [WF[:, WS + p * 384 + 256:WS + p * 384 + 384] for p in range(2)]
        QR = WF[:, WS + 768:WS + 1792]
        WR = [WF[:, WS + 1792 + p * 1024:WS + 2304 + p * 1024].rearrange("p (k n) -> p k n", k=2) for p in range(2)]
        WV = [WF[:, WS + 2304 + p * 1024:WS + 2816 + p * 1024] for p in range(2)]
        QRA = HTH[:, 0:4]
        KT = [HTL[:, 0], HTL[:, 1]]
        QT = [HTL[:, 2], HTL[:, 3]]
        QA, QB, QRF = tmp(3072, 256), tmp(3328, 256), tmp(3584, 256)
        QS = [tmp(2048, 512), tmp(2560, 512)]
        PT = [tmp(2048, 1024), tmp(3072, 1024)]
        VH = GB[:, :].rearrange("p (t n) -> p t n", t=T)
        RAWQ = RAW[:, 0:2048].rearrange("p (k n) -> p k n", k=2)

        def three(dst, pairs):
            for i, (a, b) in enumerate(pairs):
                for n, (x, y) in enumerate(((0, 0), (0, 1), (1, 0))):
                    last = nc.tensor.matmul(dst, a[x], b[y], start=(i + n == 0), stop=(i == len(pairs) - 1 and n == 2))
            return last

        def sp_3(e):
            e.wait_ge(w_lo, M_WO1)
            for k in range(2):
                e.dma_start(RAW[:, k * 1024:k * 1024 + 768], t_in["w_uq"][k * P:(k + 1) * P, :]).then_inc(s_att, 16)
            for k in range(2):
                e.dma_start(RAW[:, 2560 + k * 512:3072 + k * 512],
                            t_in["w_ukv"][:, k * 512:(k + 1) * 512]).then_inc(s_att, 16)

        def all_heads(width, a, n):
            if width == QK:
                return RAWQ[:, :, 0:HEADS * QK].rearrange("p k (h n) -> p k h n", h=HEADS)[:, :, :, a:a + n]
            return RAW[:, 2560:3584].rearrange("p (h n) -> p h n", h=HEADS)[:, :, a:a + n]

        def act_3a(e):
            e.wait_ge(s_att, 64)
            e.wait_ge(z_proj, NR)
            for k in range(2):
                nc.scalar.copy(WR[0][:, k].rearrange("p (h n) -> p h n", h=HEADS),
                               all_heads(QK, HD, ROPE)[:, k]).then_inc(b_w, 1)
            nc.scalar.copy(WV[0].rearrange("p (h n) -> p h n", h=HEADS), all_heads(2 * HD, HD, HD)).then_inc(b_w, 1)
            head_w_hi(e, 0)
            for t in range(T):
                e.wait_ge(lat_turned, t + 1)
                nc.scalar.copy(CT[0][:, :, t * P:t * P + P],
                               bank(t % 4).rearrange("p (k n) -> p k n", k=4)).then_inc(lat_hi, 1)
            for t in range(T):
                e.wait_ge(b_v, t + 1)
                nc.scalar.copy(VALL[:, t], bank(4 + t % 4)).then_inc(b_v_out, 1)
            for t in range(T):
                e.wait_ge(b_turn, t + 1)
                nc.scalar.copy(QRA[:, :, t * P:t * P + P],
                               bank(t % 4).rearrange("p (h n) -> p h n", h=HEADS)).then_inc(b_qr, 1)

        def dve_3a(e):
            for k in range(2):
                e.wait_ge(b_w, k + 1)
                nc.vector.tensor_tensor(WR[1][:, k].rearrange("p (h n) -> p h n", h=HEADS),
                                        all_heads(QK, HD, ROPE)[:, k],
                                        WR[0][:, k].rearrange("p (h n) -> p h n", h=HEADS).bitcast(F32),
                                        ALU.subtract).then_inc(b_w_lo, 1)
            e.wait_ge(b_w, 3)
            nc.vector.tensor_tensor(WV[1].rearrange("p (h n) -> p h n", h=HEADS), all_heads(2 * HD, HD, HD),
                                    WV[0].rearrange("p (h n) -> p h n", h=HEADS).bitcast(F32),
                                    ALU.subtract).then_inc(b_w_lo, 1)
            head_w_lo(e, 0)
            for t in range(T):
                e.wait_ge(lat_hi, t + 1)
                d = slice(t * P, t * P + P)
                nc.vector.tensor_tensor(CT[1][:, :, d], bank(t % 4).rearrange("p (k n) -> p k n", k=4),
                                        CT[0][:, :, d].bitcast(F32), ALU.subtract).then_inc(lat_lo, 1)

            def split(t):
                e.wait_ge(b_rot, 2 * t + 2)
                if t >= 2:
                    e.wait_ge(b_turn, t - 1)
                src = QRF.rearrange("p (h n) -> p h n", h=HEADS)
                qs = QS[t % 2].rearrange("p (h n) -> p h n", h=HEADS)
                nc.vector.tensor_copy(qs[:, :, 0:64].bitcast(F32R), src).then_inc(b_qs, 1)
                e.wait_ge(b_qs, 2 * t + 1)
                nc.vector.tensor_tensor(qs[:, :, 64:128], src, qs[:, :, 0:64], ALU.subtract).then_inc(b_qs, 1)
            e.wait_ge(r_done, NR)
            e.wait_ge(gn_rows, NR)
            for t in range(T):
                e.wait_ge(b_q, t + 1)
                if t:
                    e.wait_ge(b_rot, 2 * t)
                z = bank(4 + t % 4, 256).rearrange("p (g n) -> p g n", g=2 * HEADS)
                for x, table in ((QA, COS), (QB, SIN)):
                    w = table[:, t, 0:64:2].unsqueeze(1).to_broadcast([P, 2 * HEADS, 32])
                    nc.vector.tensor_tensor(x.rearrange("p (g n) -> p g n", g=2 * HEADS), z, w,
                                            ALU.mult).then_inc(b_ab, 1)
                split(t)

        def pool_3a(e):
            a, b, q = (x.rearrange("p (h i n) -> p h i n", h=HEADS, i=2) for x in (QA, QB, QRF))
            for t in range(T):
                e.wait_ge(b_ab, 2 * t + 2)
                if t:
                    e.wait_ge(b_qs, 2 * t)
                nc.gpsimd.tensor_tensor(q[:, :, 0], a[:, :, 0], b[:, :, 1], ALU.subtract).then_inc(b_rot, 1)
                nc.gpsimd.tensor_tensor(q[:, :, 1], a[:, :, 1], b[:, :, 0], ALU.add).then_inc(b_rot, 1)

        def pe_3a(e):
            e.wait_ge(gn_rows, NR)
            e.wait_ge(r_state, NR)
            e.wait_ge(lat_rope, 5)
            e.wait_ge(lat_rows, 2 * T)
            for t in range(T):
                if t >= 4:
                    e.wait_ge(lat_lo, t - 3)
                for k in range(4):
                    last = nc.tensor.transpose(PS[:, t % 4, k * P:k * P + P], CKV[:, t, k * P:k * P + P], ident)
                last.then_inc(lat_turned, 1)
            e.wait_ge(b_w_lo, 3)
            e.wait_ge(z_out, 2 * NR)
            e.wait_ge(lat_lo, T)

            def queries(t):
                if t < 4:
                    e.wait_ge(b_v_out, t + 5)
                else:
                    e.wait_ge(b_ab, 2 * (t - 3))
                tok = slice(t * P, t * P + P)
                three(bank(4 + t % 4, 256), [([CT[x][:, k, tok] for x in range(2)], [WR[y][:, k] for y in range(2)])
                                             for k in range(2)]).then_inc(b_q, 1)

            def turn(t):
                e.wait_ge(b_qs, 2 * t + 2)
                if t >= 4:
                    e.wait_ge(b_qr, t - 3)
                for h in range(HEADS):
                    last = nc.tensor.transpose(PS[:, t % 4, h * P:h * P + P], QS[t % 2][:, h * P:h * P + P], ident)
                last.then_inc(b_turn, 1)

            for t in range(T):
                if t >= 4:
                    e.wait_ge(b_v_out, t - 3)
                tok = slice(t * P, t * P + P)
                three(bank(4 + t % 4), [([CT[x][:, 2, tok] for x in range(2)], WV)]).then_inc(b_v, 1)
            for t in range(T):
                queries(t)
                if t >= 2:
                    turn(t - 2)
            turn(T - 2)
            turn(T - 1)

        def head_w_hi(e, h):
            nc.scalar.copy(WQ[0], RAWQ[:, :, bass.ds(h * QK, HD)]).then_inc(a_w, 1)
            nc.scalar.copy(WK[0], RAW[:, bass.ds(h * 2 * HD + 2560, HD)]).then_inc(a_w, 1)

        def head_w_lo(e, h):
            e.wait_ge(a_w, h * 2 + 2)
            nc.vector.tensor_tensor(WQ[1], RAWQ[:, :, bass.ds(h * QK, HD)], WQ[0].bitcast(F32),
                                    ALU.subtract).then_inc(a_w_lo, 1)
            nc.vector.tensor_tensor(WK[1], RAW[:, bass.ds(h * 2 * HD + 2560, HD)], WK[0].bitcast(F32),
                                    ALU.subtract).then_inc(a_w_lo, 1)

        def head_project(e, h):
            e.wait_ge(a_w_lo, h * 2 + 2)
            for b in range(2):
                blk = slice(b * HALF, (b + 1) * HALF)
                three(bank(b), [(WK, [CT[y][:, 2, blk] for y in range(2)])]).then_inc(a_proj, 1)
            for b in range(2):
                blk = slice(b * HALF, (b + 1) * HALF)
                three(bank(2 + b), [([WQ[x][:, k] for x in range(2)], [CT[y][:, k, blk] for y in range(2)])
                                    for k in range(2)]).then_inc(a_proj, 1)

        PLACES = ((KT, 0), (KT, 1), (QT, 2), (QT, 3))

        def head_hi(e, h):
            for n, (where, b) in enumerate(PLACES):
                e.wait_ge(a_proj, h * 4 + n + 1)
                blk = slice((b % 2) * HALF, (b % 2 + 1) * HALF)
                nc.scalar.copy(where[0][:, blk], bank(b)).then_inc(a_hi, 1)
            nc.scalar.copy(QR, HTH[:, bass.ds(h, 1), :].rearrange("p a n -> p (a n)")).then_inc(a_qr, 1)

        def head_lo(e, h):
            for n, (where, b) in enumerate(PLACES):
                e.wait_ge(a_hi, h * 4 + n + 1)
                blk = slice((b % 2) * HALF, (b % 2 + 1) * HALF)
                nc.vector.tensor_tensor(where[1][:, blk], bank(b), where[0][:, blk].bitcast(F32),
                                        ALU.subtract).then_inc(a_lo, 1)

        def seen(t):
            return (1, (t + 1) * P) if t < 4 else (2, (t + 1) * P // 2)

        def score_banks(t):
            nb, n = seen(t)
            b = 2 * ((t + 1) % 2)
            return PS[:, b:b + nb, 0:n]

        def pe_head(e, h, after):
            def scores(t):
                if t == 0:
                    e.wait_ge(a_lo, h * 4 + 4)
                    e.wait_ge(a_qr, h + 1)
                if t >= 2:
                    e.wait_ge(a_exp, h * T + t - 1)
                tok = slice(t * P, t * P + P)
                nb, n = seen(t)
                for c in range(nb):
                    blk = slice(c * n, c * n + max(n, 2 * P))
                    dst = bank(2 * ((t + 1) % 2) + c, max(n, 2 * P))
                    for i, (a, b) in enumerate(((QT[0], KT[0]), (QT[0], KT[1]), (QT[1], KT[0]),
                                                (QR, CT[0][:, 3]), (QR, CT[1][:, 3]))):
                        last = nc.tensor.matmul(dst, a[:, tok], b[:, blk], start=(i == 0), stop=(i == 4))
                last.then_inc(a_scores, 1)

            def turn(t):
                e.wait_ge(a_prob, h * T + t + 1)
                e.wait_ge(a_pt, h * T + t)
                for j in range(t + 1):
                    last = nc.tensor.transpose(PS[:, 4 + j // 4, (j % 4) * P:(j % 4) * P + P],
                                               tmp((t % 2) * 1024 + j * P, P), ident)
                last.then_inc(a_turn, 1)

            def values(t):
                e.wait_ge(a_vh, h + 1)
                e.wait_ge(a_pt, h * T + t + 1)
                e.wait_ge(a_o_lo, h * T + max(0, t - 1))
                for j in range(t + 1):
                    last = nc.tensor.matmul(bank(6 + t % 2, P), VH[:, j], PT[t % 2][:, j * P:j * P + P], start=(j == 0), stop=(j == t))
                last.then_inc(a_pv, 1)

            scores(0)
            scores(1)
            for t in range(T):
                if t + 2 < T:
                    scores(t + 2)
                if t >= 1:
                    values(t - 1)
                turn(t)
            e.wait_ge(a_exp, h * T + T)
            after()
            values(T - 1)

        def act_head(e, h, early, after):
            def exp(t):
                e.wait_ge(a_bias, h * T + t + 1)
                e.wait_ge(a_turn, h * T + max(0, t - 1))
                nb, n = seen(t)
                dst = tmp((t % 2) * 1024, nb * n).rearrange("p (b n) -> p b n", b=nb)
                nc.scalar.activation(dst, score_banks(t), ACT.Exp, bias=ST[:, 76 + t % 2:77 + t % 2],
                                     scale=SCALE, accum_out=ST[:, 78 + t % 2:79 + t % 2]).then_inc(a_exp, 1)

            def out_hi(t):
                e.wait_ge(a_pv, h * T + t + 1)
                nc.scalar.copy(HTH[:, bass.ds(h + 4, 1), t * P:t * P + P],
                               bank(6 + t % 2, P).unsqueeze(1)).then_inc(a_o_hi, 1)

            exp(0)
            for t in range(T):
                if t + 1 < T:
                    exp(t + 1)
                if t >= 1:
                    out_hi(t - 1)
                if t == 3:
                    early()
                e.wait_ge(a_turn, h * T + t + 1)
                e.wait_ge(a_pv, h * T + max(0, t - 1))
                n = (t + 1) * P
                src = PS[:, 4:6, :].rearrange("p b n -> p (b n)")[:, 0:n]
                nc.scalar.copy(PT[t % 2][:, 0:n], src).then_inc(a_pt, 1)
            after()
            out_hi(T - 1)

        def dve_head(e, h, early, after):
            def biggest(t):
                e.wait_ge(a_scores, h * T + t + 1)
                e.wait_ge(a_exp, h * T + max(0, t - 1))
                src = score_banks(t)
                nb, n = seen(t)
                nc.vector.memset(src[0:CHUNK, nb - 1, n - CHUNK:n], MASKED).then_inc(a_mask, 1)
                e.wait_ge(a_mask, h * T + t + 1)
                nc.vector.tensor_reduce(ST[:, 74 + t % 2:75 + t % 2], src, mybir.AxisListType.XY if nb > 1 else AXX,
                                        ALU.max).then_inc(a_max, 1)
                e.wait_ge(a_max, h * T + t + 1)
                nc.vector.tensor_scalar(ST[:, 76 + t % 2:77 + t % 2], ST[:, 74 + t % 2:75 + t % 2], -SCALE, None,
                                        ALU.mult).then_inc(a_bias, 1)

            def out_lo(t):
                e.wait_ge(a_o_hi, h * T + t + 1)
                d = slice(t * P, t * P + P)
                nc.vector.tensor_tensor(HTL[:, bass.ds(h + 4, 1), d], bank(6 + t % 2, P).unsqueeze(1),
                                        HTH[:, bass.ds(h + 4, 1), d].bitcast(F32), ALU.subtract).then_inc(a_o_lo, 1)

            def divide(t):
                e.wait_ge(a_exp, h * T + t + 1)
                n = (t + 1) * P
                nc.vector.reciprocal(ST[:, 80 + t % 2:81 + t % 2], ST[:, 78 + t % 2:79 + t % 2]).then_inc(a_rec, 1)
                e.wait_ge(a_rec, h * T + t + 1)
                p = tmp((t % 2) * 1024, n)
                nc.vector.tensor_scalar(p, p, ST[:, 80 + t % 2:81 + t % 2], None, ALU.mult).then_inc(a_prob, 1)

            biggest(0)
            biggest(1)
            divide(0)
            for t in range(T):
                if t + 2 < T:
                    biggest(t + 2)
                if t + 1 < T:
                    divide(t + 1)
                if t >= 1:
                    out_lo(t - 1)
                if t == 3:
                    early()
            after()
            out_lo(T - 1)

        def pe_3b(e):
            e.wait_ge(b_qr, T)
            head_project(e, 0)
            with e.Fori(0, HEADS - 1) as h:
                pe_head(e, h, lambda: head_project(e, h + 1))
            pe_head(e, HEADS - 1, lambda: pe_retention_turn(e))

        def nothing():
            pass

        def act_3b(e):
            head_hi(e, 0)

            def next_weights(h):
                e.wait_ge(a_proj, h * 4 + 4)
                head_w_hi(e, h + 1)

            def next_head(h):
                e.wait_ge(a_scores, h * T + T)
                head_hi(e, h + 1)
            with e.Fori(0, HEADS - 1) as h:
                act_head(e, h, lambda: next_weights(h), lambda: next_head(h))
            act_head(e, HEADS - 1, nothing, lambda: act_retention_hi(e))

        def dve_3b(e):
            head_lo(e, 0)
            with e.Fori(0, HEADS - 1) as h:
                dve_head(e, h, lambda: head_w_lo(e, h + 1), lambda: head_lo(e, h + 1))
            dve_head(e, HEADS - 1, nothing, lambda: dve_retention_lo(e))

        def pool_3b(e):
            e.wait_ge(b_v_out, T)
            e.wait_ge(r_okv, NR)
            with e.Fori(0, HEADS) as h:
                e.wait_ge(a_pv, h * T)
                nc.gpsimd.tensor_copy(VH, VALL[:, :, bass.ds(h * HD, HD)]).then_inc(a_vh, 1)

        def pe_retention_turn(e):
            e.wait_ge(r_done, NR)
            for t in range(T):
                if t >= 4:
                    e.wait_ge(rt_lo, t - 3)
                for k in range(4):
                    last = nc.tensor.transpose(PS[:, t % 4, k * P:k * P + P], RET[:, t, k * P:k * P + P], ident)
                last.then_inc(rt_turned, 1)

        def act_retention_hi(e):
            for t in range(T):
                e.wait_ge(rt_turned, t + 1)
                nc.scalar.copy(HTH[:, 0:4, t * P:t * P + P],
                               bank(t % 4).rearrange("p (k n) -> p k n", k=4)).then_inc(rt_hi, 1)

        def dve_retention_lo(e):
            for t in range(T):
                e.wait_ge(rt_hi, t + 1)
                d = slice(t * P, t * P + P)
                nc.vector.tensor_tensor(HTL[:, 0:4, d], bank(t % 4).rearrange("p (k n) -> p k n", k=4),
                                        HTH[:, 0:4, d].bitcast(F32), ALU.subtract).then_inc(rt_lo, 1)

        o_done, o_added = sem("o_done"), sem("o_added")

        def sp_4(e):
            e.wait_ge(a_w_lo, 2 * HEADS)
            sp_out_weights(e, 1, M_WO1)
            e.wait_ge(a_vh, HEADS)
            for t in range(4, T):
                e.dma_start(X3[:, t, :], t_in["x"][t * P:(t + 1) * P, :]).then_inc(s_x[t % 4], 16)
            e.wait_ge(rt_turned, T)
            for t in range(4):
                e.dma_start(X3[:, t, :], t_in["x"][t * P:(t + 1) * P, :]).then_inc(s_x[t], 16)
            e.wait_ge(a_pv, NR)
            e.dma_start(GB[:, :], t_in["ffn_norm_g"].partition_broadcast(P)).then_inc(s_gain, 16)

        def pe_4(e):
            e.wait_ge(a_o_lo, NR)
            e.wait_ge(a_pt, NR)
            for half in range(2):
                if half == 1:
                    e.wait_ge(w_lo, M_WO1 + 4)
                for t in range(T):
                    n = half * T + t
                    e.wait_ge(rt_lo, t + 1)
                    if n >= 4:
                        e.wait_ge(o_added, n - 3)
                    product(bank(4 + n % 4), t, 1 - half).then_inc(o_done, 1)
                    if half == 1 and t >= 2:
                        norm_turn(e, n_ffn, t - 2)
            norm_turn(e, n_ffn, T - 2)
            norm_turn(e, n_ffn, T - 1)

        def act_4(e):
            for c in range(4):
                e.wait_ge(s_rawb[c], 16 * (HEADS + 2))
                granule_hi(e, 0, c, M_WO1 + c)
            for t in range(T):
                squares_x(e, n_ffn, t, 48, o_added, T + t + 1)
                if t >= 2:
                    turned_hi(e, n_ffn, t - 2)
                if t in (2, 4):
                    for c in range(2):
                        ffn_hi(e, (M_FFN + c + t - 2), 8192 + (t - 2) // 2 * 4096 + c * 2048)
            turned_hi(e, n_ffn, T - 2)
            turned_hi(e, n_ffn, T - 1)

        def squares_x(e, s, t, col, ready, count):
            e.wait_ge(ready, count)
            if t:
                e.wait_ge(s.squares, t)
            norm_squares(e, s, t, col, X3[:, t, :], JUNK)

        def rows_x(e, s, t, col):
            if t >= 2:
                e.wait_ge(s.turned, t - 1)
            norm_rows(e, s, t, col, X3[:, t, :], tmp(2048 + (t % 2) * 1024, 1024))

        def add_x(e, src, t, lo, n, done):
            x = X3[:, t, lo:lo + n]
            nc.vector.tensor_tensor(x, x, src, ALU.add).then_inc(done, 1)

        def dve_4(e):
            for c in range(4):
                granule_lo(e, 0, c, M_WO1 + c)
            for half in range(2):
                for t in range(T):
                    n = half * T + t
                    e.wait_ge(o_done, n + 1)
                    if half == 0:
                        e.wait_ge(s_x[t % 4], 16 * (3 if t >= 4 else 4))
                    add_x(e, bank(4 + n % 4), t, half * HALF, HALF, o_added)
                    if half == 1:
                        if t >= 1:
                            if t == 1:
                                e.wait_ge(s_gain, 32)
                            rows_x(e, n_ffn, t - 1, 48)
                        if t >= 3:
                            turned_lo(e, n_ffn, t - 3)
                        if t in (2, 4):
                            for c in range(2):
                                ffn_lo(e, (M_FFN + c + t - 2), 8192 + (t - 2) // 2 * 4096 + c * 2048)
            rows_x(e, n_ffn, T - 1, 48)
            for t in range(T - 3, T):
                turned_lo(e, n_ffn, t)

        def pool_4(e):
            for t in range(T):
                norm_rstd(e, n_ffn, t, 48)

        f_gu, f_silu, f_hid, f_hi, f_lo = sem("f_gu"), sem("f_silu"), sem("f_hid"), sem("f_hi"), sem("f_lo")
        f_down, f_added = sem("f_down"), sem("f_added")

        def ffn_hi(e, m, a, more=0):
            arrived(e, m, more * 4)
            nc.scalar.copy(WF[:, a:a + 1024], raw(m)).then_inc(w_hi, 1)

        def ffn_lo(e, m, a, more=0):
            e.wait_ge(w_hi, m + 1 + more)
            nc.vector.tensor_tensor(WF[:, a + 1024:a + 2048], raw(m), WF[:, a:a + 1024].bitcast(F32),
                                    ALU.subtract).then_inc(w_lo, 1)

        def m_block(g):
            return M_FFN + 8 + 6 * (g - 1)

        def sp_ffn_gu(e, m, g, jj, more=0, col=0):
            for n, name in enumerate(("w_ffn_gate", "w_ffn_up")):
                w = t_in[name].rearrange("(k p) n -> p k n", p=P)
                e.wait_ge(w_lo, m + n - 3 + more)
                e.dma_start(raw(m + n).rearrange("p (k n) -> p k n", k=K),
                            w[:, :, bass.ds(col + (g * GROUP + jj) * P, P)]).then_inc(s_raw[(m + n) % 4], 16)

        def sp_ffn_down(e, m, g, more=0, row=0):
            for jj in range(GROUP):
                e.wait_ge(w_lo, m + jj - 3 + more)
                w = t_in["w_ffn_down"]
                e.dma_start(raw(m + jj), w[bass.ds(row + (g * GROUP + jj) * P, P), :]).then_inc(s_raw[(m + jj) % 4], 16)

        def sp_5(e):
            for g in range(2):
                for jj in range(2):
                    sp_ffn_gu(e, M_FFN + 4 * g + 2 * jj, g, jj)

            def block(g, i=0, last=False):
                m = m_block(g)
                sp_ffn_down(e, m, g - 1, i * 12, i * (2 * GROUP * P))
                if not last:
                    for jj in range(2):
                        sp_ffn_gu(e, m + 2 + 2 * jj, g + 1, jj, i * 12, i * (2 * GROUP * P))
            with e.Fori(0, (NG - 3) // 2) as i:
                block(1, i)
                block(2, i)
            block(NG - 2)
            block(NG - 1, last=True)
            sp_ffn_down(e, m_block(NG - 1) + 2, NG - 1)

        def pe_gu(e, g, i=0):
            for jj in range(GROUP):
                for b in range(2):
                    u = 4 * g + 2 * jj + b
                    if b == 0:
                        m = M_FFN + 2 * jj + 2 if g == 0 else (M_FFN + 4 + 2 * jj + 2 if g == 1 else m_block(g - 1) + 4 + 2 * jj)
                        e.wait_ge(w_lo, m + i * 12)
                    if g == 0:
                        e.wait_ge(n_ffn.lo, 2 * T - 2 + 2 * b)
                    if u >= 2:
                        e.wait_ge(f_hid, u - 1 + i * 8)
                    blk = slice(b * HALF, (b + 1) * HALF)
                    for x in range(2):
                        a = 8192 + 4096 * jj + 2048 * x
                        dst = bank(2 * (u % 2) + x)
                        for k in range(K):
                            w_h, w_l = WF[:, a + k * P:a + k * P + P], WF[:, a + 1024 + k * P:a + 1024 + k * P + P]
                            nc.tensor.matmul(dst, w_h, HTH[:, k, blk], start=(k == 0), stop=False)
                            nc.tensor.matmul(dst, w_h, HTL[:, k, blk], start=False, stop=False)
                            last = nc.tensor.matmul(dst, w_l, HTH[:, k, blk], start=False, stop=(k == K - 1))
                    last.then_inc(f_gu, 1)

        def pe_down(e, g, i=0, more=None):
            e.wait_ge(f_lo, 4 * (g + 1) + i * 8)
            m = m_block(g + 1) + 2 if g < NG - 1 else m_block(NG - 1) + 4
            e.wait_ge(w_lo, m + i * 12)
            for t in range(T):
                for half in range(2):
                    n = 16 * g + 2 * t + half
                    if n >= 4:
                        e.wait_ge(f_added, n - 3 + i * 32)
                    dst = bank(4 + n % 4)
                    for jj in range(GROUP):
                        hid = (g % 2) * 4096 + 2048 * jj + t * P
                        w = 16384 + 2048 * jj + half * HALF
                        nc.tensor.matmul(dst, WF[:, hid:hid + P], WF[:, w:w + HALF], start=(jj == 0), stop=False)
                        nc.tensor.matmul(dst, WF[:, hid:hid + P], WF[:, w + 1024:w + 1024 + HALF], start=False, stop=False)
                        last = nc.tensor.matmul(dst, WF[:, hid + 1024:hid + 1024 + P], WF[:, w:w + HALF],
                                                start=False, stop=(jj == GROUP - 1))
                    last.then_inc(f_down, 1)
                if more:
                    more(t)

        def pe_5(e):
            e.wait_ge(o_added, 2 * T)
            pe_gu(e, 0)
            with e.Fori(0, (NG - 3) // 2) as i:
                for g in (1, 2):
                    pe_gu(e, g, i)
                    pe_down(e, g - 1, i)
            for g in (NG - 2, NG - 1):
                pe_gu(e, g)
                pe_down(e, g - 1)

            def turn(t):
                if t == 0:
                    pt_turn(e)
                if t >= 2:
                    norm_turn(e, n_ple, t - 2)
            pe_down(e, NG - 1, more=turn)
            norm_turn(e, n_ple, T - 2)
            norm_turn(e, n_ple, T - 1)

        def act_hidden(e, g, jj, b, i=0):
            u = 4 * g + 2 * jj + b
            e.wait_ge(f_gu, u + 1 + i * 8)
            if u >= 2:
                e.wait_ge(f_hid, u - 1 + i * 8)
            nc.scalar.activation(tmp((u % 2) * HALF, HALF), bank(2 * (u % 2)), ACT.Silu).then_inc(f_silu, 1)
            e.wait_ge(f_hid, u + 1 + i * 8)
            if g >= 2 and b == 0:
                e.wait_ge(f_down, 16 * (g - 1) + i * 32)
            a = (g % 2) * 4096 + 2048 * jj + b * HALF
            nc.scalar.copy(WF[:, a:a + HALF], tmp(1024 + (u % 2) * HALF, HALF)).then_inc(f_hi, 1)

        def dve_hidden(e, g, jj, b, i=0):
            u = 4 * g + 2 * jj + b
            e.wait_ge(f_silu, u + 1 + i * 8)
            if u >= 2:
                e.wait_ge(f_lo, u - 1 + i * 8)
            h = tmp(1024 + (u % 2) * HALF, HALF)
            nc.vector.tensor_tensor(h, tmp((u % 2) * HALF, HALF), bank(2 * (u % 2) + 1), ALU.mult).then_inc(f_hid, 1)
            e.wait_ge(f_hi, u + 1 + i * 8)
            a = (g % 2) * 4096 + 2048 * jj + b * HALF
            nc.vector.tensor_tensor(WF[:, a + 1024:a + 1024 + HALF], h, WF[:, a:a + HALF].bitcast(F32),
                                    ALU.subtract).then_inc(f_lo, 1)

        def ffn_block(e, g, i, hidden, piece, adds, last=False):
            m = m_block(g)
            hidden(e, g, 0, 0, i)
            if g >= 2:
                e.wait_ge(f_down, 16 * (g - 1) + i * 32)
            for jj in range(2):
                piece(e, m + jj, 16384 + 2048 * jj, i * 12)
            hidden(e, g, 0, 1, i)
            for b in range(2):
                hidden(e, g, 1, b, i)
                if not last:
                    e.wait_ge(f_gu, 4 * g + 2 + i * 8)
                    piece(e, m + 2 + b, 8192 + 2048 * b, i * 12)
            for n in range(16):
                if adds:
                    adds(e, g - 1, n, i)
                if not last and n in (2, 6):
                    e.wait_ge(f_gu, 4 * g + 4 + i * 8)
                    piece(e, m + 4 + n // 4, 12288 + 2048 * (n // 4), i * 12)

        def add_down(e, g, n, i=0):
            e.wait_ge(f_down, 16 * g + n + 1 + i * 32)
            if g >= 1:
                e.wait_ge(f_added, 16 * (g - 1) + n + 1 + i * 32)
            add_x(e, bank(4 + (16 * g + n) % 4), n // 2, (n % 2) * HALF, HALF, f_added)

        def ffn_5(e, hidden, piece, adds, first):
            for jj in range(2):
                for b in range(2):
                    hidden(e, 0, jj, b)
                e.wait_ge(f_gu, 2 * jj + 2)
                for n in range(2):
                    piece(e, M_FFN + 4 + 2 * jj + n, 8192 + 4096 * jj + 2048 * n, 0)
            with e.Fori(0, (NG - 3) // 2) as i:
                ffn_block(e, 1, i, hidden, piece, adds)
                ffn_block(e, 2, i, hidden, piece, adds)
            ffn_block(e, NG - 2, 0, hidden, piece, adds)
            ffn_block(e, NG - 1, 0, hidden, piece, adds, last=True)
            e.wait_ge(f_down, 16 * (NG - 1))
            for jj in range(2):
                piece(e, m_block(NG - 1) + 2 + jj, 16384 + 2048 * jj, 0)

        def act_5(e):
            ffn_5(e, act_hidden, ffn_hi, None, 0)

        def dve_5(e):
            ffn_5(e, dve_hidden, ffn_lo, add_down, 0)

        s_p, p_turned, p_hi, p_lo = sem("s_p"), sem("p_turned"), sem("p_hi"), sem("p_lo")
        g_done, g_sig, g_mul, g_added, s_out = sem("g_done"), sem("g_sig"), sem("g_mul"), sem("g_added"), [sem("s_out0"), sem("s_out1")]
        M6 = M_PLE
        QC = 256
        PTP = [WF[:, 4096:6144].rearrange("p (k n) -> p k n", k=2), WF[:, 6144:8192].rearrange("p (k n) -> p k n", k=2)]
        PW = 8192
        GQ = [12288, 0]
        PIN = tmp(0, 2048).rearrange("p (t n) -> p t n", t=T)

        def sp_6(e):
            e.wait_ge(f_lo, 4 * NG)
            e.dma_start(PIN, t_in["p"].rearrange("(t p) n -> p t n", p=P)).then_inc(s_p, 16)
            e.wait_ge(n_ffn.normed, T)
            e.dma_start(GB[:, :], t_in["ple_norm_g"].partition_broadcast(P)).then_inc(s_gain, 16)
            for k in range(2):
                e.wait_ge(w_lo, M6 + k - 3)
                e.dma_start(raw(M6 + k), t_in["w_ple_proj"][k * P:(k + 1) * P, :]).then_inc(s_raw[(M6 + k) % 4], 16)
            w = t_in["w_ple_gate"].rearrange("(k p) n -> p k n", p=P)
            for q in range(4):
                for c in range(2):
                    m = M6 + 2 + 2 * q + c
                    e.wait_ge(w_lo, m - 3)
                    e.dma_start(raw(m).rearrange("p (k n) -> p k n", k=4),
                                w[:, 4 * c:4 * c + 4, q * QC:(q + 1) * QC]).then_inc(s_raw[m % 4], 16)
                if q == 1:
                    e.wait_ge(n_ple.normed, T)
                    e.dma_start(GB[:, :], t_in["final_norm_g"].partition_broadcast(P)).then_inc(s_gain, 16)
            for t in range(T):
                e.wait_ge(n_out.normed, t + 1)
                e.dma_start(out[t * P:(t + 1) * P, :], tmp(2048 + (t % 2) * 1024, 1024)).then_inc(s_out[t % 2], 16)
            for c in range(2):
                e.wait_ge(s_out[c], 16 * T // 2)

        def pt_turn(e):
            e.wait_ge(s_p, 16)
            e.wait_ge(f_hid, 4 * NG)
            for t in range(T):
                for k in range(2):
                    last = nc.tensor.transpose(PS[:, t // 2, (t % 2) * QC + k * P:(t % 2) * QC + k * P + P],
                                               PIN[:, t, k * P:k * P + P], ident)
            last.then_inc(p_turned, 1)

        def p_halves(e, s, f):
            for t in range(T):
                src = PS[:, t // 2, (t % 2) * QC:(t % 2) * QC + QC].rearrange("p (k n) -> p k n", k=2)
                f(t, src, PTP[0][:, :, t * P:t * P + P], PTP[1][:, :, t * P:t * P + P]).then_inc(s, 1)

        def act_6(e):
            e.wait_ge(p_turned, 1)
            e.wait_ge(f_down, 16 * (NG - 1))
            p_halves(e, p_hi, lambda t, src, hi, lo: nc.scalar.copy(hi, src))
            for k in range(2):
                ffn_hi(e, M6 + k, PW + 2048 * k)
            gate_hi(e, 0)
            for t in range(T):
                squares_x(e, n_ple, t, 48, f_added, 16 * (NG - 1) + 2 * t + 2)
                if t == 3:
                    pass
                if t >= 2:
                    turned_hi(e, n_ple, t - 2)
            turned_hi(e, n_ple, T - 2)
            turned_hi(e, n_ple, T - 1)
            gate_hi(e, 1)
            for q in range(4):
                for t in range(T):
                    u = q * T + t
                    e.wait_ge(g_done, u + 1)
                    if u >= 4:
                        e.wait_ge(g_mul, u - 3)
                    nc.scalar.activation(tmp((u % 4) * QC, QC), PS[:, u % 8, 0:QC], ACT.Sigmoid).then_inc(g_sig, 1)
                    if t == 0 and 1 <= q < 3:
                        gate_hi(e, q + 1)
                    if q == 3 and t >= 1:
                        squares_x(e, n_out, t - 1, 96, g_added, 3 * T + t)
            squares_x(e, n_out, T - 1, 96, g_added, 4 * T)

        def gate_hi(e, q):
            if q == 1:
                e.wait_ge(f_down, 16 * NG)
            if q >= 2:
                e.wait_ge(g_done, (q - 1) * T)
            for c in range(2):
                m, a = M6 + 2 + 2 * q + c, GQ[q % 2] + 1024 * c
                arrived(e, m)
                nc.scalar.copy(WF[:, a:a + 1024], raw(m)).then_inc(w_hi, 1)

        def gate_lo(e, q):
            for c in range(2):
                m, a = M6 + 2 + 2 * q + c, GQ[q % 2] + 1024 * c
                e.wait_ge(w_hi, m + 1)
                nc.vector.tensor_tensor(WF[:, a + 2048:a + 3072], raw(m), WF[:, a:a + 1024].bitcast(F32),
                                        ALU.subtract).then_inc(w_lo, 1)

        def dve_6(e):
            e.wait_ge(p_hi, T)
            p_halves(e, p_lo, lambda t, src, hi, lo: nc.vector.tensor_tensor(lo, src, hi.bitcast(F32), ALU.subtract))
            for k in range(2):
                ffn_lo(e, M6 + k, PW + 2048 * k)
            gate_lo(e, 0)
            e.wait_ge(s_gain, 48)
            for t in range(T):
                add_down(e, NG - 1, 2 * t)
                add_down(e, NG - 1, 2 * t + 1)
                if t >= 1:
                    rows_x(e, n_ple, t - 1, 48)
                if t >= 3:
                    turned_lo(e, n_ple, t - 3)
            rows_x(e, n_ple, T - 1, 48)
            for t in range(T - 3, T):
                turned_lo(e, n_ple, t)
            gate_lo(e, 1)
            for q in range(4):
                for t in range(T):
                    u = q * T + t
                    e.wait_ge(g_sig, u + 1)
                    if u >= 4:
                        e.wait_ge(g_added, u - 3)
                    m = tmp(1024 + (u % 4) * QC, QC)
                    nc.vector.tensor_tensor(m, tmp((u % 4) * QC, QC), PS[:, u % 8, QC:2 * QC], ALU.mult).then_inc(g_mul, 1)
                    if t == 0 and 1 <= q < 3:
                        gate_lo(e, q + 1)
                    if q == 3 and t >= 2:
                        out_rows(e, t - 2)
            out_rows(e, T - 2)
            out_rows(e, T - 1)

        def out_rows(e, t):
            if t == 0:
                e.wait_ge(s_gain, 64)
            if t >= 2:
                e.wait_ge(s_out[t % 2], 16 * (t // 2))
            norm_rows(e, n_out, t, 96, X3[:, t, :], tmp(2048 + (t % 2) * 1024, 1024))

        def pool_6(e):
            for t in range(T):
                norm_rstd(e, n_ple, t, 48)
            for q in range(4):
                for t in range(T):
                    u = q * T + t
                    e.wait_ge(g_mul, u + 1)
                    x = X3[:, t, q * QC:(q + 1) * QC]
                    nc.gpsimd.tensor_tensor(x, x, tmp(1024 + (u % 4) * QC, QC), ALU.add).then_inc(g_added, 1)
                    if q == 3 and t >= 1:
                        norm_rstd(e, n_out, t - 1, 96)
            norm_rstd(e, n_out, T - 1, 96)

        def pe_6(e):
            e.wait_ge(n_ple.lo, 2 * T)
            e.wait_ge(f_added, 16 * NG)
            e.wait_ge(p_lo, T)
            with e.Fori(0, 2) as j:
                for q in range(2):
                    e.wait_ge(w_lo, M6 + 4 + 2 * q + j * 4)
                    for t in range(T):
                        u = q * T + t
                        e.wait_ge(g_mul, j * 16 + max(0, u - 7))
                        tok = slice(t * P, t * P + P)
                        gate, emb = PS[:, u % 8, 0:QC], PS[:, u % 8, QC:2 * QC]
                        for k in range(K):
                            a = GQ[q] + k * QC
                            nc.tensor.matmul(gate, HTH[:, k, tok], WF[:, a:a + QC], start=(k == 0), stop=False)
                            nc.tensor.matmul(gate, HTH[:, k, tok], WF[:, a + 2048:a + 2048 + QC], start=False, stop=False)
                            nc.tensor.matmul(gate, HTL[:, k, tok], WF[:, a:a + QC], start=False, stop=(k == K - 1))
                        for k in range(2):
                            for n, (x, y) in enumerate(((0, 0), (0, 1), (1, 0))):
                                a = j * 512 + (PW + 2048 * k + 1024 * y + q * QC)
                                last = nc.tensor.matmul(emb, PTP[x][:, k, tok], WF[:, bass.ds(a, QC)],
                                                        start=(k + n == 0), stop=(k * n == 2))
                        last.then_inc(g_done, 1)

        block = ctx.enter_context(nc.Block())

        @block.sync
        def _(sp):
            sp_1(sp)
            sp_retention(sp)
            sp_out_weights(sp, 0, M_WO0)
            sp_3(sp)
            sp_4(sp)
            sp_5(sp)
            sp_6(sp)

        @block.gpsimd
        def _(pool):
            pool_1(pool)
            pool_2(pool)
            pool_3a(pool)
            pool_3b(pool)
            pool_4(pool)
            pool_6(pool)

        @block.scalar
        def _(act):
            act_1(act)
            act_2(act)
            act_3a(act)
            act_3b(act)
            act_4(act)
            act_5(act)
            act_6(act)

        @block.vector
        def _(dve):
            dve_1(dve)
            dve_2(dve)
            dve_3a(dve)
            dve_3b(dve)
            dve_4(dve)
            dve_5(dve)
            dve_6(dve)

        @block.tensor
        def _(pe):
            pe_1(pe)
            pe_2(pe)
            pe_3a(pe)
            pe_3b(pe)
            pe_4(pe)
            pe_5(pe)
            pe_6(pe)


def kernel(x, p, positions, mix_norm_g, w_in, q_norm_g, w_uq, kv_norm_g, w_ukv, w_o,
           ffn_norm_g, w_ffn_gate, w_ffn_up, w_ffn_down, ple_norm_g, w_ple_gate,
           w_ple_proj, final_norm_g):
    import concourse.bacc as bacc
    from concourse.bass_utils import run_bass_kernel_spmd

    table, query_decay = shape_tables()
    arrays = {
        "x": np.asarray(x)[0],
        "p": np.asarray(p)[0, 0],
        "positions": np.asarray(positions).reshape(T, P).T,
        "w_in": np.asarray(w_in)[0], "w_uq": np.asarray(w_uq)[0], "w_ukv": np.asarray(w_ukv)[0],
        "w_o": np.asarray(w_o)[0], "w_ffn_gate": np.asarray(w_ffn_gate)[0],
        "w_ffn_up": np.asarray(w_ffn_up)[0], "w_ffn_down": np.asarray(w_ffn_down)[0],
        "w_ple_gate": np.asarray(w_ple_gate)[0], "w_ple_proj": np.asarray(w_ple_proj)[0],
        "mix_norm_g": np.asarray(mix_norm_g)[0], "q_norm_g": np.asarray(q_norm_g)[0],
        "kv_norm_g": np.asarray(kv_norm_g)[0], "ffn_norm_g": np.asarray(ffn_norm_g)[0],
        "ple_norm_g": np.asarray(ple_norm_g)[0], "final_norm_g": np.asarray(final_norm_g),
        "table": table, "query_decay": query_decay,
    }
    nc = bacc.Bacc("TRN2", target_bir_lowering=False, num_devices=1, dynamic_dma_scratch_size=1024)
    maps, t_in = {}, {}
    for name, a in arrays.items():
        a = np.ascontiguousarray(a)
        maps["in_" + name] = a
        t_in[name] = nc.dram_tensor("in_" + name, a.shape, mybir.dt.from_np(a.dtype), kind="ExternalInput").ap()
    out = nc.dram_tensor("out_rows", (S, D), F32, kind="ExternalOutput").ap()
    build(nc, t_in, out)
    r = run_bass_kernel_spmd(nc, [maps], core_ids=[0])
    return r.results[0]["out_rows"].reshape(1, S, D)
```

```python
from contextlib import ExitStack

import numpy as np

import concourse.bass as bass
from concourse import mybir

F32 = mybir.dt.float32
F32R = mybir.dt.float32r
I32 = mybir.dt.int32
ALU = mybir.AluOpType
ACT = mybir.ActivationFunctionType
AXX = mybir.AxisListType.X

P = 128
S = 1024
D = 1024
T = S // P
K = D // P
CHUNK = 64
HEADS = 4
HD = 128
ROPE = 64
QL, KVL = 256, 128
MLA_IN = QL + KVL + ROPE
QK = HD + ROPE
FF = 2816
GROUP = 2
NG = FF // P // GROUP
PLE = 256
HALF = 512
EPS, GN_EPS = 1e-6, 1e-5
SCALE = float(QK) ** -0.5
MASKED = -3.0e38
TWO_PI = 2.0 * np.pi
PI_A = 6.28125
PI_B = float(np.float32(np.floor((TWO_PI - PI_A) * 2.0 ** 18) / 2.0 ** 18))
PI_C = float(TWO_PI - PI_A - PI_B)
ROUND = 1.5 * 2.0 ** 23

C_IDENT, C_INV, C_DEC = 0, P, P + 64
C_KDEC = C_DEC + HEADS * P
C_CDEC = C_KDEC + HEADS
C_END = C_CDEC + HEADS


def shape_tables():
    table = np.zeros((P, C_END), np.float32)
    table[:, C_IDENT:C_IDENT + P] = np.eye(P)
    half = HD // 2
    scaled = np.float32(-np.log(10000.0)) * np.arange(half, dtype=np.float32) / np.float32(half)
    table[:, C_INV:C_INV + half] = np.exp(scaled)
    log_g = np.log1p(-np.exp2(-5.0 - np.arange(HEADS)))
    i = np.arange(P)
    query_decay = np.zeros((P, HEADS * P), np.float32)
    for h in range(HEADS):
        seen = (i[:, None] // CHUNK) <= (i[None, :] // CHUNK)
        decay = np.exp(log_g[h] * np.abs(i[:, None] - i[None, :])) * seen * HD ** -0.5
        table[:, C_DEC + h * P:C_DEC + (h + 1) * P] = decay
        table[:, C_KDEC + h] = np.exp(log_g[h] * (P - 1.0 - i)) * HD ** -0.5
        table[:, C_CDEC + h] = np.exp(log_g[h] * P)
        query_decay[:, h * P:(h + 1) * P] = np.exp(log_g[h] * (i + 1.0))[None, :]
    return table, query_decay


def build(nc, t_in, out):
    ctx = ExitStack()
    with ctx:
        def sb(name, shape, dt=F32):
            return ctx.enter_context(nc.sbuf_tensor(name, shape, dt))

        def sem(name):
            return ctx.enter_context(nc.semaphore(name))

        X = sb("X", [P, T * D])
        HTH = sb("HTH", [P, K, S], F32R)
        HTL = sb("HTL", [P, K, S], F32R)
        WF = sb("WF", [P, 20480], F32R)
        RAW = sb("RAW", [P, 4096])
        TMP = sb("TMP", [P, 4096])
        TAB = sb("TAB", [P, 2, T, 64])
        CST = sb("CST", [P, C_END])
        GB = sb("GB", [P, D])
        GC = sb("GC", [P, QL + KVL])
        POS = sb("POS", [P, T], I32)
        POSF = sb("POSF", [P, T])
        NEGH = sb("NEGH", [P, 16])
        PIH = sb("PIH", [P, 1])
        GNE = sb("GNE", [P, 1])
        ST = sb("ST", [P, 128])
        PS = ctx.enter_context(nc.psum_tensor("PS", [P, 8, HALF], F32))

        ident = CST[:, C_IDENT:C_IDENT + P]
        X3 = X[:, :].rearrange("p (t n) -> p t n", t=T)
        COS, SIN = TAB[:, 0], TAB[:, 1]
        JUNK = TAB[:, :, :, :].rearrange("p a t n -> p (a t n)")
        RET = X[:, 0:T * HALF].rearrange("p (t n) -> p t n", t=T)
        CKV = X[:, T * HALF:2 * T * HALF].rearrange("p (t n) -> p t n", t=T)
        VALL = CKV
        QDEC = GB[:, HALF:2 * HALF]

        def tmp(a, n):
            return TMP[:, a:a + n]

        def bank(b, n=HALF):
            return PS[:, b, 0:n]

        class Norm:
            def __init__(self, name):
                self.squares = sem(name + "_squares")
                self.mean = sem(name + "_mean")
                self.rstd = sem(name + "_rstd")
                self.normed = sem(name + "_normed")
                self.turned = sem(name + "_turned")
                self.hi = sem(name + "_hi")
                self.lo = sem(name + "_lo")

        n_mix, n_ffn, n_ple, n_out = Norm("mix"), Norm("ffn"), Norm("ple"), Norm("final")
        s_decay = sem("s_decay")
        s_att = sem("s_att")
        s_ident, s_const, s_gain = sem("s_ident"), sem("s_const"), sem("s_gain")
        s_x = [sem(f"s_x{i}") for i in range(4)]
        s_raw = [sem(f"s_raw{i}") for i in range(4)]
        s_rawb = [sem(f"s_rawb{i}") for i in range(4)]
        w_hi, w_lo = sem("w_hi"), sem("w_lo")
        s_setup, s_tab, s_sin = sem("s_setup"), sem("s_tab"), sem("s_sin")
        lat_done, ckv_out = sem("lat_done"), sem("ckv_out")
        lat_mean, lat_rstd, lat_rows, lat_rope = sem("lat_mean"), sem("lat_rstd"), sem("lat_rows"), sem("lat_rope")

        def big(slot, part, k, n=HALF):
            a = slot * 8192 + part * 4096 + k * HALF
            return WF[:, a:a + n]

        def raw(m):
            return RAW[:, (m % 4) * 1024:(m % 4) * 1024 + 1024]

        M_LAT, M_RET, M_WO0, M_WO1, M_FFN = 0, 4, 20, 24, 28
        M_PLE = M_FFN + NG * 6

        def arrived(eng, m, more=0):
            eng.wait_ge(s_raw[m % 4], 16 * (m // 4 + 1) + more)

        def split_hi(e, m, dst, src, more=0):
            arrived(e, m, more * 4)
            nc.scalar.copy(dst, src).then_inc(w_hi, 1)

        def split_lo(e, m, dst, hi, src, more=0):
            e.wait_ge(w_hi, m + 1 + more)
            nc.vector.tensor_tensor(dst, src, hi.bitcast(F32), ALU.subtract).then_inc(w_lo, 1)

        def granule_hi(e, g, c, m, n=HALF, more=0):
            a = g * 8192 + c * 1024
            src, dst = raw(m), WF[:, a:a + 1024]
            if n < HALF:
                src = src[:, 0:2 * n].rearrange("p (k n) -> p k n", k=2)
                dst = dst.rearrange("p (k n) -> p k n", k=2)[:, :, 0:n]
            split_hi(e, m, dst, src, more)

        def granule_lo(e, g, c, m, n=HALF, more=0):
            a = g * 8192 + c * 1024
            src, hi, dst = raw(m), WF[:, a:a + 1024], WF[:, a + 4096:a + 5120]
            if n < HALF:
                src = src[:, 0:2 * n].rearrange("p (k n) -> p k n", k=2)
                hi = hi.rearrange("p (k n) -> p k n", k=2)[:, :, 0:n]
                dst = dst.rearrange("p (k n) -> p k n", k=2)[:, :, 0:n]
            split_lo(e, m, dst, hi, src, more)

        def product(dst, tile, slot, n=HALF, before=None):
            tok = slice(tile * P, tile * P + P)
            for k in range(K):
                if before:
                    before(k)
                w_h, w_l = big(slot, 0, k, n), big(slot, 1, k, n)
                nc.tensor.matmul(dst, HTH[:, k, tok], w_h, start=(k == 0), stop=False)
                nc.tensor.matmul(dst, HTH[:, k, tok], w_l, start=False, stop=False)
                last = nc.tensor.matmul(dst, HTL[:, k, tok], w_h, start=False, stop=(k == K - 1))
            return last

        def norm_squares(e, s, t, col, src, junk):
            nc.scalar.activation(junk, src, ACT.Square, accum_out=ST[:, col + t:col + t + 1]).then_inc(s.squares, 1)

        def norm_rstd(e, s, t, col):
            e.wait_ge(s.squares, t + 1)
            c = ST[:, col + t:col + t + 1]
            r = ST[:, col + 8 + t:col + 9 + t]
            nc.gpsimd.tensor_scalar(c, c, 1.0 / D, EPS, ALU.mult, ALU.add).then_inc(s.mean, 1)
            e.wait_ge(s.mean, t + 1)
            nc.gpsimd.tensor_tensor(r, c, NEGH[:, 0:1], ALU.pow).then_inc(s.rstd, 1)

        def norm_rows(e, s, t, col, src, dst):
            e.wait_ge(s.rstd, t + 1)
            r = ST[:, col + 8 + t:col + 9 + t]
            nc.vector.scalar_tensor_tensor(dst, src, r, GB[:, :], ALU.mult, ALU.mult).then_inc(s.normed, 1)

        def norm_turn(e, s, t):
            e.wait_ge(s.normed, t + 1)
            if t >= 2:
                e.wait_ge(s.lo, 2 * t - 2)
            b = 2 * (t % 2)
            for k in range(K):
                last = nc.tensor.transpose(PS[:, b + k // 4, (k % 4) * P:(k % 4) * P + P],
                                           tmp(2048 + (t % 2) * 1024 + k * P, P), ident)
            last.then_inc(s.turned, 1)

        def turned_hi(e, s, t):
            e.wait_ge(s.turned, t + 1)
            for j in range(2):
                src = bank(2 * (t % 2) + j).rearrange("p (k n) -> p k n", k=4)
                nc.scalar.copy(HTH[:, 4 * j:4 * j + 4, t * P:t * P + P], src).then_inc(s.hi, 1)

        def turned_lo(e, s, t):
            for j in range(2):
                e.wait_ge(s.hi, 2 * t + j + 1)
                src = bank(2 * (t % 2) + j).rearrange("p (k n) -> p k n", k=4)
                d = slice(t * P, t * P + P)
                nc.vector.tensor_tensor(HTL[:, 4 * j:4 * j + 4, d], src,
                                        HTH[:, 4 * j:4 * j + 4, d].bitcast(F32), ALU.subtract).then_inc(s.lo, 1)

        def sp_1(e):
            e.dma_start(X3[:, 0, :], t_in["x"][0:P, :]).then_inc(s_x[0], 16)
            e.dma_start(ident, t_in["table"][:, C_IDENT:C_IDENT + P]).then_inc(s_ident, 16)
            e.dma_start(GB[:, :], t_in["mix_norm_g"].partition_broadcast(P)).then_inc(s_gain, 16)
            w = t_in["w_in"].rearrange("(k p) n -> p k n", p=P)
            for m in range(4):
                e.dma_start(raw(m)[:, 0:2 * MLA_IN].rearrange("p (k n) -> p k n", k=2),
                            w[:, 2 * m:2 * m + 2, 4 * HALF:4 * HALF + MLA_IN]).then_inc(s_raw[m % 4], 16)
            for t in range(1, 4):
                e.dma_start(X3[:, t, :], t_in["x"][t * P:(t + 1) * P, :]).then_inc(s_x[t], 16)
            e.dma_start(CST[:, C_INV:C_END], t_in["table"][:, C_INV:C_END]).then_inc(s_const, 16)
            e.dma_start(POS[:, :], t_in["positions"]).then_inc(s_const, 16)
            e.dma_start(GC[:, 0:QL], t_in["q_norm_g"].partition_broadcast(P)).then_inc(s_const, 16)
            e.dma_start(GC[:, QL:QL + KVL], t_in["kv_norm_g"].partition_broadcast(P)).then_inc(s_const, 16)
            for t in range(4, T):
                e.wait_ge(n_mix.normed, t - 3)
                e.dma_start(X3[:, t % 4, :], t_in["x"][t * P:(t + 1) * P, :]).then_inc(s_x[t % 4], 16)

        def pool_setup(e):
            nc.gpsimd.memset(NEGH[:, :], -0.5).then_inc(s_setup, 1)
            nc.gpsimd.memset(PIH[:, :], float(np.pi / 2)).then_inc(s_setup, 1)
            nc.gpsimd.memset(GNE[:, :], GN_EPS).then_inc(s_setup, 1)
            e.wait_ge(s_setup, 3)

        def pool_1(e):
            pool_setup(e)

            def latent_rstd(t):
                e.wait_ge(ckv_out, 3 * t + 2)
                q, kv = ST[:, 16 + 2 * t:17 + 2 * t], ST[:, 17 + 2 * t:18 + 2 * t]
                nc.gpsimd.tensor_scalar(q, q, 1.0 / QL, EPS, ALU.mult, ALU.add).then_inc(lat_mean, 1)
                nc.gpsimd.tensor_scalar(kv, kv, 1.0 / KVL, EPS, ALU.mult, ALU.add).then_inc(lat_mean, 1)
                e.wait_ge(lat_mean, 2 * t + 2)
                nc.gpsimd.tensor_tensor(ST[:, 32 + 2 * t:34 + 2 * t], ST[:, 16 + 2 * t:18 + 2 * t], NEGH[:, 0:2],
                                        ALU.pow).then_inc(lat_rstd, 1)
            norm_rstd(e, n_mix, 0, 0)
            norm_rstd(e, n_mix, 1, 0)
            for t in range(T):
                if t + 2 < T:
                    norm_rstd(e, n_mix, t + 2, 0)
                if t >= 1:
                    latent_rstd(t - 1)
            latent_rstd(T - 1)

        def act_1(e):
            def squares(t):
                e.wait_ge(s_x[t % 4], 16 * (t // 4 + 1))
                if t:
                    e.wait_ge(n_mix.squares, t)
                norm_squares(e, n_mix, t, 0, X3[:, t % 4, :], tmp(0, 1024))
            squares(0)
            for c in range(4):
                granule_hi(e, 0, c, c, MLA_IN)
            squares(1)
            for t in range(T):
                turned_hi(e, n_mix, t)
                if t + 2 < T:
                    squares(t + 2)
                if t >= 1:
                    latent_out(e, t - 1)
                if t >= 4:
                    e.wait_ge(s_rawb[t - 4], 16)
                    granule_hi(e, 1, t - 4, M_RET + t - 4)
                if t == 3:
                    tables_act(e)
            e.wait_ge(n_mix.normed, T)
            e.dma_start(QDEC, t_in["query_decay"]).then_inc(s_decay, 16)
            latent_out(e, T - 1)

        def latent_out(e, t):
            e.wait_ge(lat_done, t + 1)
            b = PS[:, 4 + t % 2]
            if t:
                e.wait_ge(ckv_out, 3 * t)
            nc.scalar.activation(SINK_Q, b[:, 0:QL], ACT.Square, accum_out=ST[:, 16 + 2 * t:17 + 2 * t]).then_inc(ckv_out, 1)
            nc.scalar.activation(SINK_KV, b[:, QL:QL + KVL], ACT.Square, accum_out=ST[:, 17 + 2 * t:18 + 2 * t]).then_inc(ckv_out, 1)
            nc.scalar.copy(CKV[:, t, 0:MLA_IN], b[:, 0:MLA_IN]).then_inc(ckv_out, 1)

        SINK_Q, SINK_KV = tmp(1024, QL), tmp(1280, KVL)

        def tables_dve(e):
            n = [0]
            ang = COS
            turns = tmp(1536, 512).rearrange("p (t n) -> p t n", t=T)

            def link(i):
                n[0] += 1
                i.then_inc(s_tab, 1)
                e.wait_ge(s_tab, n[0])

            e.wait_ge(s_const, 16 * 4)
            e.wait_ge(s_setup, 2)
            link(nc.vector.tensor_copy(POSF[:, :], POS[:, :]))
            link(nc.vector.tensor_tensor(ang, POSF[:, :].unsqueeze(2).to_broadcast([P, T, 64]),
                                         CST[:, C_INV:C_INV + 64].unsqueeze(1).to_broadcast([P, T, 64]), ALU.mult))
            link(nc.vector.tensor_scalar(turns, ang, 1.0 / TWO_PI, ROUND, ALU.mult, ALU.add))
            link(nc.vector.tensor_scalar(turns, turns, ROUND, None, ALU.subtract))
            for part in (PI_A, PI_B, PI_C):
                link(nc.vector.scalar_tensor_tensor(ang, turns, -part, ang, ALU.mult, ALU.add))
            link(nc.vector.tensor_scalar(ang, ang, 3.1415925, -3.1415925, ALU.min, ALU.max))
            link(nc.vector.scalar_tensor_tensor(turns, ang, -1.0, ang, ALU.mult, ALU.max))

        N_TAB = 9

        def tables_act(e):
            e.wait_ge(s_tab, N_TAB)
            turns = tmp(1536, 512).rearrange("p (t n) -> p t n", t=T)
            nc.scalar.activation(SIN, COS, ACT.Sin).then_inc(s_sin, 1)
            e.wait_ge(s_sin, 1)
            nc.scalar.activation(COS, turns, ACT.Sin, bias=PIH[:, 0:1], scale=-1.0).then_inc(s_sin, 1)

        def dve_1(e):
            def rows(t):
                if t == 0:
                    e.wait_ge(s_gain, 16)
                if t >= 2:
                    e.wait_ge(n_mix.turned, t - 1)
                norm_rows(e, n_mix, t, 0, X3[:, t % 4, :], tmp(2048 + (t % 2) * 1024, 1024))
            rows(0)
            for c in range(4):
                granule_lo(e, 0, c, c, MLA_IN)
            rows(1)
            for t in range(T):
                turned_lo(e, n_mix, t)
                if t + 2 < T:
                    rows(t + 2)
                if t >= 4:
                    granule_lo(e, 1, t - 4, M_RET + t - 4)
                if t == 2:
                    tables_dve(e)
                if t >= 3:
                    latent_rows(e, t - 3)
            for t in range(T - 3, T):
                latent_rows(e, t)
            e.wait_ge(s_sin, 2)
            e.wait_ge(n_mix.turned, T)
            z = CKV[:, :, QL + KVL:MLA_IN].rearrange("p t (h n) -> p t h n", h=2)
            a4, b4 = (tmp(c, 512).rearrange("p (t h n) -> p t h n", t=T, h=2) for c in (3072, 3584))
            for x, table in ((a4, COS), (b4, SIN)):
                w = table[:, :, 0:64:2].unsqueeze(2).to_broadcast([P, T, 2, 32])
                nc.vector.tensor_tensor(x, z, w, ALU.mult).then_inc(lat_rope, 1)
            e.wait_ge(lat_rope, 2)
            nc.vector.tensor_tensor(z[:, :, 0], a4[:, :, 0], b4[:, :, 1], ALU.subtract).then_inc(lat_rope, 1)
            nc.vector.tensor_tensor(z[:, :, 1], a4[:, :, 1], b4[:, :, 0], ALU.add).then_inc(lat_rope, 1)
            e.wait_ge(lat_rope, 4)
            nc.vector.tensor_copy(CKV[:, :, MLA_IN:HALF], CKV[:, :, QL + KVL:MLA_IN]).then_inc(lat_rope, 1)

        def latent_rows(e, t):
            e.wait_ge(lat_rstd, t + 1)
            e.wait_ge(ckv_out, 3 * t + 3)
            for n, (a, b) in enumerate(((0, QL), (QL, QL + KVL))):
                c = CKV[:, t, a:b]
                nc.vector.scalar_tensor_tensor(c, c, ST[:, 32 + 2 * t + n:33 + 2 * t + n], GC[:, a:b],
                                               ALU.mult, ALU.mult).then_inc(lat_rows, 1)

        def pe_1(e):
            e.wait_ge(s_ident, 16)
            norm_turn(e, n_mix, 0)
            for t in range(T):
                if t + 1 < T:
                    norm_turn(e, n_mix, t + 1)
                e.wait_ge(n_mix.lo, 2 * t + 2)
                if t >= 2:
                    e.wait_ge(ckv_out, 3 * (t - 1))
                product(bank(4 + t % 2, MLA_IN), t, 0, MLA_IN,
                        (lambda k: e.wait_ge(w_lo, k // 2 + 1)) if t == 0 else None).then_inc(lat_done, 1)

        z_proj, z_out = sem("z_proj"), sem("z_out")
        rot_ab, rot = sem("rot_ab"), sem("rot")
        qk_turned, qk_out, qd_out = sem("qk_turned"), sem("qk_out"), sem("qd_out")
        r_scores, r_probs, r_okv = sem("r_scores"), sem("r_probs"), sem("r_okv")
        r_state = sem("r_state")
        gn_stats, gn_mean, gn_rstd, gn_rows, r_done = (sem("gn_stats"), sem("gn_mean"), sem("gn_rstd"),
                                                       sem("gn_rows"), sem("r_done"))
        UNITS = 16

        def Z(u):
            return tmp((u % 4) * 512, 512)

        AB = tmp(2048, 512)
        PT2 = [tmp(2560, 128), tmp(2688, 128)]
        ON = [tmp(2816, 128), tmp(2944, 128)]
        QKT = [tmp(3072, 256), tmp(3328, 256)]
        QDT = [tmp(3584, 128), tmp(3712, 128)]
        STATE = tmp(3840, 128)
        KD = [GB[:, c * P:c * P + P] for c in range(4)]
        B_T, B_S, B_KV = 0, 1, 3
        B_O = (2, 6)

        def sp_retention(e):
            w = t_in["w_in"][:, 0:4 * HALF].rearrange("(k p) (s c) -> p k s c", p=P, s=4)
            with e.Fori(0, HEADS) as h:
                for c in range(4):
                    e.wait_ge(w_lo, M_RET + c - 3 + 4 * h)
                    for k in range(2):
                        e.dma_start(RAW[:, c * 1024 + k * HALF:c * 1024 + (k + 1) * HALF].rearrange("p (s c) -> p s c", s=4),
                                    w[:, 2 * c + k, :, bass.ds(h * HD, HD)]).then_inc((s_rawb if k else s_raw)[c], 16)

        def sp_out_weights(e, half, m0):
            w = t_in["w_o"].rearrange("(k p) n -> p k n", p=P)
            for c in range(4):
                e.wait_ge(w_lo, m0 + c - 3)
                for k in range(2):
                    e.dma_start(raw(m0 + c)[:, k * HALF:(k + 1) * HALF],
                                w[:, 2 * c + k, half * HALF:(half + 1) * HALF]).then_inc((s_rawb if k else s_raw)[c], 16)

        def pe_2(e):
            e.wait_ge(ckv_out, 3 * T)
            with e.Fori(0, HEADS * T // UNITS) as i:
                B = i * UNITS
                for s in range(UNITS + 3):
                    if s < UNITS:
                        if s % T == 0:
                            e.wait_ge(w_lo, M_RET + 4 * (s // T + 1) + i * 8)
                        e.wait_ge(z_out, B * 2 + 2 * max(0, s - 1))
                        product(bank(4 + s % 2), s % T, 1 - s // T).then_inc(z_proj, 1)
                    u = s - 1
                    if 0 <= u < UNITS:
                        e.wait_ge(rot, B * 3 + 3 * u + 2)
                        e.wait_ge(qk_out, B + u)
                        nc.tensor.transpose(PS[:, B_T, 0:P], Z(u)[:, 0:P], ident)
                        nc.tensor.transpose(PS[:, B_T, P:2 * P], Z(u)[:, P:2 * P], ident).then_inc(qk_turned, 1)
                    u = s - 2
                    if 0 <= u < UNITS:
                        e.wait_ge(qk_out, B + u + 1)
                        e.wait_ge(r_probs, B + u)
                        nc.tensor.matmul(bank(B_S, P), QKT[u % 2][:, P:2 * P], QKT[u % 2][:, 0:P],
                                         start=True, stop=True).then_inc(r_scores, 1)
                    u = s - 3
                    if 0 <= u < UNITS:
                        e.wait_ge(r_probs, B + u + 1)
                        e.wait_ge(qd_out, B + u + 1)
                        e.wait_ge(rot, B * 3 + 3 * u + 3)
                        e.wait_ge(r_state, B + u)
                        e.wait_ge(gn_rows, B + max(0, u - 1))
                        V = Z(u)[:, 2 * P:3 * P]
                        nc.tensor.matmul(bank(B_O[u % 2], P), PT2[u % 2], V, start=True, stop=(u % T == 0))
                        if u % T:
                            nc.tensor.matmul(bank(B_O[u % 2], P), QDT[u % 2], STATE, start=False, stop=True)
                        nc.tensor.matmul(bank(B_KV, P), KD[u % 4], V, start=True, stop=True).then_inc(r_okv, 1)

        def act_2(e):
            with e.Fori(0, HEADS * T // UNITS) as i:
                B = i * UNITS
                for s in range(UNITS + 3):
                    if s < UNITS:
                        e.wait_ge(z_proj, B + s + 1)
                        e.wait_ge(r_done, B + max(0, s - 3))
                        e.wait_ge(r_okv, B + max(0, s - 3))
                        b = PS[:, 4 + s % 2]
                        nc.scalar.copy(Z(s)[:, 0:3 * P], b[:, 0:3 * P]).then_inc(z_out, 1)
                        nc.scalar.activation(Z(s)[:, 3 * P:4 * P], b[:, 3 * P:4 * P], ACT.Silu).then_inc(z_out, 1)
                    u = s - 1
                    if 0 <= u < UNITS:
                        e.wait_ge(qk_turned, B + u + 1)
                        e.wait_ge(r_scores, B + max(0, u - 1))
                        e.wait_ge(qd_out, B + max(0, u - 1))
                        nc.scalar.copy(QKT[u % 2], bank(B_T, 2 * P)).then_inc(qk_out, 1)
                    if s < UNITS and s % 2 == 0:
                        hh, c = s // T, s % T // 2
                        e.wait_ge(z_proj, B + hh * T)
                        piece_m = M_RET + 4 + 4 * hh + c
                        e.wait_ge(s_raw[c], 16 * (piece_m // 4 + 1) + i * 32)
                        e.wait_ge(s_rawb[c], 16 * (hh + 2) + i * 32)
                        a = hh * 8192 + c * 1024
                        nc.scalar.copy(WF[:, a:a + 1024], RAW[:, c * 1024:(c + 1) * 1024]).then_inc(w_hi, 1)

        def pool_2(e):
            e.wait_ge(s_const, 16 * 4)
            with e.Fori(0, HEADS * T // UNITS) as i:
                B = i * UNITS
                for s in range(UNITS + 3):
                    if s < UNITS:
                        z = Z(s)[:, 0:2 * P].rearrange("p (q h n) -> p q h n", q=2, h=2)
                        ab = AB.rearrange("p (x q h n) -> p x q h n", x=2, q=2, h=2)
                        e.wait_ge(rot_ab, B * 2 + 2 * s + 2)
                        nc.gpsimd.tensor_tensor(z[:, :, 0], ab[:, 0, :, 0], ab[:, 1, :, 1], ALU.subtract).then_inc(rot, 1)
                        nc.gpsimd.tensor_tensor(z[:, :, 1], ab[:, 0, :, 1], ab[:, 1, :, 0], ALU.add).then_inc(rot, 1)
                        e.wait_ge(rot, B * 3 + 3 * s + 2)
                        e.wait_ge(r_okv, B + max(0, s - 3))
                        dec = HDEC[s // T]
                        nc.gpsimd.tensor_tensor(KD[s % 4], Z(s)[:, P:2 * P], dec.to_broadcast([P, P]),
                                                ALU.mult).then_inc(rot, 1)
                    u = s - 3
                    if 0 <= u < UNITS:
                        e.wait_ge(gn_stats, B * 2 + 2 * u + 2)
                        var, r = ST[:, 65:66], ST[:, 66:67]
                        nc.gpsimd.tensor_tensor(r, var, GNE[:, 0:1], ALU.add).then_inc(gn_mean, 1)
                        e.wait_ge(gn_mean, B + u + 1)
                        nc.gpsimd.tensor_tensor(r, r, NEGH[:, 0:1], ALU.pow).then_inc(gn_rstd, 1)
                        e.wait_ge(gn_rows, B + u + 1)
                        hcol = i * 2 * HD + (u // T) * HD
                        nc.gpsimd.tensor_tensor(RET[:, u % T, bass.ds(hcol, HD)], ON[u % 2],
                                                Z(u)[:, 3 * P:4 * P], ALU.mult).then_inc(r_done, 1)

        HCON = sb("HCON", [P, 2 * 2])
        HDEC = [HCON[:, 0:1], HCON[:, 1:2]]
        HCD = [HCON[:, 2:3], HCON[:, 3:4]]
        s_hcon = sem("s_hcon")

        def dve_2(e):
            with e.Fori(0, HEADS * T // UNITS) as i:
                B = i * UNITS
                e.wait_ge(rot, B * 3)
                e.wait_ge(r_state, B)
                nc.vector.tensor_copy(HCON[:, 0:2], CST[:, bass.ds(i * 2 + C_KDEC, 2)]).then_inc(s_hcon, 1)
                nc.vector.tensor_copy(HCON[:, 2:4], CST[:, bass.ds(i * 2 + C_CDEC, 2)]).then_inc(s_hcon, 1)
                e.wait_ge(s_hcon, i * 2 + 2)
                for s in range(UNITS + 3):
                    if s < UNITS:
                        z = Z(s)[:, 0:2 * P].rearrange("p (g n) -> p g n", g=4)
                        ab = AB.rearrange("p (x g n) -> p x g n", x=2, g=4)
                        if s == 0:
                            e.wait_ge(s_sin, 2)
                            e.wait_ge(s_decay, 16)
                        e.wait_ge(z_out, B * 2 + 2 * s + 2)
                        e.wait_ge(rot, B * 3 + (3 * s - 1 if s else 0))
                        for x, table in enumerate((COS, SIN)):
                            w = table[:, s % T].unsqueeze(1).to_broadcast([P, 4, 64])
                            nc.vector.tensor_tensor(ab[:, x], z, w, ALU.mult).then_inc(rot_ab, 1)
                    u = s - 1
                    if 0 <= u < UNITS:
                        e.wait_ge(qk_out, B + u + 1)
                        e.wait_ge(r_okv, B + max(0, u - 1))
                        col = i * 2 * P + (u // T) * P
                        nc.vector.tensor_tensor(QDT[u % 2], QKT[u % 2][:, 0:P], QDEC[:, bass.ds(col, P)],
                                                ALU.mult).then_inc(qd_out, 1)
                    u = s - 2
                    if 0 <= u < UNITS:
                        e.wait_ge(r_scores, B + u + 1)
                        e.wait_ge(r_okv, B + max(0, u - 1))
                        col = i * 2 * P + ((u // T) * P + C_DEC)
                        nc.vector.tensor_tensor(PT2[u % 2], bank(B_S, P), CST[:, bass.ds(col, P)],
                                                ALU.mult).then_inc(r_probs, 1)
                    u = s - 3
                    if 0 <= u < UNITS:
                        e.wait_ge(r_okv, B + u + 1)
                        nc.vector.bn_stats(ST[:, 68:74], bank(B_O[u % 2], P)).then_inc(gn_stats, 1)
                        e.wait_ge(r_state, B + u)
                        e.wait_ge(gn_stats, B * 2 + 2 * u + 1)
                        if u % T:
                            nc.vector.scalar_tensor_tensor(STATE, STATE, HCD[u // T], bank(B_KV, P),
                                                           ALU.mult, ALU.add).then_inc(r_state, 1)
                        else:
                            nc.vector.tensor_copy(STATE, bank(B_KV, P)).then_inc(r_state, 1)
                        nc.vector.bn_aggr(ST[:, 64:66], ST[:, 68:74]).then_inc(gn_stats, 1)
                        e.wait_ge(gn_rstd, B + u + 1)
                        e.wait_ge(r_done, B + max(0, u - 1))
                        nc.vector.tensor_scalar(ON[u % 2], bank(B_O[u % 2], P), ST[:, 64:65], ST[:, 66:67],
                                                ALU.subtract, ALU.mult).then_inc(gn_rows, 1)
                    if s < UNITS and s % 2 == 0:
                        hh, c = s // T, s % T // 2
                        e.wait_ge(z_proj, B + hh * T)
                        e.wait_ge(w_hi, M_RET + 4 + 4 * hh + c + 1 + i * 8)
                        a = hh * 8192 + c * 1024
                        nc.vector.tensor_tensor(WF[:, a + 4096:a + 5120], RAW[:, c * 1024:(c + 1) * 1024],
                                                WF[:, a:a + 1024].bitcast(F32), ALU.subtract).then_inc(w_lo, 1)

        lat_turned, lat_hi, lat_lo = sem("lat_turned"), sem("lat_hi"), sem("lat_lo")
        b_w, b_w_lo, b_v, b_v_out = sem("b_w"), sem("b_w_lo"), sem("b_v"), sem("b_v_out")
        b_q, b_ab, b_rot, b_qs, b_turn, b_qr = (sem("b_q"), sem("b_ab"), sem("b_rot"), sem("b_qs"),
                                                sem("b_turn"), sem("b_qr"))
        a_w, a_w_lo = sem("a_w"), sem("a_w_lo")
        a_proj, a_hi, a_lo, a_qr = sem("a_proj"), sem("a_hi"), sem("a_lo"), sem("a_qr")
        a_scores, a_mask, a_max, a_bias = sem("a_scores"), sem("a_mask"), sem("a_max"), sem("a_bias")
        a_exp, a_rec, a_prob, a_turn = sem("a_exp"), sem("a_rec"), sem("a_prob"), sem("a_turn")
        a_pt, a_pv, a_o_hi, a_o_lo = sem("a_pt"), sem("a_pv"), sem("a_o_hi"), sem("a_o_lo")
        a_vh = sem("a_vh")
        rt_turned, rt_hi, rt_lo = sem("rt_turned"), sem("rt_hi"), sem("rt_lo")
        NR = HEADS * T

        CT = [WF[:, 0:4096].rearrange("p (k n) -> p k n", k=4), WF[:, 4096:8192].rearrange("p (k n) -> p k n", k=4)]
        WS = 16384
        WQ = [WF[:, WS + p * 384:WS + p * 384 + 256].rearrange("p (k n) -> p k n", k=2) for p in range(2)]
        WK = [WF[:, WS + p * 384 + 256:WS + p * 384 + 384] for p in range(2)]
        QR = WF[:, WS + 768:WS + 1792]
        WR = [WF[:, WS + 1792 + p * 1024:WS + 2304 + p * 1024].rearrange("p (k n) -> p k n", k=2) for p in range(2)]
        WV = [WF[:, WS + 2304 + p * 1024:WS + 2816 + p * 1024] for p in range(2)]
        QRA = HTH[:, 0:4]
        KT = [HTL[:, 0], HTL[:, 1]]
        QT = [HTL[:, 2], HTL[:, 3]]
        QA, QB, QRF = ([tmp(a, 256), tmp(a + 256, 256)] for a in (0, 512, 1024))
        QS = [tmp(2048, 512), tmp(2560, 512)]
        PT = [tmp(2048, 1024), tmp(3072, 1024)]
        VH = GB[:, :].rearrange("p (t n) -> p t n", t=T)
        RAWQ = RAW[:, 0:2048].rearrange("p (k n) -> p k n", k=2)

        def three(dst, pairs):
            for i, (a, b) in enumerate(pairs):
                for n, (x, y) in enumerate(((0, 0), (0, 1), (1, 0))):
                    last = nc.tensor.matmul(dst, a[x], b[y], start=(i + n == 0), stop=(i == len(pairs) - 1 and n == 2))
            return last

        def sp_3(e):
            e.wait_ge(w_lo, M_WO1)
            for k in range(2):
                e.dma_start(RAW[:, k * 1024:k * 1024 + 768], t_in["w_uq"][k * P:(k + 1) * P, :]).then_inc(s_att, 16)
            for k in range(2):
                e.dma_start(RAW[:, 2560 + k * 512:3072 + k * 512],
                            t_in["w_ukv"][:, k * 512:(k + 1) * 512]).then_inc(s_att, 16)

        def all_heads(width, a, n):
            if width == QK:
                return RAWQ[:, :, 0:HEADS * QK].rearrange("p k (h n) -> p k h n", h=HEADS)[:, :, :, a:a + n]
            return RAW[:, 2560:3584].rearrange("p (h n) -> p h n", h=HEADS)[:, :, a:a + n]

        def act_3a(e):
            e.wait_ge(s_att, 64)
            e.wait_ge(z_proj, NR)
            for k in range(2):
                nc.scalar.copy(WR[0][:, k].rearrange("p (h n) -> p h n", h=HEADS),
                               all_heads(QK, HD, ROPE)[:, k]).then_inc(b_w, 1)
            nc.scalar.copy(WV[0].rearrange("p (h n) -> p h n", h=HEADS), all_heads(2 * HD, HD, HD)).then_inc(b_w, 1)
            head_w_hi(e, 0)
            for t in range(T):
                e.wait_ge(lat_turned, t + 1)
                nc.scalar.copy(CT[0][:, :, t * P:t * P + P],
                               bank(t % 4).rearrange("p (k n) -> p k n", k=4)).then_inc(lat_hi, 1)
            for t in range(T + 2):
                if t < T:
                    e.wait_ge(b_v, t + 1)
                    nc.scalar.copy(VALL[:, t], bank(4 + t % 2)).then_inc(b_v_out, 1)
                if t >= 2:
                    e.wait_ge(b_turn, t - 1)
                    nc.scalar.copy(QRA[:, :, (t - 2) * P:(t - 1) * P],
                                   bank((t - 2) % 4).rearrange("p (h n) -> p h n", h=HEADS)).then_inc(b_qr, 1)

        def dve_3a(e):
            for k in range(2):
                e.wait_ge(b_w, k + 1)
                nc.vector.tensor_tensor(WR[1][:, k].rearrange("p (h n) -> p h n", h=HEADS),
                                        all_heads(QK, HD, ROPE)[:, k],
                                        WR[0][:, k].rearrange("p (h n) -> p h n", h=HEADS).bitcast(F32),
                                        ALU.subtract).then_inc(b_w_lo, 1)
            e.wait_ge(b_w, 3)
            nc.vector.tensor_tensor(WV[1].rearrange("p (h n) -> p h n", h=HEADS), all_heads(2 * HD, HD, HD),
                                    WV[0].rearrange("p (h n) -> p h n", h=HEADS).bitcast(F32),
                                    ALU.subtract).then_inc(b_w_lo, 1)
            head_w_lo(e, 0)
            for t in range(T):
                e.wait_ge(lat_hi, t + 1)
                d = slice(t * P, t * P + P)
                nc.vector.tensor_tensor(CT[1][:, :, d], bank(t % 4).rearrange("p (k n) -> p k n", k=4),
                                        CT[0][:, :, d].bitcast(F32), ALU.subtract).then_inc(lat_lo, 1)

            def split(t):
                e.wait_ge(b_rot, 2 * t + 2)
                if t >= 2:
                    e.wait_ge(b_turn, t - 1)
                src = QRF[t % 2].rearrange("p (h n) -> p h n", h=HEADS)
                qs = QS[t % 2].rearrange("p (h n) -> p h n", h=HEADS)
                nc.vector.tensor_copy(qs[:, :, 0:64].bitcast(F32R), src).then_inc(b_qs, 1)
                e.wait_ge(b_qs, 2 * t + 1)
                nc.vector.tensor_tensor(qs[:, :, 64:128], src, qs[:, :, 0:64], ALU.subtract).then_inc(b_qs, 1)
            e.wait_ge(r_done, NR)
            e.wait_ge(gn_rows, NR)
            for t in range(T):
                e.wait_ge(b_q, t + 1)
                if t >= 2:
                    e.wait_ge(b_rot, 2 * t - 2)
                z = bank(6 + t % 2, 256).rearrange("p (g n) -> p g n", g=2 * HEADS)
                for x, table in ((QA[t % 2], COS), (QB[t % 2], SIN)):
                    w = table[:, t, 0:64:2].unsqueeze(1).to_broadcast([P, 2 * HEADS, 32])
                    nc.vector.tensor_tensor(x.rearrange("p (g n) -> p g n", g=2 * HEADS), z, w,
                                            ALU.mult).then_inc(b_ab, 1)
                if t:
                    split(t - 1)
            split(T - 1)

        def pool_3a(e):
            for t in range(T):
                a, b, q = (x[t % 2].rearrange("p (h i n) -> p h i n", h=HEADS, i=2) for x in (QA, QB, QRF))
                e.wait_ge(b_ab, 2 * t + 2)
                if t >= 2:
                    e.wait_ge(b_qs, 2 * t - 2)
                nc.gpsimd.tensor_tensor(q[:, :, 0], a[:, :, 0], b[:, :, 1], ALU.subtract).then_inc(b_rot, 1)
                nc.gpsimd.tensor_tensor(q[:, :, 1], a[:, :, 1], b[:, :, 0], ALU.add).then_inc(b_rot, 1)

        def pe_3a(e):
            e.wait_ge(gn_rows, NR)
            e.wait_ge(r_state, NR)
            e.wait_ge(lat_rope, 5)
            e.wait_ge(lat_rows, 2 * T)
            for t in range(T):
                if t >= 4:
                    e.wait_ge(lat_lo, t - 3)
                for k in range(4):
                    last = nc.tensor.transpose(PS[:, t % 4, k * P:k * P + P], CKV[:, t, k * P:k * P + P], ident)
                last.then_inc(lat_turned, 1)
            e.wait_ge(b_w_lo, 3)
            e.wait_ge(z_out, 2 * NR)

            def queries(t):
                e.wait_ge(lat_lo, t + 1)
                if t >= 2:
                    e.wait_ge(b_ab, 2 * (t - 1))
                tok = slice(t * P, t * P + P)
                three(bank(6 + t % 2, 256), [([CT[x][:, k, tok] for x in range(2)], [WR[y][:, k] for y in range(2)])
                                             for k in range(2)]).then_inc(b_q, 1)

            def turn(t):
                e.wait_ge(b_qs, 2 * t + 2)
                if t < 4:
                    e.wait_ge(lat_lo, T)
                else:
                    e.wait_ge(b_qr, t - 3)
                for h in range(HEADS):
                    last = nc.tensor.transpose(PS[:, t % 4, h * P:h * P + P], QS[t % 2][:, h * P:h * P + P], ident)
                last.then_inc(b_turn, 1)

            for t in range(T):
                queries(t)
                if t >= 2:
                    e.wait_ge(b_v_out, t - 1)
                tok = slice(t * P, t * P + P)
                three(bank(4 + t % 2), [([CT[x][:, 2, tok] for x in range(2)], WV)]).then_inc(b_v, 1)
                if t >= 2:
                    turn(t - 2)
            turn(T - 2)
            turn(T - 1)

        def head_w_hi(e, h):
            nc.scalar.copy(WQ[0], RAWQ[:, :, bass.ds(h * QK, HD)]).then_inc(a_w, 1)
            nc.scalar.copy(WK[0], RAW[:, bass.ds(h * 2 * HD + 2560, HD)]).then_inc(a_w, 1)

        def head_w_lo(e, h):
            e.wait_ge(a_w, h * 2 + 2)
            nc.vector.tensor_tensor(WQ[1], RAWQ[:, :, bass.ds(h * QK, HD)], WQ[0].bitcast(F32),
                                    ALU.subtract).then_inc(a_w_lo, 1)
            nc.vector.tensor_tensor(WK[1], RAW[:, bass.ds(h * 2 * HD + 2560, HD)], WK[0].bitcast(F32),
                                    ALU.subtract).then_inc(a_w_lo, 1)

        def head_queries(e, h, b):
            if b == 0:
                e.wait_ge(a_w_lo, h * 2 + 2)
            blk = slice(b * HALF, (b + 1) * HALF)
            three(bank(2 + b), [([WQ[x][:, k] for x in range(2)], [CT[y][:, k, blk] for y in range(2)])
                                for k in range(2)]).then_inc(a_proj, 1)

        def head_keys(e, h):
            for b in range(2):
                blk = slice(b * HALF, (b + 1) * HALF)
                three(bank(b), [(WK, [CT[y][:, 2, blk] for y in range(2)])]).then_inc(a_proj, 1)

        PLACES = ((QT, 2), (QT, 3), (KT, 0), (KT, 1))

        def head_hi(e, h, part):
            if part == 1:
                nc.scalar.copy(QR[:, 0:2 * P], rotary(h, slice(0, 2 * P))).then_inc(a_qr, 1)
            for n in (2 * part, 2 * part + 1):
                where, b = PLACES[n]
                e.wait_ge(a_proj, h * 4 + n + 1)
                blk = slice((b % 2) * HALF, (b % 2 + 1) * HALF)
                nc.scalar.copy(where[0][:, blk], bank(b)).then_inc(a_hi, 1)
            if part == 1:
                nc.scalar.copy(QR[:, 2 * P:S], rotary(h, slice(2 * P, S))).then_inc(a_qr, 1)

        def rotary(h, tok):
            return HTH[:, bass.ds(h, 1), tok].rearrange("p a n -> p (a n)")

        def head_lo(e, h):
            for n, (where, b) in enumerate(PLACES):
                e.wait_ge(a_hi, h * 4 + n + 1)
                blk = slice((b % 2) * HALF, (b % 2 + 1) * HALF)
                nc.vector.tensor_tensor(where[1][:, blk], bank(b), where[0][:, blk].bitcast(F32),
                                        ALU.subtract).then_inc(a_lo, 1)

        def seen(t):
            return (1, (t + 1) * P) if t < 4 else (2, (t + 1) * P // 2)

        def score_banks(t):
            nb, n = seen(t)
            b = 2 * ((t + 1) % 2)
            return PS[:, b:b + nb, 0:n]

        def pe_head(e, h, early, after):
            def scores(t):
                if t == 0:
                    e.wait_ge(a_lo, h * 4 + 4)
                if t in (0, 2):
                    e.wait_ge(a_qr, h * 2 + (2 if t else 1))
                if t >= 2:
                    e.wait_ge(a_exp, h * T + t - 1)
                tok = slice(t * P, t * P + P)
                nb, n = seen(t)
                for c in range(nb):
                    blk = slice(c * n, c * n + max(n, 2 * P))
                    dst = bank(2 * ((t + 1) % 2) + c, max(n, 2 * P))
                    for i, (a, b) in enumerate(((QT[0], KT[0]), (QT[0], KT[1]), (QT[1], KT[0]),
                                                (QR, CT[0][:, 3]), (QR, CT[1][:, 3]))):
                        last = nc.tensor.matmul(dst, a[:, tok], b[:, blk], start=(i == 0), stop=(i == 4))
                last.then_inc(a_scores, 1)

            def turn(t):
                e.wait_ge(a_prob, h * T + t + 1)
                e.wait_ge(a_pt, h * T + t)
                for j in range(t + 1):
                    last = nc.tensor.transpose(PS[:, 4 + j // 4, (j % 4) * P:(j % 4) * P + P],
                                               tmp((t % 2) * 1024 + j * P, P), ident)
                last.then_inc(a_turn, 1)

            def values(t):
                e.wait_ge(a_vh, h * 2 + (1 if t < 2 else 2))
                e.wait_ge(a_pt, h * T + t + 1)
                e.wait_ge(a_o_lo, h * T + max(0, t - 1))
                for j in range(t + 1):
                    last = nc.tensor.matmul(bank(6 + t % 2, P), VH[:, j], PT[t % 2][:, j * P:j * P + P], start=(j == 0), stop=(j == t))
                last.then_inc(a_pv, 1)

            scores(0)
            scores(1)
            for t in range(T):
                if t + 2 < T:
                    scores(t + 2)
                else:
                    e.wait_ge(a_exp, h * T + T - 1)
                    early(t + 2 - T)
                if t >= 1:
                    values(t - 1)
                turn(t)
            e.wait_ge(a_exp, h * T + T)
            after()
            values(T - 1)

        def act_head(e, h, early, late, after):
            def exp(t):
                e.wait_ge(a_bias, h * T + t + 1)
                e.wait_ge(a_turn, h * T + max(0, t - 1))
                nb, n = seen(t)
                dst = tmp((t % 2) * 1024, nb * n).rearrange("p (b n) -> p b n", b=nb)
                nc.scalar.activation(dst, score_banks(t), ACT.Exp, bias=ST[:, 76 + t % 2:77 + t % 2],
                                     scale=SCALE, accum_out=ST[:, 78 + t % 2:79 + t % 2]).then_inc(a_exp, 1)

            def out_hi(t):
                e.wait_ge(a_pv, h * T + t + 1)
                nc.scalar.copy(HTH[:, bass.ds(h + 4, 1), t * P:t * P + P],
                               bank(6 + t % 2, P).unsqueeze(1)).then_inc(a_o_hi, 1)

            exp(0)
            for t in range(T):
                if t + 1 < T:
                    exp(t + 1)
                if t >= 1:
                    out_hi(t - 1)
                if t == 3:
                    early()
                if t == T - 1:
                    late()
                e.wait_ge(a_turn, h * T + t + 1)
                e.wait_ge(a_pv, h * T + max(0, t - 1))
                n = (t + 1) * P
                src = PS[:, 4:6, :].rearrange("p b n -> p (b n)")[:, 0:n]
                nc.scalar.copy(PT[t % 2][:, 0:n], src).then_inc(a_pt, 1)
            after()
            out_hi(T - 1)

        def dve_head(e, h, early, after):
            def biggest(t):
                e.wait_ge(a_scores, h * T + t + 1)
                e.wait_ge(a_exp, h * T + max(0, t - 1))
                src = score_banks(t)
                nb, n = seen(t)
                nc.vector.memset(src[0:CHUNK, nb - 1, n - CHUNK:n], MASKED).then_inc(a_mask, 1)
                e.wait_ge(a_mask, h * T + t + 1)
                nc.vector.tensor_reduce(ST[:, 74 + t % 2:75 + t % 2], src, mybir.AxisListType.XY if nb > 1 else AXX,
                                        ALU.max).then_inc(a_max, 1)
                e.wait_ge(a_max, h * T + t + 1)
                nc.vector.tensor_scalar(ST[:, 76 + t % 2:77 + t % 2], ST[:, 74 + t % 2:75 + t % 2], -SCALE, None,
                                        ALU.mult).then_inc(a_bias, 1)

            def out_lo(t):
                e.wait_ge(a_o_hi, h * T + t + 1)
                d = slice(t * P, t * P + P)
                nc.vector.tensor_tensor(HTL[:, bass.ds(h + 4, 1), d], bank(6 + t % 2, P).unsqueeze(1),
                                        HTH[:, bass.ds(h + 4, 1), d].bitcast(F32), ALU.subtract).then_inc(a_o_lo, 1)

            def divide(t):
                e.wait_ge(a_exp, h * T + t + 1)
                n = (t + 1) * P
                nc.vector.reciprocal(ST[:, 80 + t % 2:81 + t % 2], ST[:, 78 + t % 2:79 + t % 2]).then_inc(a_rec, 1)
                e.wait_ge(a_rec, h * T + t + 1)
                p = tmp((t % 2) * 1024, n)
                nc.vector.tensor_scalar(p, p, ST[:, 80 + t % 2:81 + t % 2], None, ALU.mult).then_inc(a_prob, 1)

            biggest(0)
            biggest(1)
            divide(0)
            for t in range(T):
                if t + 2 < T:
                    biggest(t + 2)
                if t + 1 < T:
                    divide(t + 1)
                if t >= 1:
                    out_lo(t - 1)
                if t == 3:
                    early()
            after()
            out_lo(T - 1)

        def pe_3b(e):
            e.wait_ge(b_qr, T)
            head_queries(e, 0, 0)
            head_queries(e, 0, 1)
            head_keys(e, 0)
            with e.Fori(0, HEADS - 1) as h:
                pe_head(e, h, lambda b: head_queries(e, h + 1, b), lambda: head_keys(e, h + 1))
            e.wait_ge(r_done, NR)
            pe_head(e, HEADS - 1, lambda b: pe_retention_turn(e, [b]), lambda: pe_retention_turn(e, range(2, T)))

        def nothing():
            pass

        def act_3b(e):
            head_hi(e, 0, 0)
            head_hi(e, 0, 1)

            def next_weights(h):
                e.wait_ge(a_proj, h * 4 + 4)
                head_w_hi(e, h + 1)

            def next_queries(h):
                e.wait_ge(a_scores, h * T + T)
                head_hi(e, h + 1, 0)
            with e.Fori(0, HEADS - 1) as h:
                act_head(e, h, lambda: next_weights(h), lambda: next_queries(h), lambda: head_hi(e, h + 1, 1))
            act_head(e, HEADS - 1, nothing, nothing, lambda: act_retention_hi(e))

        def dve_3b(e):
            head_lo(e, 0)
            with e.Fori(0, HEADS - 1) as h:
                dve_head(e, h, lambda: head_w_lo(e, h + 1), lambda: head_lo(e, h + 1))
            dve_head(e, HEADS - 1, nothing, lambda: dve_retention_lo(e))

        def pool_3b(e):
            e.wait_ge(b_v_out, T)
            e.wait_ge(r_okv, NR)
            with e.Fori(0, HEADS) as h:
                e.wait_ge(a_pv, h * T)
                for a, b in ((0, 2), (2, T)):
                    nc.gpsimd.tensor_copy(VH[:, a:b], VALL[:, a:b, bass.ds(h * HD, HD)]).then_inc(a_vh, 1)

        def pe_retention_turn(e, tiles):
            for t in tiles:
                if t >= 4:
                    e.wait_ge(rt_lo, t - 3)
                for k in range(4):
                    last = nc.tensor.transpose(PS[:, (t + 2) % 4, k * P:k * P + P], RET[:, t, k * P:k * P + P], ident)
                last.then_inc(rt_turned, 1)

        def act_retention_hi(e):
            for t in range(T):
                e.wait_ge(rt_turned, t + 1)
                nc.scalar.copy(HTH[:, 0:4, t * P:t * P + P],
                               bank((t + 2) % 4).rearrange("p (k n) -> p k n", k=4)).then_inc(rt_hi, 1)

        def dve_retention_lo(e):
            for t in range(T):
                e.wait_ge(rt_hi, t + 1)
                d = slice(t * P, t * P + P)
                nc.vector.tensor_tensor(HTL[:, 0:4, d], bank((t + 2) % 4).rearrange("p (k n) -> p k n", k=4),
                                        HTH[:, 0:4, d].bitcast(F32), ALU.subtract).then_inc(rt_lo, 1)

        o_done, o_added = sem("o_done"), sem("o_added")

        def sp_4(e):
            e.wait_ge(a_w_lo, 2 * HEADS)
            sp_out_weights(e, 1, M_WO1)
            e.wait_ge(a_vh, 2 * HEADS)
            for t in range(4, T):
                e.dma_start(X3[:, t, :], t_in["x"][t * P:(t + 1) * P, :]).then_inc(s_x[t % 4], 16)
            e.wait_ge(rt_turned, T)
            for t in range(4):
                e.dma_start(X3[:, t, :], t_in["x"][t * P:(t + 1) * P, :]).then_inc(s_x[t], 16)
            e.wait_ge(a_pv, NR)
            e.dma_start(GB[:, :], t_in["ffn_norm_g"].partition_broadcast(P)).then_inc(s_gain, 16)

        def pe_4(e):
            e.wait_ge(a_o_lo, NR)
            e.wait_ge(a_pt, NR)
            for half in range(2):
                if half == 1:
                    e.wait_ge(w_lo, M_WO1 + 4)
                for t in range(T):
                    n = half * T + t
                    e.wait_ge(rt_lo, t + 1)
                    if n >= 4:
                        e.wait_ge(o_added, n - 3)
                    product(bank(4 + n % 4), t, 1 - half).then_inc(o_done, 1)
                    if half == 1 and t >= 2:
                        norm_turn(e, n_ffn, t - 2)
            e.wait_ge(w_lo, M_FFN + 2)
            e.wait_ge(n_ffn.lo, T)
            e.wait_ge(o_added, 2 * T - 2)
            gate_up(0, 0, 0, gu_bank(0))
            norm_turn(e, n_ffn, T - 2)
            gate_up(0, 0, 1, gu_bank(0)).then_inc(f_gu, 1)
            norm_turn(e, n_ffn, T - 1)

        def act_4(e):
            for c in range(4):
                e.wait_ge(s_rawb[c], 16 * (HEADS + 2))
                granule_hi(e, 0, c, M_WO1 + c)
            for t in range(T):
                squares_x(e, n_ffn, t, 48, o_added, T + t + 1)
                if t >= 2:
                    turned_hi(e, n_ffn, t - 2)
                if t in (2, 4):
                    for c in range(2):
                        ffn_hi(e, (M_FFN + c + t - 2), 8192 + (t - 2) // 2 * 4096 + c * 2048)
            turned_hi(e, n_ffn, T - 2)
            turned_hi(e, n_ffn, T - 1)

        def squares_x(e, s, t, col, ready, count):
            e.wait_ge(ready, count)
            if t:
                e.wait_ge(s.squares, t)
            norm_squares(e, s, t, col, X3[:, t, :], JUNK)

        def rows_x(e, s, t, col):
            if t >= 2:
                e.wait_ge(s.turned, t - 1)
            norm_rows(e, s, t, col, X3[:, t, :], tmp(2048 + (t % 2) * 1024, 1024))

        def add_x(e, src, t, lo, n, done):
            x = X3[:, t, lo:lo + n]
            nc.vector.tensor_tensor(x, x, src, ALU.add).then_inc(done, 1)

        def dve_4(e):
            for c in range(4):
                granule_lo(e, 0, c, M_WO1 + c)
            for half in range(2):
                for t in range(T):
                    n = half * T + t
                    e.wait_ge(o_done, n + 1)
                    if half == 0:
                        e.wait_ge(s_x[t % 4], 16 * (3 if t >= 4 else 4))
                    add_x(e, bank(4 + n % 4), t, half * HALF, HALF, o_added)
                    if half == 1:
                        if t >= 1:
                            if t == 1:
                                e.wait_ge(s_gain, 32)
                            rows_x(e, n_ffn, t - 1, 48)
                        if t >= 3:
                            turned_lo(e, n_ffn, t - 3)
            rows_x(e, n_ffn, T - 1, 48)
            for t in range(T - 3, T):
                turned_lo(e, n_ffn, t)

        def pool_4(e):
            e.wait_ge(w_lo, M_FFN)
            for t in range(T):
                norm_rstd(e, n_ffn, t, 48)
                if t in (2, 3, 4, 5):
                    split_pool(e, M_FFN + t - 2, 8192 + 2048 * (t - 2), 1024)

        f_gu, f_silu, f_hid, f_hi, f_lo = sem("f_gu"), sem("f_silu"), sem("f_hid"), sem("f_hi"), sem("f_lo")
        f_down, f_added = sem("f_down"), sem("f_added")
        s_p, p_turned, p_hi, p_lo = sem("s_p"), sem("p_turned"), sem("p_hi"), sem("p_lo")
        LAST_DOWN = 8192
        QC = 256
        PIN = tmp(0, 2048).rearrange("p (t n) -> p t n", t=T)
        PTP = [WF[:, c:c + 2048].rearrange("p (k n) -> p k n", k=2) for c in (12288, 14336)]

        def p_half(t, s, f):
            src = PS[:, t // 2, (t % 2) * QC:(t % 2) * QC + QC].rearrange("p (k n) -> p k n", k=2)
            f(src, PTP[0][:, :, t * P:t * P + P], PTP[1][:, :, t * P:t * P + P]).then_inc(s, 1)

        def ffn_hi(e, m, a, more=0):
            arrived(e, m, more * 4)
            nc.scalar.copy(WF[:, a:a + 1024], raw(m)).then_inc(w_hi, 1)

        def ffn_lo(e, m, a, more=0):
            e.wait_ge(w_hi, m + 1 + more)
            nc.vector.tensor_tensor(WF[:, a + 1024:a + 2048], raw(m), WF[:, a:a + 1024].bitcast(F32),
                                    ALU.subtract).then_inc(w_lo, 1)

        def split_pool(e, m, a, n):
            e.wait_ge(w_hi, m + 1)
            nc.gpsimd.tensor_tensor(WF[:, a + n:a + n + 1024], raw(m), WF[:, a:a + 1024].bitcast(F32),
                                    ALU.subtract).then_inc(w_lo, 1)

        def m_block(g):
            return M_FFN + 8 + 6 * (g - 1)

        def sp_ffn_gu(e, m, g, jj, more=0, col=0):
            for n, name in enumerate(("w_ffn_gate", "w_ffn_up")):
                w = t_in[name].rearrange("(k p) n -> p k n", p=P)
                e.wait_ge(w_lo, m + n - 3 + more)
                e.dma_start(raw(m + n).rearrange("p (k n) -> p k n", k=K),
                            w[:, :, bass.ds(col + (g * GROUP + jj) * P, P)]).then_inc(s_raw[(m + n) % 4], 16)

        def sp_ffn_down(e, m, g, more=0, row=0):
            for jj in range(GROUP):
                e.wait_ge(w_lo, m + jj - 3 + more)
                w = t_in["w_ffn_down"]
                e.dma_start(raw(m + jj), w[bass.ds(row + (g * GROUP + jj) * P, P), :]).then_inc(s_raw[(m + jj) % 4], 16)

        def sp_5(e):
            for g in range(2):
                for jj in range(2):
                    sp_ffn_gu(e, M_FFN + 4 * g + 2 * jj, g, jj)

            def block(g, i=0, last=False):
                m = m_block(g)
                sp_ffn_down(e, m, g - 1, i * 12, i * (2 * GROUP * P))
                if not last:
                    for jj in range(2):
                        sp_ffn_gu(e, m + 2 + 2 * jj, g + 1, jj, i * 12, i * (2 * GROUP * P))
            with e.Fori(0, (NG - 3) // 2) as i:
                block(1, i)
                block(2, i)
            block(NG - 2)
            block(NG - 1, last=True)
            sp_ffn_down(e, m_block(NG - 1) + 2, NG - 1)

        def gu_bank(u):
            return 4 if u == 0 else 2 * (u % 2)

        def gate_up(jj, b, x, first):
            blk = slice(b * HALF, (b + 1) * HALF)
            a = 8192 + 4096 * jj + 2048 * x
            dst = bank(first + x)
            for k in range(K):
                w_h, w_l = WF[:, a + k * P:a + k * P + P], WF[:, a + 1024 + k * P:a + 1024 + k * P + P]
                nc.tensor.matmul(dst, w_h, HTH[:, k, blk], start=(k == 0), stop=False)
                nc.tensor.matmul(dst, w_h, HTL[:, k, blk], start=False, stop=False)
                last = nc.tensor.matmul(dst, w_l, HTH[:, k, blk], start=False, stop=(k == K - 1))
            return last

        def pe_gu(e, g, i=0):
            for jj in range(GROUP):
                for b in range(2):
                    u = 4 * g + 2 * jj + b
                    if b == 0:
                        m = M_FFN + 2 * jj + 2 if g == 0 else (M_FFN + 4 + 2 * jj + 2 if g == 1 else m_block(g - 1) + 4 + 2 * jj)
                        e.wait_ge(w_lo, m + i * 12)
                    if u == 0:
                        continue
                    if u == 1:
                        e.wait_ge(n_ffn.lo, 2 * T)
                    if u >= 2:
                        e.wait_ge(f_hid, u - 1 + i * 8)
                    gate_up(jj, b, 0, gu_bank(u))
                    gate_up(jj, b, 1, gu_bank(u)).then_inc(f_gu, 1)

        def pe_down(e, g, i=0, more=None):
            e.wait_ge(f_lo, 4 * (g + 1) + i * 8)
            m = m_block(g + 1) + 2 if g < NG - 1 else m_block(NG - 1) + 4
            e.wait_ge(w_lo, m + i * 12)
            for t in range(T):
                for half in range(2):
                    n = 16 * g + 2 * t + half
                    if n >= 4:
                        e.wait_ge(f_added, n - 3 + i * 32)
                    dst = bank(4 + n % 4)
                    for jj in range(GROUP):
                        hid = (g % 2) * 4096 + 2048 * jj + t * P
                        w = (LAST_DOWN if g == NG - 1 else 16384) + 2048 * jj + half * HALF
                        nc.tensor.matmul(dst, WF[:, hid:hid + P], WF[:, w:w + HALF], start=(jj == 0), stop=False)
                        nc.tensor.matmul(dst, WF[:, hid:hid + P], WF[:, w + 1024:w + 1024 + HALF], start=False, stop=False)
                        last = nc.tensor.matmul(dst, WF[:, hid + 1024:hid + 1024 + P], WF[:, w:w + HALF],
                                                start=False, stop=(jj == GROUP - 1))
                    last.then_inc(f_down, 1)
                if more:
                    more(t)

        def pe_5(e):
            e.wait_ge(o_added, 2 * T)
            pe_gu(e, 0)
            with e.Fori(0, (NG - 3) // 2) as i:
                for g in (1, 2):
                    pe_gu(e, g, i)
                    pe_down(e, g - 1, i)
            pe_gu(e, NG - 2)
            pe_down(e, NG - 3)
            pe_gu(e, NG - 1)
            pe_down(e, NG - 2, more=lambda t: pt_turn(e) if t == 3 else None)

            def turn(t):
                if t >= 2:
                    norm_turn(e, n_ple, t - 2)
            pe_down(e, NG - 1, more=turn)
            pe_6_first(e)

        def act_hidden(e, g, jj, b, i=0):
            u = 4 * g + 2 * jj + b
            e.wait_ge(f_gu, u + 1 + i * 8)
            if u >= 2:
                e.wait_ge(f_hid, u - 1 + i * 8)
            nc.scalar.activation(tmp((u % 2) * HALF, HALF), bank(gu_bank(u)), ACT.Silu).then_inc(f_silu, 1)
            e.wait_ge(f_hid, u + 1 + i * 8)
            if g >= 2 and b == 0:
                e.wait_ge(f_down, 16 * (g - 1) + i * 32)
            a = (g % 2) * 4096 + 2048 * jj + b * HALF
            nc.scalar.copy(WF[:, a:a + HALF], tmp(1024 + (u % 2) * HALF, HALF)).then_inc(f_hi, 1)

        def dve_hidden(e, g, jj, b, i=0):
            u = 4 * g + 2 * jj + b
            e.wait_ge(f_silu, u + 1 + i * 8)
            if u >= 2:
                e.wait_ge(f_lo, u - 1 + i * 8)
            h = tmp(1024 + (u % 2) * HALF, HALF)
            nc.vector.tensor_tensor(h, tmp((u % 2) * HALF, HALF), bank(gu_bank(u) + 1), ALU.mult).then_inc(f_hid, 1)
            e.wait_ge(f_hi, u + 1 + i * 8)
            a = (g % 2) * 4096 + 2048 * jj + b * HALF
            nc.vector.tensor_tensor(WF[:, a + 1024:a + 1024 + HALF], h, WF[:, a:a + HALF].bitcast(F32),
                                    ALU.subtract).then_inc(f_lo, 1)

        def ffn_block(e, g, i, hidden, piece, adds, last=False, between=None):
            m = m_block(g)
            hidden(e, g, 0, 0, i)
            if g >= 2:
                e.wait_ge(f_down, 16 * (g - 1) + i * 32)
            for jj in range(2):
                piece(e, m + jj, 16384 + 2048 * jj, i * 12)
            hidden(e, g, 0, 1, i)
            for b in range(2):
                hidden(e, g, 1, b, i)
                if not last:
                    e.wait_ge(f_gu, 4 * g + 2 + i * 8)
                    piece(e, m + 2 + b, 8192 + 2048 * b, i * 12)
            for n in range(16):
                if adds:
                    adds(e, g - 1, n, i)
                if last:
                    between(e, n)
                if not last and n in (2, 6):
                    e.wait_ge(f_gu, 4 * g + 4 + i * 8)
                    piece(e, m + 4 + n // 4, 12288 + 2048 * (n // 4), i * 12)

        def add_down(e, g, n, i=0):
            e.wait_ge(f_down, 16 * g + n + 1 + i * 32)
            if g >= 1:
                e.wait_ge(f_added, 16 * (g - 1) + n + 1 + i * 32)
            add_x(e, bank(4 + (16 * g + n) % 4), n // 2, (n % 2) * HALF, HALF, f_added)

        def ffn_5(e, hidden, piece, adds, between):
            for jj in range(2):
                for b in range(2):
                    hidden(e, 0, jj, b)
                e.wait_ge(f_gu, 2 * jj + 2)
                if jj == 0:
                    e.wait_ge(w_lo, M_FFN + 4)
                for n in range(2):
                    piece(e, M_FFN + 4 + 2 * jj + n, 8192 + 4096 * jj + 2048 * n, 0)
            with e.Fori(0, (NG - 3) // 2) as i:
                ffn_block(e, 1, i, hidden, piece, adds)
                ffn_block(e, 2, i, hidden, piece, adds)
            ffn_block(e, NG - 2, 0, hidden, piece, adds)
            ffn_block(e, NG - 1, 0, hidden, piece, adds, last=True, between=between)

        def act_5(e):
            def between(e, n):
                if n == 0:
                    e.wait_ge(f_gu, 4 * NG - 2)
                    for jj in range(2):
                        ffn_hi(e, m_block(NG - 1) + 2 + jj, LAST_DOWN + 2048 * jj)
                if n == 1:
                    e.wait_ge(p_turned, 1)
                    e.wait_ge(f_gu, 4 * NG)
                    for t in range(T):
                        p_half(t, p_hi, lambda src, hi, lo: nc.scalar.copy(hi, src))
            ffn_5(e, act_hidden, ffn_hi, None, between)

        def dve_5(e):
            def between(e, n):
                if n in (2, 4):
                    jj = n // 2 - 1
                    ffn_lo(e, m_block(NG - 1) + 2 + jj, LAST_DOWN + 2048 * jj)
                if n >= 12:
                    for t in (2 * n - 24, 2 * n - 23):
                        e.wait_ge(p_hi, t // 2 * 2 + 2)
                        p_half(t, p_lo, lambda src, hi, lo: nc.vector.tensor_tensor(lo, src, hi.bitcast(F32),
                                                                                    ALU.subtract))
            ffn_5(e, dve_hidden, ffn_lo, add_down, between)

        g_done, g_sig, g_mul, g_added = sem("g_done"), sem("g_sig"), sem("g_mul"), sem("g_added")
        s_out = [sem(f"s_out{i}") for i in range(4)]
        M6 = M_PLE
        PW = 16384
        GQ = [4096, 0, 4096, 8192]

        def sp_6(e):
            e.wait_ge(f_lo, 4 * NG)
            e.dma_start(PIN, t_in["p"].rearrange("(t p) n -> p t n", p=P)).then_inc(s_p, 16)
            e.wait_ge(n_ffn.normed, T)
            e.dma_start(GB[:, :], t_in["ple_norm_g"].partition_broadcast(P)).then_inc(s_gain, 16)
            for k in range(2):
                e.wait_ge(w_lo, M6 + k - 3)
                e.dma_start(raw(M6 + k), t_in["w_ple_proj"][k * P:(k + 1) * P, :]).then_inc(s_raw[(M6 + k) % 4], 16)
            w = t_in["w_ple_gate"].rearrange("(k p) n -> p k n", p=P)
            for q in range(4):
                for c in range(2):
                    m = M6 + 2 + 2 * q + c
                    e.wait_ge(w_lo, m - 3)
                    e.dma_start(raw(m).rearrange("p (k n) -> p k n", k=4),
                                w[:, 4 * c:4 * c + 4, q * QC:(q + 1) * QC]).then_inc(s_raw[m % 4], 16)
                if q == 1:
                    e.wait_ge(n_ple.normed, T)
                    e.dma_start(GB[:, :], t_in["final_norm_g"].partition_broadcast(P)).then_inc(s_gain, 16)
            for t in range(T):
                e.wait_ge(n_out.normed, t + 1)
                e.dma_start(out[t * P:(t + 1) * P, :], raw(t)).then_inc(s_out[t % 4], 16)
            for c in range(4):
                e.wait_ge(s_out[c], 16 * T // 4)

        def pt_turn(e):
            e.wait_ge(s_p, 16)
            e.wait_ge(f_hid, 4 * NG)
            for t in range(T):
                for k in range(2):
                    last = nc.tensor.transpose(PS[:, t // 2, (t % 2) * QC + k * P:(t % 2) * QC + k * P + P],
                                               PIN[:, t, k * P:k * P + P], ident)
            last.then_inc(p_turned, 1)

        def act_6(e):
            e.wait_ge(f_down, 16 * (NG - 1))
            for k in range(2):
                ffn_hi(e, M6 + k, PW + 2048 * k)
            for t in range(T):
                squares_x(e, n_ple, t, 48, f_added, 16 * (NG - 1) + 2 * t + 2)
                if t == 1:
                    gate_hi(e, 0)
                if t >= 2:
                    turned_hi(e, n_ple, t - 2)
            turned_hi(e, n_ple, T - 2)
            turned_hi(e, n_ple, T - 1)
            gate_hi(e, 1)
            for q in range(4):
                for t in range(T):
                    u = q * T + t
                    e.wait_ge(g_done, u + 1)
                    if u >= 4:
                        e.wait_ge(g_mul, u - 3)
                    nc.scalar.activation(tmp((u % 4) * QC, QC), PS[:, (u + 4) % 8, 0:QC], ACT.Sigmoid).then_inc(g_sig, 1)
                    if t == 0 and 1 <= q < 3:
                        gate_hi(e, q + 1)
                    if q == 3 and t >= 1:
                        squares_x(e, n_out, t - 1, 96, g_added, 3 * T + t)
            squares_x(e, n_out, T - 1, 96, g_added, 4 * T)

        def gate_hi(e, q):
            if q == 1:
                e.wait_ge(f_down, 16 * NG)
            if q == 2:
                e.wait_ge(g_done, T)
            for c in range(2):
                m, a = M6 + 2 + 2 * q + c, GQ[q] + 1024 * c
                arrived(e, m)
                nc.scalar.copy(WF[:, a:a + 1024], raw(m)).then_inc(w_hi, 1)

        def gate_lo(e, q):
            for c in range(2):
                m, a = M6 + 2 + 2 * q + c, GQ[q] + 1024 * c
                e.wait_ge(w_hi, m + 1)
                nc.vector.tensor_tensor(WF[:, a + 2048:a + 3072], raw(m), WF[:, a:a + 1024].bitcast(F32),
                                        ALU.subtract).then_inc(w_lo, 1)

        def dve_6(e):
            e.wait_ge(s_gain, 48)
            for t in range(T):
                add_down(e, NG - 1, 2 * t)
                add_down(e, NG - 1, 2 * t + 1)
                if t >= 1:
                    rows_x(e, n_ple, t - 1, 48)
                if t >= 3:
                    turned_lo(e, n_ple, t - 3)
            rows_x(e, n_ple, T - 1, 48)
            for t in range(T - 3, T):
                turned_lo(e, n_ple, t)
            e.wait_ge(w_lo, M6 + 4)
            gate_lo(e, 1)
            for q in range(4):
                for t in range(T):
                    u = q * T + t
                    e.wait_ge(g_sig, u + 1)
                    if u >= 4:
                        e.wait_ge(g_added, u - 3)
                    m = tmp(1024 + (u % 4) * QC, QC)
                    nc.vector.tensor_tensor(m, tmp((u % 4) * QC, QC), PS[:, (u + 4) % 8, QC:2 * QC], ALU.mult).then_inc(g_mul, 1)
                    if t == 0 and 1 <= q < 3:
                        gate_lo(e, q + 1)
                    if q == 3 and t >= 2:
                        out_rows(e, t - 2)
            out_rows(e, T - 2)
            out_rows(e, T - 1)

        def out_rows(e, t):
            if t == 0:
                e.wait_ge(s_gain, 64)
            if t >= 4:
                e.wait_ge(s_out[t % 4], 16)
            norm_rows(e, n_out, t, 96, X3[:, t, :], raw(t))

        def pool_6(e):
            for t in range(T):
                norm_rstd(e, n_ple, t, 48)
                if t < 4:
                    a, n = (PW + 2048 * t, 1024) if t < 2 else (GQ[0] + 1024 * (t - 2), 2048)
                    split_pool(e, M6 + t, a, n)
            for q in range(4):
                for t in range(T):
                    u = q * T + t
                    e.wait_ge(g_mul, u + 1)
                    x = X3[:, t, q * QC:(q + 1) * QC]
                    nc.gpsimd.tensor_tensor(x, x, tmp(1024 + (u % 4) * QC, QC), ALU.add).then_inc(g_added, 1)
                    if q == 3 and t >= 1:
                        norm_rstd(e, n_out, t - 1, 96)
            norm_rstd(e, n_out, T - 1, 96)

        def gate_unit(t, place, col, first):
            tok = slice(t * P, t * P + P)
            b = (first + t) % 8
            gate, emb = PS[:, b, 0:QC], PS[:, b, QC:2 * QC]
            for k in range(K):
                w_h, w_l = WF[:, bass.ds(place + k * QC, QC)], WF[:, bass.ds(place + (2048 + k * QC), QC)]
                nc.tensor.matmul(gate, HTH[:, k, tok], w_h, start=(k == 0), stop=False)
                nc.tensor.matmul(gate, HTH[:, k, tok], w_l, start=False, stop=False)
                nc.tensor.matmul(gate, HTL[:, k, tok], w_h, start=False, stop=(k == K - 1))
            for k in range(2):
                for n, (x, y) in enumerate(((0, 0), (0, 1), (1, 0))):
                    last = nc.tensor.matmul(emb, PTP[x][:, k, tok], WF[:, bass.ds(col + (PW + 2048 * k + 1024 * y), QC)],
                                            start=(k + n == 0), stop=(k * n == 2))
            last.then_inc(g_done, 1)

        def pe_6_first(e):
            e.wait_ge(f_added, 16 * NG)
            e.wait_ge(w_lo, M6 + 4)
            e.wait_ge(p_lo, T)
            for t in range(T):
                e.wait_ge(n_ple.lo, 2 * t + 2 if t < 4 else 2 * T)
                gate_unit(t, GQ[0], 0, 4)
                if t < 2:
                    norm_turn(e, n_ple, T - 2 + t)

        def pe_6(e):
            with e.Fori(0, 3) as j:
                e.wait_ge(w_lo, M6 + 6 + j * 2)
                for t in range(T):
                    e.wait_ge(g_mul, j * T + (t + 1))
                    gate_unit(t, j * 4096 + GQ[1], j * QC + QC, 4)

        block = ctx.enter_context(nc.Block())

        @block.sync
        def _(sp):
            sp_1(sp)
            sp_retention(sp)
            sp_out_weights(sp, 0, M_WO0)
            sp_3(sp)
            sp_4(sp)
            sp_5(sp)
            sp_6(sp)

        @block.gpsimd
        def _(pool):
            pool_1(pool)
            pool_2(pool)
            pool_3a(pool)
            pool_3b(pool)
            pool_4(pool)
            pool_6(pool)

        @block.scalar
        def _(act):
            act_1(act)
            act_2(act)
            act_3a(act)
            act_3b(act)
            act_4(act)
            act_5(act)
            act_6(act)

        @block.vector
        def _(dve):
            dve_1(dve)
            dve_2(dve)
            dve_3a(dve)
            dve_3b(dve)
            dve_4(dve)
            dve_5(dve)
            dve_6(dve)

        @block.tensor
        def _(pe):
            pe_1(pe)
            pe_2(pe)
            pe_3a(pe)
            pe_3b(pe)
            pe_4(pe)
            pe_5(pe)
            pe_6(pe)


def kernel(x, p, positions, mix_norm_g, w_in, q_norm_g, w_uq, kv_norm_g, w_ukv, w_o,
           ffn_norm_g, w_ffn_gate, w_ffn_up, w_ffn_down, ple_norm_g, w_ple_gate,
           w_ple_proj, final_norm_g):
    import concourse.bacc as bacc
    from concourse.bass_utils import run_bass_kernel_spmd

    table, query_decay = shape_tables()
    arrays = {
        "x": np.asarray(x)[0],
        "p": np.asarray(p)[0, 0],
        "positions": np.asarray(positions).reshape(T, P).T,
        "w_in": np.asarray(w_in)[0], "w_uq": np.asarray(w_uq)[0], "w_ukv": np.asarray(w_ukv)[0],
        "w_o": np.asarray(w_o)[0], "w_ffn_gate": np.asarray(w_ffn_gate)[0],
        "w_ffn_up": np.asarray(w_ffn_up)[0], "w_ffn_down": np.asarray(w_ffn_down)[0],
        "w_ple_gate": np.asarray(w_ple_gate)[0], "w_ple_proj": np.asarray(w_ple_proj)[0],
        "mix_norm_g": np.asarray(mix_norm_g)[0], "q_norm_g": np.asarray(q_norm_g)[0],
        "kv_norm_g": np.asarray(kv_norm_g)[0], "ffn_norm_g": np.asarray(ffn_norm_g)[0],
        "ple_norm_g": np.asarray(ple_norm_g)[0], "final_norm_g": np.asarray(final_norm_g),
        "table": table, "query_decay": query_decay,
    }
    nc = bacc.Bacc("TRN2", target_bir_lowering=False, num_devices=1, dynamic_dma_scratch_size=1024)
    maps, t_in = {}, {}
    for name, a in arrays.items():
        a = np.ascontiguousarray(a)
        maps["in_" + name] = a
        t_in[name] = nc.dram_tensor("in_" + name, a.shape, mybir.dt.from_np(a.dtype), kind="ExternalInput").ap()
    out = nc.dram_tensor("out_rows", (S, D), F32, kind="ExternalOutput").ap()
    build(nc, t_in, out)
    r = run_bass_kernel_spmd(nc, [maps], core_ids=[0])
    return r.results[0]["out_rows"].reshape(1, S, D)
```
